# Optimizing a Trainium2 kernel written in Bass

```python
import jax, jax.numpy as jnp
from jax import lax
import numpy as np
import math
import jax
import jax.numpy as jnp

D_MODEL = 1024
BATCH = 1
SEQ = 512
DEPTH = 1

HEAD_DIM = 64
A_HEADS = D_MODEL // (2 * HEAD_DIM)
A_KV_HEADS = max(1, A_HEADS // 4)
A_WINDOW = 128
B_HEADS = D_MODEL // (2 * HEAD_DIM)
B_PATTERNS = ((128, 1), (512, 4), (2048, 16))
BLOCK = 128
ROPE_THETA = 10000.0
EPS = 1e-6
NEG = -1e30

A_WIDTH = A_HEADS * HEAD_DIM
A_KV_WIDTH = A_KV_HEADS * HEAD_DIM
B_WIDTH = B_HEADS * HEAD_DIM
MIX_WIDTH = A_WIDTH + B_WIDTH
IN_SPLITS = (A_WIDTH, A_KV_WIDTH, A_KV_WIDTH, A_WIDTH, B_WIDTH, B_WIDTH, B_WIDTH, B_WIDTH)
IN_WIDTH = sum(IN_SPLITS)


def rmsnorm(t, gain):
    tf = t.astype(jnp.float32)
    tf = tf * lax.rsqrt(jnp.mean(tf * tf, axis=-1, keepdims=True) + EPS)
    return (tf * gain.astype(jnp.float32)).astype(t.dtype)

def rope(t, pos):
    half = HEAD_DIM // 2
    inv = ROPE_THETA ** (-jnp.arange(half, dtype=jnp.float32) / half)
    ang = pos.astype(jnp.float32)[:, None] * inv[None, :]
    cos = jnp.cos(ang)[:, None, :]
    sin = jnp.sin(ang)[:, None, :]
    tf = t.astype(jnp.float32)
    t1, t2 = tf[..., :half], tf[..., half:]
    return jnp.concatenate([t1 * cos - t2 * sin, t2 * cos + t1 * sin], axis=-1).astype(t.dtype)

def banded_attention(q, k, v, max_dist, sinks=None):
    n, L, h, d = q.shape
    hkv = k.shape[2]
    g = h // hkv
    nb = -(-L // BLOCK)
    lp = nb * BLOCK
    pad = lp - L
    q = jnp.pad(q, ((0, 0), (0, pad), (0, 0), (0, 0)))
    k = jnp.pad(k, ((0, 0), (BLOCK, pad), (0, 0), (0, 0)))
    v = jnp.pad(v, ((0, 0), (BLOCK, pad), (0, 0), (0, 0)))
    qb = q.reshape(n, nb, BLOCK, hkv, g, d)
    kb = k.reshape(n, nb + 1, BLOCK, hkv, d)
    vb = v.reshape(n, nb + 1, BLOCK, hkv, d)
    kw = jnp.concatenate([kb[:, :-1], kb[:, 1:]], axis=2)
    vw = jnp.concatenate([vb[:, :-1], vb[:, 1:]], axis=2)
    s = jnp.einsum("nbqkgd,nbskd->nbkgqs", qb, kw,
                   preferred_element_type=jnp.float32) * (d ** -0.5)
    qi = jnp.arange(BLOCK)[:, None]
    sj = jnp.arange(2 * BLOCK)[None, :]
    dist = qi - sj + BLOCK
    key_pos = jnp.arange(nb)[:, None] * BLOCK - BLOCK + sj
    valid = ((dist >= 0) & (dist <= max_dist))[None] & (key_pos >= 0)[:, None, :]
    s = jnp.where(valid[None, :, None, None], s, NEG)
    m = s.max(axis=-1)
    if sinks is not None:
        sk = sinks.astype(jnp.float32).reshape(hkv, g)[None, None, :, :, None]
        m = jnp.maximum(m, sk)
    p = jnp.exp(s - m[..., None])
    l = p.sum(axis=-1)
    if sinks is not None:
        l = l + jnp.exp(sk - m)
    o = jnp.einsum("nbkgqs,nbskd->nbqkgd", p, vw.astype(jnp.float32))
    m = m.transpose(0, 1, 4, 2, 3)
    l = l.transpose(0, 1, 4, 2, 3)
    o = o / l[..., None]
    o = o.reshape(n, lp, h, d)[:, :L]
    m = m.reshape(n, lp, h)[:, :L]
    l = l.reshape(n, lp, h)[:, :L]
    return o, m, l

def dilated_attention(q, k, v):
    b, S, h, d = q.shape
    outs, ms, ls = [], [], []
    for window, dil in B_PATTERNS:
        L = S // dil

        def fold(t):
            return t.reshape(b, L, dil, h, d).transpose(0, 2, 1, 3, 4).reshape(b * dil, L, h, d)

        o, m, l = banded_attention(fold(q), fold(k), fold(v), window // dil)
        outs.append(o.reshape(b, dil, L, h, d).transpose(0, 2, 1, 3, 4).reshape(b, S, h, d))
        ms.append(m.reshape(b, dil, L, h).transpose(0, 2, 1, 3).reshape(b, S, h))
        ls.append(l.reshape(b, dil, L, h).transpose(0, 2, 1, 3).reshape(b, S, h))
    o = jnp.stack(outs)
    m = jnp.stack(ms)
    l = jnp.stack(ls)
    w = l * jnp.exp(m - m.max(axis=0, keepdims=True))
    return (w[..., None] * o).sum(axis=0) / w.sum(axis=0)[..., None]

def first_inputs(seed: int = 0) -> dict:
    key = jax.random.key(seed)
    ks = jax.random.split(key, 10)
    f32 = jnp.float32
    x = jax.random.normal(ks[0], (BATCH, SEQ, D_MODEL), f32)
    norm_gain = 1.0 + 0.1 * jax.random.normal(ks[1], (DEPTH, D_MODEL), f32)
    w_in = jax.random.normal(ks[2], (DEPTH, D_MODEL, IN_WIDTH), f32) * D_MODEL ** -0.5
    q_norm_a = 1.0 + 0.1 * jax.random.normal(ks[3], (DEPTH, HEAD_DIM), f32)
    k_norm_a = 1.0 + 0.1 * jax.random.normal(ks[4], (DEPTH, HEAD_DIM), f32)
    sinks_a = 0.5 * jax.random.normal(ks[5], (DEPTH, A_HEADS), f32)
    q_norm_b = 1.0 + 0.1 * jax.random.normal(ks[6], (DEPTH, HEAD_DIM), f32)
    k_norm_b = 1.0 + 0.1 * jax.random.normal(ks[7], (DEPTH, HEAD_DIM), f32)
    w_out = jax.random.normal(ks[8], (DEPTH, MIX_WIDTH, D_MODEL), f32) * MIX_WIDTH ** -0.5
    return {"x": x, "norm_gain": norm_gain, "w_in": w_in,
            "q_norm_a": q_norm_a, "k_norm_a": k_norm_a, "sinks_a": sinks_a,
            "q_norm_b": q_norm_b, "k_norm_b": k_norm_b, "w_out": w_out}

def first_block(x, norm_gain, w_in, q_norm_a, k_norm_a, sinks_a, q_norm_b, k_norm_b, w_out):
    b, S, _ = x.shape
    pos = jnp.arange(S)
    split_at = [int(c) for c in np.cumsum(IN_SPLITS)[:-1]]
    for i in range(DEPTH):
        hdn = rmsnorm(x, norm_gain[i])
        proj = jnp.einsum("bsd,de->bse", hdn, w_in[i])
        q_a, k_a, v_a, g_a, q_b, k_b, v_b, g_b = jnp.split(proj, split_at, axis=-1)

        q_a = rope(rmsnorm(q_a.reshape(b, S, A_HEADS, HEAD_DIM), q_norm_a[i]), pos)
        k_a = rope(rmsnorm(k_a.reshape(b, S, A_KV_HEADS, HEAD_DIM), k_norm_a[i]), pos)
        v_a = v_a.reshape(b, S, A_KV_HEADS, HEAD_DIM)
        o_a, _, _ = banded_attention(q_a, k_a, v_a, A_WINDOW - 1, sinks=sinks_a[i])
        o_a = o_a.reshape(b, S, A_WIDTH).astype(x.dtype) * jax.nn.silu(g_a)

        q_b = rope(rmsnorm(q_b.reshape(b, S, B_HEADS, HEAD_DIM), q_norm_b[i]), pos)
        k_b = rope(rmsnorm(k_b.reshape(b, S, B_HEADS, HEAD_DIM), k_norm_b[i]), pos)
        v_b = v_b.reshape(b, S, B_HEADS, HEAD_DIM)
        o_b = dilated_attention(q_b, k_b, v_b)
        o_b = o_b.reshape(b, S, B_WIDTH).astype(x.dtype) * jax.nn.silu(g_b)

        mixed = jnp.concatenate([o_a, o_b], axis=-1)
        x = x + jnp.einsum("bse,ed->bsd", mixed, w_out[i])
    return x


DEPTH_2 = 2

GRID_W = 64
CTX_LEN = 256
D_CONV = 512
CONV_K = 31
D_SSD = 512
SSD_HEADDIM = 64
SSD_HEADS = D_SSD // SSD_HEADDIM
SSD_GROUPS = 2
SSD_STATE = 128
SSD_CONV_K = 5
SSD_CHUNK = 128
D_BC = SSD_GROUPS * SSD_STATE
D_XBC = D_SSD + 2 * D_BC
D_MIX = D_CONV + D_SSD
D_IN = 2 * D_CONV + D_SSD + D_XBC + 2 * SSD_HEADS
MOE_GROUPS = 4
MOE_PER_GROUP = 4
N_EXPERTS = MOE_GROUPS * MOE_PER_GROUP
MOE_TOPK = 2
EXPERT_FF = 256
RMS_EPS = 1e-6
LN_EPS = 1e-5


def rms_norm(x, g):
    xf = x.astype(jnp.float32)
    y = xf * lax.rsqrt(jnp.mean(jnp.square(xf), axis=-1, keepdims=True) + RMS_EPS)
    return (y * g.astype(jnp.float32)).astype(x.dtype)

def layer_norm(x, g, b):
    xf = x.astype(jnp.float32)
    mu = jnp.mean(xf, axis=-1, keepdims=True)
    var = jnp.mean(jnp.square(xf - mu), axis=-1, keepdims=True)
    y = (xf - mu) * lax.rsqrt(var + LN_EPS)
    return (y * g.astype(jnp.float32) + b.astype(jnp.float32)).astype(x.dtype)

def modulate(h, shift, scale):
    return h * (1.0 + scale) + shift

def ada_mod(cvec, w_ada, b_ada, n):
    m = jax.nn.silu(cvec) @ w_ada[:, :n * D_MODEL] + b_ada[:n * D_MODEL]
    return jnp.split(m, n, axis=-1)

def dwconv_seq(v, w):
    k, ch = w.shape
    return lax.conv_general_dilated(
        v, w[:, None, :].astype(v.dtype), (1,), [(k // 2, k // 2)],
        dimension_numbers=("NWC", "WIO", "NWC"), feature_group_count=ch)

def dwconv_grid(v, w, axis):
    k, ch = w.shape
    if axis == 1:
        taps, pad = w[:, None, None, :], [(k // 2, k // 2), (0, 0)]
    else:
        taps, pad = w[None, :, None, :], [(0, 0), (k // 2, k // 2)]
    return lax.conv_general_dilated(
        v, taps.astype(v.dtype), (1, 1), pad,
        dimension_numbers=("NHWC", "HWIO", "NHWC"), feature_group_count=ch)

def split_proj(proj):
    o1, o2, o3, o4 = D_CONV, 2 * D_CONV, 2 * D_CONV + D_SSD, 2 * D_CONV + D_SSD + D_XBC
    return proj[..., :o1], proj[..., o1:o2], proj[..., o2:o3], proj[..., o3:o4], proj[..., o4:]

def conformer_conv(u, gate, p, rows):
    v = u * jax.nn.sigmoid(gate)
    if rows is None:
        y = dwconv_seq(v, p["conv_w"])
    else:
        b, l, ch = v.shape
        half = ch // 2
        vg = v.reshape(b, rows, GRID_W, ch)
        y = jnp.concatenate([dwconv_grid(vg[..., :half], p["conv_w"][:, :half], 2),
                             dwconv_grid(vg[..., half:], p["conv_w"][:, half:], 1)],
                            axis=-1).reshape(b, l, ch)
    return jax.nn.silu(layer_norm(y + p["conv_b"], p["conv_ln_g"], p["conv_ln_b"]))

def group_to_heads(v):
    b, l, _ = v.shape
    return jnp.repeat(v.reshape(b, l, SSD_GROUPS, SSD_STATE), SSD_HEADS // SSD_GROUPS, axis=2)

def ssd_scan_inputs(xbc_raw, dt_raw, p):
    b, l, ch = xbc_raw.shape
    xbc = jax.nn.silu(dwconv_seq(xbc_raw, p["ssd_conv_w"][:, :ch]) + p["ssd_conv_b"][:ch])
    xs = xbc[..., :D_SSD].reshape(b, l, SSD_HEADS, SSD_HEADDIM)
    bm = group_to_heads(xbc[..., D_SSD:D_SSD + D_BC])
    cm = group_to_heads(xbc[..., D_SSD + D_BC:]) if ch == D_XBC else None
    dt = jax.nn.softplus(dt_raw.astype(jnp.float32).reshape(b, l, 2, SSD_HEADS)
                         + p["dt_bias"].astype(jnp.float32))
    return xs, bm, cm, dt

def flip_seq(t):
    return jnp.flip(t, axis=1)

def ssd_chunked(xs, dt, a, bm, cm, h0):
    b, l, nh, hp = xs.shape
    n = bm.shape[-1]
    nc = l // SSD_CHUNK
    a_cum = jnp.cumsum((dt * a).reshape(b, nc, SSD_CHUNK, nh), axis=2)
    xdt = (xs * dt[..., None]).reshape(b, nc, SSD_CHUNK, nh, hp)
    bc = bm.reshape(b, nc, SSD_CHUNK, nh, n)
    cc = cm.reshape(b, nc, SSD_CHUNK, nh, n)
    causal = jnp.tril(jnp.ones((SSD_CHUNK, SSD_CHUNK), dtype=bool))
    seg = a_cum[:, :, :, None, :] - a_cum[:, :, None, :, :]
    decay_ls = jnp.exp(jnp.where(causal[None, None, :, :, None], seg, -jnp.inf))
    scores = jnp.einsum("bclhn,bcshn->bclsh", cc, bc) * decay_ls
    y_diag = jnp.einsum("bclsh,bcshp->bclhp", scores, xdt)
    decay_to_end = jnp.exp(a_cum[:, :, -1:, :] - a_cum)
    chunk_states = jnp.einsum("bclh,bclhn,bclhp->bchpn", decay_to_end, bc, xdt)
    chunk_decay = jnp.exp(a_cum[:, :, -1, :])

    def step(h, inp):
        s, d = inp
        return h * d[:, :, None, None] + s, h

    _, h_prev = lax.scan(step, h0.astype(chunk_states.dtype),
                         (jnp.swapaxes(chunk_states, 0, 1), jnp.swapaxes(chunk_decay, 0, 1)))
    h_prev = jnp.swapaxes(h_prev, 0, 1)
    y_off = jnp.einsum("bclhn,bchpn,bclh->bclhp", cc, h_prev, jnp.exp(a_cum))
    return (y_diag + y_off).reshape(b, l, nh, hp)

def ssd_final_state(xs, dt, a, bm):
    la = jnp.cumsum(dt * a, axis=1)
    w = jnp.exp(la[:, -1:, :] - la) * dt
    return jnp.einsum("blh,blhn,blhp->bhpn", w, bm, xs)

def context_states(xs, bm, dt, a):
    hf = ssd_final_state(xs, dt[:, :, 0], a[0], bm)
    hb = ssd_final_state(flip_seq(xs), flip_seq(dt[:, :, 1]), a[1], flip_seq(bm))
    return hf, hb

def mixer_output(u, gate, z, xs, bm, cm, dt, a, h0_f, h0_b, p, rows):
    conv_out = conformer_conv(u, gate, p, rows)
    y_f = ssd_chunked(xs, dt[:, :, 0], a[0], bm, cm, h0_f)
    y_b = flip_seq(ssd_chunked(flip_seq(xs), flip_seq(dt[:, :, 1]), a[1],
                               flip_seq(bm), flip_seq(cm), h0_b))
    y = y_f + y_b + p["d_skip"][:, None] * xs
    b, l = xs.shape[:2]
    ssd_out = rms_norm(y.reshape(b, l, D_SSD) * jax.nn.silu(z), p["ssd_norm_g"])
    return jnp.concatenate([conv_out, ssd_out], axis=-1) @ p["w_out"]

def hier_moe(h, p):
    b, l, d = h.shape
    t = h.reshape(b * l, d)
    g_logits = (t @ p["w_rg"] + p["b_rg"]).astype(jnp.float32)
    g_sel = jnp.argmax(g_logits, axis=-1)
    g_prob = jnp.take_along_axis(jax.nn.softmax(g_logits, axis=-1), g_sel[:, None], axis=-1)
    e_logits = (t @ p["w_re"] + p["b_re"]).astype(jnp.float32).reshape(-1, MOE_GROUPS, MOE_PER_GROUP)
    e_logits = jnp.take_along_axis(e_logits, g_sel[:, None, None], axis=1)[:, 0]
    top_v, top_i = lax.top_k(jax.nn.softmax(e_logits, axis=-1), MOE_TOPK)
    w_sel = g_prob * top_v / jnp.sum(top_v, axis=-1, keepdims=True)
    e_id = g_sel[:, None] * MOE_PER_GROUP + top_i
    comb = jnp.einsum("tk,tke->et", w_sel, jax.nn.one_hot(e_id, N_EXPERTS, dtype=jnp.float32))

    def expert(acc, ew):
        wg, wu, wd, cw = ew
        hid = jax.nn.silu(t @ wg) * (t @ wu)
        return acc + (cw[:, None] * (hid @ wd)).astype(acc.dtype), None

    out, _ = lax.scan(expert, jnp.zeros(t.shape, jnp.float32),
                      (p["w_gate"], p["w_up"], p["w_down"], comb))
    return out.reshape(b, l, d)

def second_inputs(seed: int = 0) -> dict:
    key = jax.random.key(seed)
    ks = iter(jax.random.split(key, 40))
    f32 = jnp.float32

    def nrm(shape, scale):
        return scale * jax.random.normal(next(ks), shape, f32)

    def gain(shape):
        return 1.0 + nrm(shape, 0.02)

    dt0 = jnp.exp(jax.random.uniform(next(ks), (DEPTH_2, 2, SSD_HEADS), f32,
                                     math.log(1e-3), math.log(1e-1)))
    return {
        "x": nrm((BATCH, SEQ, D_MODEL), 1.0),
        "c": nrm((BATCH, D_MODEL), 1.0),
        "ctx": nrm((BATCH, CTX_LEN, D_MODEL), 1.0),
        "c_ctx": nrm((D_MODEL,), 1.0),
        "w_ada": nrm((DEPTH_2, D_MODEL, 6 * D_MODEL), 0.5 * D_MODEL ** -0.5),
        "b_ada": nrm((DEPTH_2, 6 * D_MODEL), 0.02),
        "g_mix": gain((DEPTH_2, D_MODEL)),
        "g_ffn": gain((DEPTH_2, D_MODEL)),
        "w_in": nrm((DEPTH_2, D_MODEL, D_IN), D_MODEL ** -0.5),
        "conv_w": nrm((DEPTH_2, CONV_K, D_CONV), CONV_K ** -0.5),
        "conv_b": nrm((DEPTH_2, D_CONV), 0.02),
        "conv_ln_g": gain((DEPTH_2, D_CONV)),
        "conv_ln_b": nrm((DEPTH_2, D_CONV), 0.02),
        "ssd_conv_w": nrm((DEPTH_2, SSD_CONV_K, D_XBC), SSD_CONV_K ** -0.5),
        "ssd_conv_b": nrm((DEPTH_2, D_XBC), 0.02),
        "dt_bias": dt0 + jnp.log(-jnp.expm1(-dt0)),
        "a_log": jnp.log(jax.random.uniform(next(ks), (DEPTH_2, 2, SSD_HEADS), f32, 1.0, 16.0)),
        "d_skip": gain((DEPTH_2, SSD_HEADS)),
        "ssd_norm_g": gain((DEPTH_2, D_SSD)),
        "w_out": nrm((DEPTH_2, D_MIX, D_MODEL), D_MIX ** -0.5),
        "w_router_group": nrm((DEPTH_2, D_MODEL, MOE_GROUPS), D_MODEL ** -0.5),
        "b_router_group": nrm((DEPTH_2, MOE_GROUPS), 0.01),
        "w_router_expert": nrm((DEPTH_2, D_MODEL, N_EXPERTS), D_MODEL ** -0.5),
        "b_router_expert": nrm((DEPTH_2, N_EXPERTS), 0.01),
        "w_gate": nrm((DEPTH_2, N_EXPERTS, D_MODEL, EXPERT_FF), D_MODEL ** -0.5),
        "w_up": nrm((DEPTH_2, N_EXPERTS, D_MODEL, EXPERT_FF), D_MODEL ** -0.5),
        "w_down": nrm((DEPTH_2, N_EXPERTS, EXPERT_FF, D_MODEL), EXPERT_FF ** -0.5),
        "g_final": gain((D_MODEL,)),
    }

def second_block(x, c, ctx, c_ctx, w_ada, b_ada, g_mix, g_ffn, w_in, conv_w, conv_b, conv_ln_g,
              conv_ln_b, ssd_conv_w, ssd_conv_b, dt_bias, a_log, d_skip, ssd_norm_g, w_out,
              w_router_group, b_router_group, w_router_expert, b_router_expert,
              w_gate, w_up, w_down, g_final):
    rows = x.shape[1] // GRID_W
    h_x, h_c = x, ctx
    lo = 2 * D_CONV + D_SSD
    for l in range(DEPTH_2):
        last = l == DEPTH_2 - 1
        p = {"w_in": w_in[l], "conv_w": conv_w[l], "conv_b": conv_b[l], "conv_ln_g": conv_ln_g[l],
             "conv_ln_b": conv_ln_b[l], "ssd_conv_w": ssd_conv_w[l], "ssd_conv_b": ssd_conv_b[l],
             "dt_bias": dt_bias[l], "d_skip": d_skip[l], "ssd_norm_g": ssd_norm_g[l],
             "w_out": w_out[l], "w_rg": w_router_group[l], "b_rg": b_router_group[l],
             "w_re": w_router_expert[l], "b_re": b_router_expert[l],
             "w_gate": w_gate[l], "w_up": w_up[l], "w_down": w_down[l]}
        a = -jnp.exp(a_log[l].astype(jnp.float32))
        sh1, sc1, gt1, sh2, sc2, gt2 = [m[:, None, :] for m in ada_mod(c, w_ada[l], b_ada[l], 6)]

        if last:
            csh1, csc1 = ada_mod(c_ctx, w_ada[l], b_ada[l], 2)
            hc = modulate(rms_norm(h_c, g_mix[l]), csh1, csc1)
            w_xb_dt = jnp.concatenate([p["w_in"][:, lo:lo + D_SSD + D_BC], p["w_in"][:, lo + D_XBC:]], axis=1)
            proj_c = hc @ w_xb_dt
            xs_c, bm_c, _, dt_c = ssd_scan_inputs(proj_c[..., :D_SSD + D_BC], proj_c[..., D_SSD + D_BC:], p)
        else:
            csh1, csc1, cgt1, csh2, csc2, cgt2 = ada_mod(c_ctx, w_ada[l], b_ada[l], 6)
            hc = modulate(rms_norm(h_c, g_mix[l]), csh1, csc1)
            uc, gc, zc, xbc_c, dtr_c = split_proj(hc @ p["w_in"])
            xs_c, bm_c, cm_c, dt_c = ssd_scan_inputs(xbc_c, dtr_c, p)
        hf0, hb0 = context_states(xs_c, bm_c, dt_c, a)

        hx = modulate(rms_norm(h_x, g_mix[l]), sh1, sc1)
        u, gate, z, xbc, dt_raw = split_proj(hx @ p["w_in"])
        xs, bm, cm, dt = ssd_scan_inputs(xbc, dt_raw, p)
        h_x = h_x + gt1 * mixer_output(u, gate, z, xs, bm, cm, dt, a, hf0, hb0, p, rows)
        h_x = h_x + gt2 * hier_moe(modulate(rms_norm(h_x, g_ffn[l]), sh2, sc2), p)

        if not last:
            zero = jnp.zeros_like(hf0)
            h_c = h_c + cgt1 * mixer_output(uc, gc, zc, xs_c, bm_c, cm_c, dt_c, a, zero, zero, p, None)
            h_c = h_c + cgt2 * hier_moe(modulate(rms_norm(h_c, g_ffn[l]), csh2, csc2), p)

    return rms_norm(h_x, g_final).astype(x.dtype)


def setup_inputs(seed=0):
    out = dict(first_inputs(seed))
    for name, value in second_inputs(seed + 1).items():
        if name != "x":
            out[name + "_2"] = value
    return out


def reference(
    x, norm_gain, w_in, q_norm_a, k_norm_a, sinks_a, q_norm_b, k_norm_b, w_out, c_2, ctx_2,
    c_ctx_2, w_ada_2, b_ada_2, g_mix_2, g_ffn_2, w_in_2, conv_w_2, conv_b_2, conv_ln_g_2,
    conv_ln_b_2, ssd_conv_w_2, ssd_conv_b_2, dt_bias_2, a_log_2, d_skip_2, ssd_norm_g_2,
    w_out_2, w_router_group_2, b_router_group_2, w_router_expert_2, b_router_expert_2, w_gate_2,
    w_up_2, w_down_2, g_final_2,
):
    x = first_block(
        x, norm_gain, w_in, q_norm_a, k_norm_a, sinks_a, q_norm_b, k_norm_b, w_out,
    )
    return second_block(
        x, c_2, ctx_2, c_ctx_2, w_ada_2, b_ada_2, g_mix_2, g_ffn_2, w_in_2, conv_w_2, conv_b_2,
        conv_ln_g_2, conv_ln_b_2, ssd_conv_w_2, ssd_conv_b_2, dt_bias_2, a_log_2, d_skip_2,
        ssd_norm_g_2, w_out_2, w_router_group_2, b_router_group_2, w_router_expert_2,
        b_router_expert_2, w_gate_2, w_up_2, w_down_2, g_final_2,
    )


_drawn_inputs = setup_inputs


def setup_inputs(seed=0):
    import zlib

    import numpy as np

    out = dict(_drawn_inputs(seed))
    spreads = {}
    factors = {'q_norm_a': 5.551,
     'k_norm_a': 6.275,
     'sinks_a': 8.0,
     'q_norm_b': 5.507,
     'k_norm_b': 5.838,
     'ctx_2': 3.477,
     'c_ctx_2': 3.358,
     'g_mix_2': 5.319,
     'g_ffn_2': 4.681,
     'conv_b_2': 5.504,
     'conv_ln_g_2': 8.0,
     'conv_ln_b_2': 8.0,
     'ssd_conv_b_2': 5.42,
     'd_skip_2': 200.0,
     'ssd_norm_g_2': 7.756,
     'b_router_group_2': 8.0,
     'b_router_expert_2': 8.0,
     'g_final_2': 22.812}
    for name, (base, spread) in spreads.items():
        noise = np.random.default_rng([zlib.crc32(name.encode()), seed]).standard_normal(out[name].shape)
        drawn = base * np.exp(spread * noise) if base else spread * noise
        out[name] = jnp.asarray(drawn.astype(out[name].dtype))
    for name, factor in factors.items():
        out[name] = (out[name] * factor).astype(out[name].dtype)
    return out
```

```python
import concourse.bass as bass
from concourse import mybir
from contextlib import ExitStack

F32 = mybir.dt.float32
ALU = mybir.AluOpType
ACT = mybir.ActivationFunctionType
AX = mybir.AxisListType

P = 128
D = 1024
KC = D // P
SEQ, CTX = 512, 256
NXT, NCT = SEQ // P, CTX // P
NT = NXT + NCT
TOK = SEQ + CTX
EPS, LN_EPS = 1e-6, 1e-5
HD = 64
AH = BH = 8
AKV = 2
SCALE = HD ** -0.5
NEG = -1e30
LAYERS = 2
GRID_W = 64
ROWS = SEQ // GRID_W
CK, SK = 31, 5
DC = DS = 512
SH = 8
NS_ = 128
DIN = 2576
NG, NPG, NE = 4, 4, 16
FF = 256

C_ID, C_LE, C_LT, C_GE, C_GT, C_ONE = (P * n for n in range(6))
C_MA = 6 * P
C_MB = C_MA + 2 * P
C_CS = C_MB + 4 * P
NCONST = C_CS + 4 * HD
V_NG, V_C, V_CC = 0, 8, 16
V_L = 24
V_LN = 40
B_QK, B_SK, B_DTB, B_AL, B_DS, B_BR, B_GF = 0, 256, 264, 296, 328, 344, 384
NB = B_GF + D


class Mark:

    def __init__(self, sem, count, loop):
        self.sem, self.count, self.loop = sem, count, loop

    def value(self):
        if self.loop is None:
            return self.count
        return self.loop.value(self.sem, self.count)


class Loop:

    def __init__(self, book, name, n):
        self.book, self.name, self.n = book, name, n
        self.i = None
        self.base = {}
        self.local = {}
        self.per = book.known.get(name, {}).get("per", {})
        self.carried = book.known.get(name, {}).get("carry", {})
        self.out = {}

    def value(self, sem, count):
        k = sem.name
        if self.i is None:
            return self.base[k] + (self.n - 1) * self.local.get(k, 0) + count
        return self.base[k] + count + self.i * self.per.get(k, 0)

    def prev(self, name):
        if name not in self.carried:
            return None
        k, count = self.carried[name]
        return Prev(self, self.book.sems[k], count - self.per[k])

    def carry(self, name, mark):
        self.out[name] = (mark.sem.name, mark.count)


class Prev:
    def __init__(self, loop, sem, count):
        self.loop, self.sem, self.count = loop, sem, count

    def value(self):
        return self.loop.value(self.sem, self.count)


class Book:

    def __init__(self, known):
        self.known, self.sems, self.loop, self.found = known, {}, None, {}
        self.lanes = []


class Lane:

    def __init__(self, book, eng, sem):
        self.book, self.eng, self.sem, self.count = book, eng, sem, 0
        self.seen = {}
        book.sems[sem.name] = sem
        book.lanes.append(self)

    def mark(self, inst):
        inst.then_inc(self.sem, 1)
        loop = self.book.loop
        if loop is None:
            self.count += 1
            return Mark(self.sem, self.count, None)
        k = self.sem.name
        loop.local[k] = loop.local.get(k, 0) + 1
        return Mark(self.sem, loop.local[k], loop)

    def last(self):
        loop = self.book.loop
        if loop is None:
            return Mark(self.sem, self.count, None)
        return Mark(self.sem, loop.local.get(self.sem.name, 0), loop)

    def need(self, *marks):
        for m in marks:
            if m is None:
                continue
            if isinstance(m, (list, tuple)):
                self.need(*m)
                continue
            v = m.value()
            if isinstance(v, int):
                if self.seen.get(m.sem.name, 0) >= v or v <= 0:
                    continue
                if self.book.loop is None:
                    self.seen[m.sem.name] = v
            self.eng.wait_ge(m.sem, v)


def program(nc, ins, out, known):
    book = Book(known)
    ctx = ExitStack()
    with ctx:
        def sem(name):
            return ctx.enter_context(nc.semaphore(name))

        pe = Lane(book, nc.tensor, sem("pe_done"))
        dve = Lane(book, nc.vector, sem("dve_done"))
        act = Lane(book, nc.scalar, sem("act_done"))
        pool = Lane(book, nc.gpsimd, sem("pool_done"))
        sp = nc.sync
        PE, DVE, ACTE, POOL = nc.tensor, nc.vector, nc.scalar, nc.gpsimd
        lanes = [pe, dve, act, pool]

        spl = Lane(book, nc.sync, sem("sync_done"))

        class loop_over:

            def __init__(self, name, n):
                self.loop = Loop(book, name, n)

            def __enter__(self):
                lp = self.loop
                for x in book.lanes:
                    lp.base[x.sem.name] = x.count
                self.cm = nc.Fori(0, lp.n)
                lp.i = self.cm.__enter__()
                book.loop = lp
                return lp

            def __exit__(self, *a):
                lp = self.loop
                self.cm.__exit__(*a)
                book.loop, lp.i = None, None
                for x in book.lanes:
                    x.count += lp.n * lp.local.get(x.sem.name, 0)
                book.found[lp.name] = {"per": dict(lp.local), "carry": dict(lp.out)}

        def phase():
            marks = [x.last() for x in lanes]
            for x in lanes:
                x.need(*marks)

        sb = ctx.enter_context(nc.sbuf_tensor("arena", [P, 53200], F32))
        top = [0]

        def place(n):
            at = top[0]
            top[0] += n
            return at

        def view(at, *dims):
            n = 1
            for d in dims:
                n *= d
            v = sb[:, at:at + n]
            if len(dims) == 2:
                v = v.rearrange("p (a b) -> p a b", b=dims[1])
            elif len(dims) == 3:
                v = v.rearrange("p (a b c) -> p a b c", b=dims[1], c=dims[2])
            return v

        NSLOT = 4
        SLOT = KC * 512
        ring_at = place(NSLOT * SLOT)
        resid = view(place(NT * D), NT, D)
        const = view(place(NCONST), NCONST)
        vec = view(place(5 * P), 5 * P)
        bc = view(place(NB), NB)
        mods = view(place(LAYERS * 48 * 2), LAYERS, 48, 2)
        router = view(place(LAYERS * KC * 20), LAYERS, KC, 20)
        gate_at = place(2 * D)
        gates = view(gate_at, 2, D)
        stat_at = place(1024)
        zone = top[0]
        ident = const[:, C_ID:C_ID + P]
        ones = const[:, C_ONE:C_ONE + P]

        psum = [ctx.enter_context(nc.psum_tensor(f"psum{n}", [P, 512], F32)) for n in range(8)]
        bank_free = [None] * 8
        turn = [0]

        def bank():
            n = turn[0] % 8
            turn[0] += 1
            pe.need(bank_free[n])
            return n

        slot_full = [sem(f"slot_full{n}") for n in range(NSLOT)]
        slot_count = [0] * NSLOT
        slot_free = [None] * NSLOT
        slot_turn = [0]

        def slot_view(n, width):
            return sb[:, ring_at + n * SLOT:ring_at + n * SLOT + KC * width].rearrange("p (k n) -> p k n", n=width)

        def fetch(src, width):
            n = slot_turn[0] % NSLOT
            slot_turn[0] += 1
            spl.need(slot_free[n])
            dst = slot_view(n, width)
            sp.dma_start(dst, src.rearrange("(k p) n -> p k n", p=P)).then_inc(slot_full[n], 16)
            slot_count[n] += 16
            return dst, Mark(slot_full[n], slot_count[n], None), n

        s_small = sem("small_loaded")
        rows = view(zone, 5, P)
        small = [0]

        def load(dst, src):
            nc.scalar.dma_start(dst, src).then_inc(s_small, 16)
            small[0] += 16
        load(const, ins["consts"])
        load(resid[:, 0:NXT, :], ins["x"][0].rearrange("(t p) d -> p t d", p=P))

        def load_rows(g, r, src, n):
            load(rows[r:r + n, g, :], src)
        load_rows(0, V_NG, ins["norm_gain"].rearrange("a (k n) -> (a k) n", n=P), 8)
        load_rows(0, V_C, ins["c_2"].rearrange("a (k n) -> (a k) n", n=P), 8)
        load_rows(0, V_CC, ins["c_ctx_2"].rearrange("(k n) -> k n", n=P), 8)
        for l in range(LAYERS):
            at = V_L + l * V_LN
            for name, n in (("g_mix_2", 8), ("g_ffn_2", 8), ("conv_b_2", 4), ("conv_ln_g_2", 4),
                            ("conv_ln_b_2", 4), ("ssd_conv_b_2", 8), ("ssd_norm_g_2", 4)):
                load_rows(0, at, ins[name][l].rearrange("(k n) -> k n", n=P), n)
                at += n
            load_rows(1, l * 48, ins["b_ada_2"][l].rearrange("(k n) -> k n", n=P), 48)
            load_rows(2 + l, 0, ins["conv_w_2"][l].rearrange("t (k n) -> (t k) n", n=P), 4 * CK)
            load_rows(4, l * 40, ins["ssd_conv_w_2"][l].rearrange("t (k n) -> (t k) n", n=P), 8 * SK)

        def load_bc(at, src):
            n = src.shape[-1]
            load(bc[:, at:at + n], src.partition_broadcast(P))
        for n, name in enumerate(("q_norm_a", "k_norm_a", "q_norm_b", "k_norm_b")):
            load_bc(B_QK + n * HD, ins[name][0])
        load_bc(B_SK, ins["sinks_a"][0])
        for l in range(LAYERS):
            load_bc(B_DTB + l * 16, ins["dt_bias_2"][l].rearrange("a h -> (a h)"))
            load_bc(B_AL + l * 16, ins["a_log_2"][l].rearrange("a h -> (a h)"))
            load_bc(B_DS + l * 8, ins["d_skip_2"][l])
            load_bc(B_BR + l * 20, ins["b_router_group_2"][l])
            load_bc(B_BR + l * 20 + 4, ins["b_router_expert_2"][l])
            load(router[:, l, :, 0:4], ins["w_router_group_2"][l].rearrange("(k p) n -> p k n", p=P))
            load(router[:, l, :, 4:20], ins["w_router_expert_2"][l].rearrange("(k p) n -> p k n", p=P))
        load_bc(B_GF, ins["g_final_2"])
        load(resid[:, NXT:NT, :], ins["ctx_2"][0].rearrange("(t p) d -> p t d", p=P))
        m_small = Mark(s_small, small[0], None)

        for x in lanes:
            x.need(m_small)
        nrow = [V_L + 2 * V_LN, 96, 4 * CK, 4 * CK, 80]
        b = bank()
        for g in range(4):
            m = pe.mark(PE.transpose(psum[b][:, g * P:g * P + nrow[g]], rows[0:nrow[g], g, :], ident[0:nrow[g], 0:nrow[g]]))
        b2 = bank()
        m2 = pe.mark(PE.transpose(psum[b2][:, 0:nrow[4]], rows[0:nrow[4], 4, :], ident[0:nrow[4], 0:nrow[4]]))
        dve.need(m)
        for g in range(4):
            mv = dve.mark(DVE.tensor_copy(vec[:, g * P:g * P + nrow[g]], psum[b][:, g * P:g * P + nrow[g]]))
        dve.need(m2)
        mv = dve.mark(DVE.tensor_copy(vec[:, 4 * P:4 * P + nrow[4]], psum[b2][:, 0:nrow[4]]))
        bank_free[b] = bank_free[b2] = mv
        cvec = view(stat_at, KC, 2)
        act.need(mv)
        for j, at in enumerate((V_C, V_CC)):
            m_cvec = act.mark(ACTE.activation(cvec[:, :, j], vec[:, at:at + KC], ACT.Silu))
        phase()

        def ada_piece(l, n):
            w, ready, s = fetch(ins["w_ada_2"][l][:, n * 512:(n + 1) * 512], 512)
            pe.need(ready)
            b = bank()
            for f in range(4):
                for k in range(KC):
                    i = PE.matmul(psum[b][:, 2 * f:2 * f + 2], w[:, k, f * P:(f + 1) * P], cvec[:, k, :],
                                  start=k == 0, stop=k == KC - 1)
            m = pe.mark(i)
            slot_free[s] = m
            dve.need(m)
            bias = vec[:, P + l * 48 + 4 * n:P + l * 48 + 4 * n + 4].unsqueeze(2).to_broadcast([P, 4, 2])
            bank_free[b] = dve.mark(DVE.tensor_tensor(
                mods[:, l, 4 * n:4 * n + 4, :], psum[b][:, 0:8].rearrange("p (f j) -> p f j", j=2), bias, ALU.add))
        ada_todo = [(l, n) for l in range(LAYERS) for n in range(12)]

        def some_ada(n):
            for _ in range(n):
                if ada_todo:
                    ada_piece(*ada_todo.pop(0))

        stats = view(stat_at + 16, 96)
        def rms_rows(tiles, width, src, scratch, at=0, eps=EPS):
            for t in tiles:
                act.need(act.last())
                act.mark(ACTE.activation(scratch, src(t), ACT.Square, accum_out=stats[:, at + t:at + t + 1]))
            a, z = at + tiles[0], at + tiles[-1] + 1
            dve.need(act.last())
            m = dve.mark(DVE.tensor_scalar(stats[:, a:z], stats[:, a:z], 1.0 / width, eps, ALU.mult, ALU.add))
            act.need(m)
            m = act.mark(ACTE.activation(stats[:, a:z], stats[:, a:z], ACT.Sqrt))
            dve.need(m)
            return dve.mark(DVE.reciprocal(stats[:, a:z], stats[:, a:z]))

        def normed_features(tiles_of, dst, xn, scale_of, bias_of):
            tiles = [t for ts, _ in tiles_of for t in ts]
            m = rms_rows(tiles, D, lambda t: resid[:, t, :], xn[:, tiles[0], :])
            dve.need(m)
            ms = {}
            act.need(m)
            for t in tiles:
                if t % 2:
                    ms[t] = dve.mark(DVE.tensor_scalar(xn[:, t, :], resid[:, t, :], stats[:, t:t + 1], None, ALU.mult))
                else:
                    ms[t] = act.mark(ACTE.activation(xn[:, t, :], resid[:, t, :], ACT.Copy, scale=stats[:, t:t + 1]))
            for k in range(KC):
                for ts, which in tiles_of:
                    b = bank()
                    for j, t in enumerate(ts):
                        pe.need(ms[t])
                        i = PE.transpose(psum[b][:, j * P:(j + 1) * P], xn[:, t, k * P:(k + 1) * P], ident)
                    m = pe.mark(i)
                    n = len(ts) * P
                    o = dst[:, k, ts[0] * P:ts[0] * P + n]
                    sc, bi = scale_of(k, which), bias_of(k, which)
                    if k % 2:
                        dve.need(m)
                        if bi is None:
                            bank_free[b] = dve.mark(DVE.tensor_scalar(o, psum[b][:, 0:n], sc, None, ALU.mult))
                        else:
                            bank_free[b] = dve.mark(DVE.tensor_scalar(o, psum[b][:, 0:n], sc, bi, ALU.mult, ALU.add))
                    else:
                        act.need(m)
                        bank_free[b] = act.mark(ACTE.activation(o, psum[b][:, 0:n], ACT.Identity, scale=sc,
                                                                bias=0.0 if bi is None else bi))

        def tok_product(xT, t, w, width, cols=0, start=True, stop=True, kc=KC, b=None, off=0):
            if b is None:
                b = bank()
            for k in range(kc):
                i = PE.matmul(psum[b][:, off:off + width], xT[:, k, t * P:(t + 1) * P], w[:, k, cols:cols + width],
                              start=k == 0, stop=k == kc - 1)
            return b, pe.mark(i)

        z = zone
        hT = view(z, KC, SEQ); z += KC * SEQ
        qkT_at = z
        qTA = view(z, 4, SEQ); z += 4 * SEQ
        kTA = view(z, 4, SEQ); z += 4 * SEQ
        qTB = view(z, 4, SEQ); z += 4 * SEQ
        kTB = view(z, 4, SEQ); z += 4 * SEQ
        vA = view(z, NXT, 4, HD); z += NXT * 256
        vB = view(z, NXT, 4, P); z += NXT * 512
        mix = view(z, NXT, D); z += NXT * D
        tmp_at = z; z += 2048
        cosg = view(gate_at, 4, NXT, HD)
        sing = view(gate_at + 1024, 4, NXT, HD)
        assert z <= 53200
        tabs = const[:, C_CS:C_CS + 4 * HD].rearrange("p (t n) -> p t n", n=HD)
        for n in range(4):
            g = bc[:, B_QK + n * HD:B_QK + (n + 1) * HD]
            gl, gh = (g[:, o:o + 32].unsqueeze(1).to_broadcast([P, NXT, 32]) for o in (0, 32))
            pool.mark(POOL.tensor_tensor(cosg[:, n, :, 0:32], tabs[:, :, 0:32], gl, ALU.mult))
            pool.mark(POOL.tensor_tensor(cosg[:, n, :, 32:64], tabs[:, :, 0:32], gh, ALU.mult))
            pool.mark(POOL.tensor_tensor(sing[:, n, :, 32:64], tabs[:, :, 32:64], gl, ALU.mult))
            m = pool.mark(POOL.tensor_tensor(sing[:, n, :, 0:32], tabs[:, :, 32:64], gh, ALU.mult))
            pool.need(m)
            m_tab = pool.mark(POOL.tensor_scalar(sing[:, n, :, 0:32], sing[:, n, :, 0:32], -1.0, None, ALU.mult))

        xn = view(qkT_at, NXT, D)
        normed_features([(list(range(NXT)), 0)], hT, xn,
                        lambda k, w: vec[:, V_NG + k:V_NG + k + 1], lambda k, w: None)
        phase()

        sq = view(tmp_at, 512)
        qn = view(tmp_at + 512, 512)
        rot = view(tmp_at + 1024, 512)
        crs = view(tmp_at + 1536, 512)
        dve.need(m_tab)
        pool.need(m_tab)
        reads = {"qn": None, "rot": None}

        def rotary(b, m, kind, heads, t, dst, dup):
            n = heads * HD
            act.need(m, dve.last())
            ma = act.mark(ACTE.activation(sq[:, 0:n], psum[b][:, 0:n], ACT.Square))
            hs = stats[:, 0:heads]
            dve.need(ma)
            m1 = dve.mark(DVE.tensor_reduce(hs, sq[:, 0:n].rearrange("p (h d) -> p h d", d=HD), AX.X, ALU.add))
            dve.need(m1)
            m1 = dve.mark(DVE.tensor_scalar(hs, hs, 1.0 / HD, EPS, ALU.mult, ALU.add))
            act.need(m1)
            m1 = act.mark(ACTE.activation(hs, hs, ACT.Sqrt))
            dve.need(m1)
            m1 = dve.mark(DVE.reciprocal(hs, hs))
            dve.need(m1, reads["qn"])
            q3 = qn[:, 0:n].rearrange("p (h d) -> p h d", d=HD)
            r3 = rot[:, 0:n].rearrange("p (h d) -> p h d", d=HD)
            c3 = crs[:, 0:n].rearrange("p (h d) -> p h d", d=HD)
            m1 = dve.mark(DVE.tensor_tensor(q3, psum[b][:, 0:n].rearrange("p (h d) -> p h d", d=HD),
                                            hs.unsqueeze(2).to_broadcast([P, heads, HD]), ALU.mult))
            bank_free[b] = m1
            pool.need(m1, dve.last())
            pool.mark(POOL.tensor_tensor(c3[:, :, 0:32], q3[:, :, 32:64],
                                         sing[:, kind, t:t + 1, 0:32].to_broadcast([P, heads, 32]), ALU.mult))
            m2 = pool.mark(POOL.tensor_tensor(c3[:, :, 32:64], q3[:, :, 0:32],
                                              sing[:, kind, t:t + 1, 32:64].to_broadcast([P, heads, 32]), ALU.mult))
            reads["qn"] = m2
            dve.need(m1, reads["rot"])
            m3 = dve.mark(DVE.tensor_tensor(r3, q3, cosg[:, kind, t:t + 1, :].to_broadcast([P, heads, HD]), ALU.mult))
            dve.need(m2, m3)
            m3 = dve.mark(DVE.tensor_tensor(r3, r3, c3, ALU.add))
            if dup:
                d4 = qn[:, 0:4 * HD].rearrange("p (h c d) -> p h c d", c=2, d=HD)
                dve.need(m3)
                for c in range(2):
                    m3 = dve.mark(DVE.tensor_copy(d4[:, :, c, :], r3))
                src, pairs = qn, 2
            else:
                src, pairs = rot, 4
            b = bank()
            pe.need(m3)
            for j in range(pairs):
                i = PE.transpose(psum[b][:, j * P:(j + 1) * P], src[:, j * P:(j + 1) * P], ident)
            m4 = pe.mark(i)
            reads["rot"] = m4
            if dup:
                reads["qn"] = m4
            act.need(m4)
            got = psum[b][:, 0:pairs * P].rearrange("p (j t) -> p j t", t=P)
            if dup:
                for kv in range(2):
                    o = dst[:, 2 * kv:2 * kv + 2, t * P:(t + 1) * P]
                    m5 = act.mark(ACTE.activation(o, got[:, kv:kv + 1, :].to_broadcast([P, 2, P]), ACT.Copy))
            else:
                m5 = act.mark(ACTE.activation(dst[:, :, t * P:(t + 1) * P], got, ACT.Copy))
            bank_free[b] = m5

        def in_piece(c0, width, use):
            w, ready, s = fetch(ins["w_in"][0][:, c0:c0 + width], width)
            pe.need(ready)
            late = []
            for t in range(NXT):
                b, m = tok_product(hT, t, w, width)
                late.append((b, m, t))
                if len(late) > 1:
                    use(*late.pop(0))
            slot_free[s] = m
            use(*late.pop(0))

        def use_q(kind, dst):
            return lambda b, m, t: rotary(b, m, kind, 8, t, dst, False)

        def use_kv_a(b, m, t):
            act.need(m)
            v = psum[b][:, 128:256].rearrange("p (h d) -> p h d", d=HD)
            for kv in range(2):
                act.mark(ACTE.activation(vA[:, t, 2 * kv:2 * kv + 2, :], v[:, kv:kv + 1, :].to_broadcast([P, 2, HD]), ACT.Copy))
            rotary(b, m, 1, 2, t, kTA, True)

        def use_v_b(b, m, t):
            act.need(m)
            bank_free[b] = act.mark(ACTE.activation(vB[:, t, :, :].rearrange("p a b -> p (a b)"), psum[b][:], ACT.Copy))

        def use_gate(off):
            def f(b, m, t):
                act.need(m)
                bank_free[b] = act.mark(ACTE.activation(mix[:, t, off:off + 512], psum[b][:], ACT.Silu))
            return f
        in_piece(0, 512, use_q(0, qTA)); some_ada(2)
        in_piece(512, 256, use_kv_a); some_ada(1)
        in_piece(1280, 512, use_q(2, qTB)); some_ada(2)
        in_piece(1792, 512, use_q(3, kTB)); some_ada(2)
        in_piece(2304, 512, use_v_b); some_ada(2)
        in_piece(768, 512, use_gate(0)); some_ada(2)
        in_piece(2816, 512, use_gate(512)); some_ada(2)
        phase()

        NPB = 3
        pb = [view(zone + n * 512, 512) for n in range(NPB)]
        pT = [view(zone + (NPB + n) * 512, 512) for n in range(NPB)]
        qs = [view(zone + 2 * NPB * 512 + n * SEQ, SEQ) for n in range(2)]
        ks = [view(gate_at + n * SEQ, SEQ) for n in range(2)]
        st = view(stat_at + 128, 16, 8)
        S_B, T_B, O_B = (0, 1, 2), (3, 4, 5), (6, 7)
        maskA = const[:, C_MA:C_MA + 256]
        maskB = const[:, C_MB:C_MB + 512]
        with loop_over("attention", 4) as lp:
            i = lp.i
            def pair(x):
                return x[:, bass.ts(i, 1), :].rearrange("p a b -> p (a b)")
            pe_all = lp.prev("pe")
            dve.need(pe_all)
            pool.need(pe_all)
            mq = [dve.mark(DVE.tensor_copy(qs[0], pair(qTA))), dve.mark(DVE.tensor_copy(qs[1], pair(qTB)))]
            mk = [pool.mark(POOL.tensor_copy(ks[0], pair(kTA))), pool.mark(POOL.tensor_copy(ks[1], pair(kTB)))]
            units = [(k, par, t) for par in range(2) for k in range(2) for t in range(NXT)]
            state = {}

            def keys(k, t):
                return range(max(0, t - 1), t + 1) if k == 0 else range(t + 1)

            def scores(u):
                k, par, t = units[u]
                kt = keys(k, t)
                pe.need(mq[k], mk[k], state.get(("max", u - 3)) or lp.prev(f"max{(u - 3) % 16}"))
                half = slice(par * HD, par * HD + HD)
                kT = ks[k][half, kt[0] * P:(kt[-1] + 1) * P]
                state["s", u] = pe.mark(PE.matmul(psum[S_B[u % 3]][:, 0:len(kt) * P], qs[k][half, t * P:(t + 1) * P], kT,
                                                  start=True, stop=True))

            def softmax(u):
                k, par, t = units[u]
                n = len(keys(k, t)) * P
                mask = maskA[:, 256 - n:256] if k == 0 else maskB[:, 512 - n:512]
                c = st[:, u, :]
                dve.need(state["s", u], state.get(("tr", u - NPB)) or lp.prev(f"tr{(u - NPB) % 16}"))
                dve.mark(DVE.memset(c[:, 7:8], 0.0))
                m = dve.mark(DVE.tensor_tensor_reduce(pb[u % NPB][:, 0:n], psum[S_B[u % 3]][:, 0:n], mask, SCALE, NEG,
                                                      ALU.add, ALU.max, c[:, 0:1]))
                state["max", u] = m
                dve.need(m)
                if k == 0:
                    sk = bc[:, B_SK:B_SK + 8].rearrange("p (i h) -> p i h", h=2)[:, bass.ts(i, 1), par]
                    m = dve.mark(DVE.tensor_tensor(c[:, 0:1], c[:, 0:1], sk, ALU.max))
                    dve.need(m)
                m = dve.mark(DVE.tensor_scalar(c[:, 1:2], c[:, 0:1], -1.0, None, ALU.mult))
                act.need(m)
                m2 = act.mark(ACTE.activation(pb[u % NPB][:, 0:n], pb[u % NPB][:, 0:n], ACT.Exp, bias=c[:, 1:2],
                                              accum_out=c[:, 2:3]))
                if k == 0:
                    m2 = act.mark(ACTE.activation(c[:, 3:4], sk, ACT.Exp, bias=c[:, 1:2]))
                state["exp", u] = m2
                dve.need(m2)
                if k == 0:
                    m = dve.mark(DVE.tensor_tensor(c[:, 2:3], c[:, 2:3], c[:, 3:4], ALU.add))
                    dve.need(m)
                state["rec", u] = dve.mark(DVE.reciprocal(c[:, 4:5], c[:, 2:3]))

            def turn_p(u):
                k, par, t = units[u]
                n = len(keys(k, t))
                pe.need(state["exp", u], state.get(("pT", u - 3)) or lp.prev(f"pT{(u - 3) % 16}"))
                for j in range(n):
                    x = PE.transpose(psum[T_B[u % 3]][:, j * P:(j + 1) * P], pb[u % NPB][:, j * P:(j + 1) * P], ident)
                m = pe.mark(x)
                state["tr", u] = m
                act.need(m, state.get(("pv", u - NPB)) or lp.prev(f"pv{(u - NPB) % 16}"))
                state["pT", u] = act.mark(ACTE.activation(pT[u % NPB][:, 0:n * P], psum[T_B[u % 3]][:, 0:n * P], ACT.Copy))

            def value(u):
                k, par, t = units[u]
                kt_ = keys(k, t)
                pe.need(state["pT", u], state.get(("o", u - 2)) or lp.prev(f"o{(u - 2) % 16}"))
                o = psum[O_B[u % 2]][:, 0:HD]
                for j, kt in enumerate(kt_):
                    if k == 0:
                        v = vA[:, kt, bass.ts(i, 1), :].rearrange("p a b -> p (a b)")
                    else:
                        v = vB[:, kt, bass.ts(i, 1), par * HD:(par + 1) * HD].rearrange("p a b -> p (a b)")
                    x = PE.matmul(o, pT[u % NPB][:, j * P:(j + 1) * P], v, start=j == 0, stop=j == len(kt_) - 1)
                state["pv", u] = pe.mark(x)
                dve.need(state["pv", u], state["rec", u])
                g = mix[:, t, k * 512:(k + 1) * 512].rearrange("p (i n) -> p i n", n=P)[:, bass.ts(i, 1), par * HD:(par + 1) * HD]
                g = g.rearrange("p a b -> p (a b)")
                state["o", u] = dve.mark(DVE.scalar_tensor_tensor(g, o, st[:, u, 4:5], g, ALU.mult, ALU.mult))

            n = len(units)
            for u in range(n + 3):
                if u < n:
                    scores(u)
                    softmax(u)
                if u >= 1 and u - 1 < n:
                    turn_p(u - 1)
                if u >= 2 and u - 2 < n:
                    value(u - 2)
            for u in range(n - 3, n):
                for key in ("max", "tr", "pT", "pv", "o"):
                    lp.carry(f"{key}{u}", state[key, u])
            lp.carry("pe", pe.last())
        for n in range(8):
            bank_free[n] = [dve.last(), act.last()]
        phase()

        mT = view(qkT_at, KC, SEQ)

        def transposed(src, tiles, k_of, dst, dst_k, scale=None):
            for k in range(k_of):
                for ts in (tiles[i:i + 4] for i in range(0, len(tiles), 4)):
                    b = bank()
                    for j, t in enumerate(ts):
                        i = PE.transpose(psum[b][:, j * P:(j + 1) * P], src[:, t, k * P:(k + 1) * P], ident)
                    m = pe.mark(i)
                    o = dst[:, dst_k + k, ts[0] * P:(ts[-1] + 1) * P]
                    n = len(ts) * P
                    if k % 2:
                        dve.need(m)
                        if scale is None:
                            mo = dve.mark(DVE.tensor_copy(o, psum[b][:, 0:n]))
                        else:
                            mo = dve.mark(DVE.tensor_scalar(o, psum[b][:, 0:n], scale(k), None, ALU.mult))
                    else:
                        act.need(m)
                        mo = act.mark(ACTE.activation(o, psum[b][:, 0:n], ACT.Copy, scale=1.0 if scale is None else scale(k)))
                    bank_free[b] = mo
        transposed(mix, list(range(NXT)), KC, mT, 0)
        some_ada(3)
        phase()
        for h in range(2):
            w, ready, s = fetch(ins["w_out"][0][:, h * 512:(h + 1) * 512], 512)
            pe.need(ready)
            for t in range(NXT):
                b, m = tok_product(mT, t, w, 512)
                dve.need(m)
                r = resid[:, t, h * 512:(h + 1) * 512]
                bank_free[b] = dve.mark(DVE.tensor_tensor(r, r, psum[b][:], ALU.add))
            slot_free[s] = m
            some_ada(2)
        some_ada(24)
        phase()

        for l in range(LAYERS):
            last = l == LAYERS - 1
            xt, ct = list(range(NXT)), list(range(NXT, NT))
            streams = [(xt, 0), (ct, 1)]
            full = [(xt, 0)] if last else streams
            vl = V_L + l * V_LN
            V_GM, V_GF, V_CB, V_LG, V_LB, V_SB, V_SN = vl, vl + 8, vl + 16, vl + 20, vl + 24, vl + 28, vl + 36

            effs = view(stat_at + 256, 2, KC, 2)
            for n, (vg, sc) in enumerate(((V_GM, 8), (V_GF, 32))):
                m = dve.mark(DVE.tensor_scalar(effs[:, n, :, :], mods[:, l, sc:sc + 8, :], 1.0, None, ALU.add))
                dve.need(m)
                m = dve.mark(DVE.tensor_tensor(effs[:, n, :, :], effs[:, n, :, :],
                                               vec[:, vg:vg + 8].unsqueeze(2).to_broadcast([P, KC, 2]), ALU.mult))
            phase()

            def gate_rows(g0):
                for _, which in full:
                    for h in range(2):
                        b = bank()
                        for k in range(4):
                            col = mods[:, l, g0 + 4 * h + k, which:which + 1].to_broadcast([P, P])
                            i = PE.matmul(psum[b][:, k * P:(k + 1) * P], col, ident, start=True, stop=True)
                        m = pe.mark(i)
                        act.need(m)
                        bank_free[b] = act.mark(ACTE.activation(gates[:, which, h * 512:(h + 1) * 512], psum[b][:], ACT.Copy))

            z = zone
            hT = view(z, KC, TOK); h_at = z; z += KC * TOK
            sg_at = z; sg = view(z, 4, TOK); z += 4 * TOK
            vc_at = z; z += 3672
            zs_at = z; zs = view(z, NT, DS); z += NT * DS
            xp_at = z; z += KC * (TOK + 2 * (SK - 1))
            assert z <= 53200, z
            xn = view(sg_at, NT, D)
            normed_features(streams, hT, xn,
                            lambda k, w: effs[:, 0, k, w:w + 1], lambda k, w: mods[:, l, k, w:w + 1])
            phase()
            gate_rows(16)

            v1 = view(vc_at, 2, ROWS, GRID_W + CK - 1)
            v2 = view(vc_at + 2 * ROWS * (GRID_W + CK - 1), 2, SEQ)
            v3 = view(vc_at + 2 * ROWS * (GRID_W + CK - 1) + 2 * SEQ, 4, CTX + CK - 1)
            xbcx = view(xp_at, KC, SEQ + SK - 1)
            xbcc = view(xp_at + KC * (SEQ + SK - 1), KC, CTX + SK - 1)
            mz = pool.mark(POOL.memset(view(vc_at, 3672), 0.0))
            mz = pool.mark(POOL.memset(view(xp_at, KC * (TOK + 2 * (SK - 1))), 0.0))
            H2 = CK // 2
            H5 = SK // 2

            def feature_piece(c0, which_streams, use, nf=4):
                w, ready, s = fetch(ins["w_in_2"][l][:, c0:c0 + 128 * nf], 128 * nf)
                pe.need(ready)
                for f in range(nf):
                    for ts, which in which_streams:
                        b = bank()
                        n = len(ts) * P
                        for k in range(KC):
                            i = PE.matmul(psum[b][:, 0:n], w[:, k, f * P:(f + 1) * P], hT[:, k, ts[0] * P:ts[0] * P + n],
                                          start=k == 0, stop=k == KC - 1)
                        m = pe.mark(i)
                        use(b, m, f, ts, which, n)
                slot_free[s] = m

            def use_sig(b, m, f, ts, which, n):
                act.need(m)
                bank_free[b] = act.mark(ACTE.activation(sg[:, f, ts[0] * P:ts[0] * P + n], psum[b][:, 0:n], ACT.Sigmoid))

            def use_u(b, m, f, ts, which, n):
                dve.need(m, mz, act.last())
                s3 = sg[:, f, ts[0] * P:ts[0] * P + n]
                p3 = psum[b][:, 0:n]
                if which == 1:
                    o = v3[:, f, H2:H2 + CTX]
                elif f < 2:
                    o = v1[:, f, :, H2:H2 + GRID_W]
                    s3 = s3.rearrange("p (r c) -> p r c", c=GRID_W)
                    p3 = p3.rearrange("p (r c) -> p r c", c=GRID_W)
                else:
                    o = v2[:, f - 2, :]
                bank_free[b] = dve.mark(DVE.tensor_tensor(o, p3, s3, ALU.mult))

            def use_xbc(c):
                def f_(b, m, f, ts, which, n):
                    act.need(m, mz)
                    dst = (xbcx, xbcc)[which][:, c + f, H5:H5 + n]
                    bank_free[b] = act.mark(ACTE.activation(dst, psum[b][:, 0:n], ACT.Copy))
                return f_
            feature_piece(512, full, use_sig)
            feature_piece(0, full, use_u)
            w, ready, s = fetch(ins["w_in_2"][l][:, 1024:1536], 512)
            pe.need(ready)
            for ts, which in full:
                for t in ts:
                    b, m = tok_product(hT, t, w, 512)
                    act.need(m)
                    bank_free[b] = act.mark(ACTE.activation(zs[:, t, :], psum[b][:], ACT.Silu))
            slot_free[s] = m
            feature_piece(1536, streams, use_xbc(0))
            if last:
                feature_piece(2048, streams, use_xbc(4), nf=2)
                feature_piece(2304, full, use_xbc(6), nf=2)
            else:
                feature_piece(2048, streams, use_xbc(4))
            w, ready, s = fetch(ins["w_in_2"][l][:, 2560:2576], 16)
            pe.need(ready)
            dt = view(stat_at + 320, NT, 16)
            dta = view(stat_at + 416, NT, 16)
            e1 = view(stat_at + 512, NT, 16)
            av = view(stat_at + 608, 16)
            b = bank()
            for t in range(NT):
                for k in range(KC):
                    i = PE.matmul(psum[b][:, 16 * t:16 * t + 16], hT[:, k, t * P:(t + 1) * P], w[:, k, :],
                                  start=k == 0, stop=k == KC - 1)
            m = pe.mark(i)
            slot_free[s] = m
            dve.need(m)
            m = dve.mark(DVE.tensor_tensor(dt, psum[b][:, 0:16 * NT].rearrange("p (t n) -> p t n", n=16),
                                           bc[:, B_DTB + 16 * l:B_DTB + 16 * l + 16].unsqueeze(1).to_broadcast([P, NT, 16]), ALU.add))
            bank_free[b] = m
            act.need(m)
            m = act.mark(ACTE.activation(e1, dt, ACT.Abs))
            act.need(m)
            m = act.mark(ACTE.activation(e1, e1, ACT.Exp, scale=-1.0))
            act.need(m)
            m = act.mark(ACTE.activation(e1, e1, ACT.Ln, bias=1.0))
            ma = act.mark(ACTE.activation(av, bc[:, B_AL + 16 * l:B_AL + 16 * l + 16], ACT.Exp))
            dve.need(m)
            m = dve.mark(DVE.scalar_tensor_tensor(dt, dt, 0.0, e1, ALU.max, ALU.add))
            dve.need(m, ma)
            m = dve.mark(DVE.scalar_tensor_tensor(dta, dt, -1.0, av.unsqueeze(1).to_broadcast([P, NT, 16]), ALU.mult, ALU.mult))
            phase()

            xbc = view(h_at, KC, TOK)
            def taps5(src, c, n, o):
                cw = lambda j: vec[:, 4 * P + 40 * l + 8 * j + c:4 * P + 40 * l + 8 * j + c + 1]
                m = dve.mark(DVE.tensor_scalar(o, src[:, c, 0:n], cw(0), vec[:, V_SB + c:V_SB + c + 1], ALU.mult, ALU.add))
                for j in range(1, SK):
                    dve.need(m)
                    m = dve.mark(DVE.scalar_tensor_tensor(o, src[:, c, j:j + n], cw(j), o, ALU.mult, ALU.add))
                act.need(m)
                return act.mark(ACTE.activation(o, o, ACT.Silu))
            for c in range(KC):
                taps5(xbcx, c, SEQ, xbc[:, c, 0:SEQ])
                if c < 6 or not last:
                    taps5(xbcc, c, CTX, xbc[:, c, SEQ:TOK])
            cy = view(sg_at, 4, TOK)
            def wide(j, c):
                return vec[:, (2 + l) * P + 4 * j + c:(2 + l) * P + 4 * j + c + 1]
            for c in range(2):
                o = cy[:, c, 0:SEQ].rearrange("p (r w) -> p r w", w=GRID_W)
                m = dve.mark(DVE.tensor_scalar(o, v1[:, c, :, 0:GRID_W], wide(0, c), vec[:, V_CB + c:V_CB + c + 1], ALU.mult, ALU.add))
                for j in range(1, CK):
                    dve.need(m)
                    m = dve.mark(DVE.scalar_tensor_tensor(o, v1[:, c, :, j:j + GRID_W], wide(j, c), o, ALU.mult, ALU.add))
            for c in range(2):
                o = cy[:, 2 + c, 0:SEQ]
                m = dve.mark(DVE.tensor_scalar(o, v2[:, c, :], wide(H2, 2 + c), vec[:, V_CB + 2 + c:V_CB + 3 + c], ALU.mult, ALU.add))
                for d in range(1 - ROWS, ROWS):
                    if d == 0:
                        continue
                    r0, r1 = max(0, -d) * GRID_W, (ROWS - max(0, d)) * GRID_W
                    dve.need(m)
                    m = dve.mark(DVE.scalar_tensor_tensor(o[:, r0:r1], v2[:, c, r0 + d * GRID_W:r1 + d * GRID_W],
                                                          wide(H2 + d, 2 + c), o[:, r0:r1], ALU.mult, ALU.add))
            if not last:
                for c in range(4):
                    o = cy[:, c, SEQ:TOK]
                    m = dve.mark(DVE.tensor_scalar(o, v3[:, c, 0:CTX], wide(0, c), vec[:, V_CB + c:V_CB + c + 1], ALU.mult, ALU.add))
                    for j in range(1, CK):
                        dve.need(m)
                        m = dve.mark(DVE.scalar_tensor_tensor(o, v3[:, c, j:j + CTX], wide(j, c), o, ALU.mult, ALU.add))
            phase()

            sqv = view(vc_at, 4, 512)
            mu = view(vc_at + 2048, 512)
            rs = view(vc_at + 2560, 512)
            for ts, which in full:
                a, n = ts[0] * P, len(ts) * P
                b = bank()
                for c in range(4):
                    i = PE.matmul(psum[b][:, 0:n], ones, cy[:, c, a:a + n], start=c == 0, stop=c == 3)
                m = pe.mark(i)
                act.need(m, dve.last())
                m = act.mark(ACTE.activation(mu[:, 0:n], psum[b][:, 0:n], ACT.Copy, scale=1.0 / DC))
                bank_free[b] = m
                dve.need(m)
                m = dve.mark(DVE.tensor_tensor(cy[:, :, a:a + n], cy[:, :, a:a + n],
                                               mu[:, 0:n].unsqueeze(1).to_broadcast([P, 4, n]), ALU.subtract))
                act.need(m, pe.last())
                m = act.mark(ACTE.activation(sqv[:, :, 0:n], cy[:, :, a:a + n], ACT.Square))
                b = bank()
                pe.need(m)
                for c in range(4):
                    i = PE.matmul(psum[b][:, 0:n], ones, sqv[:, c, 0:n], start=c == 0, stop=c == 3)
                m = pe.mark(i)
                dve.need(m)
                m = dve.mark(DVE.tensor_scalar(rs[:, 0:n], psum[b][:, 0:n], 1.0 / DC, LN_EPS, ALU.mult, ALU.add))
                bank_free[b] = m
                act.need(m)
                m = act.mark(ACTE.activation(rs[:, 0:n], rs[:, 0:n], ACT.Sqrt))
                dve.need(m)
                m = dve.mark(DVE.reciprocal(rs[:, 0:n], rs[:, 0:n]))
                dve.need(m)
                m = dve.mark(DVE.tensor_tensor(cy[:, :, a:a + n], cy[:, :, a:a + n],
                                               rs[:, 0:n].unsqueeze(1).to_broadcast([P, 4, n]), ALU.mult))
                act.need(m)
                for c in range(4):
                    m = act.mark(ACTE.activation(cy[:, c, a:a + n], cy[:, c, a:a + n], ACT.Silu,
                                                 scale=vec[:, V_LG + c:V_LG + c + 1], bias=vec[:, V_LB + c:V_LB + c + 1]))
            tk = view(xp_at, NT, 6 * P)
            for t in range(NT):
                for c0, n in ((0, 4), (4, 2)):
                    b = bank()
                    for j in range(n):
                        i = PE.transpose(psum[b][:, j * P:(j + 1) * P], xbc[:, c0 + j, t * P:(t + 1) * P], ident)
                    m = pe.mark(i)
                    x = (dve, act)[t % 2]
                    x.need(m)
                    o, q = tk[:, t, c0 * P:(c0 + n) * P], psum[b][:, 0:n * P]
                    bank_free[b] = x.mark(DVE.tensor_copy(o, q) if t % 2 == 0 else ACTE.activation(o, q, ACT.Copy))
            phase()

            za = h_at
            ex = view(za, 4, NT, SH); za += 4 * NT * SH
            tot = view(za, NT, 16); za += NT * 16
            grow = view(za, SH, P); za += SH * P
            xw = view(za, DS); za += DS
            hst = view(za, DS); za += DS
            yt = view(za, DS); za += DS
            assert za <= h_at + 4 * TOK
            za = xp_at + NT * 6 * P
            md = view(za, SH, P); za += SH * P
            assert za <= 53200
            ef = view(vc_at + 3072 - 3072, 8)
            za = xp_at + NT * 6 * P + SH * P
            ys_at = vc_at
            ys = view(ys_at, NT, DS)
            E_at = za
            ef = view(za, SH, P); za += SH * P
            assert za <= 53200 + 0, za
            eb = grow
            dt_dir = lambda t, d: dt[:, t, 8 * d:8 * d + 8]
            b = bank()
            for n, (msk, d) in enumerate(((C_LE, 0), (C_GE, 1), (C_GT, 0), (C_LT, 1))):
                i = PE.matmul(psum[b][:, 48 * n:48 * n + 48].rearrange("p (t h) -> p t h", h=8), const[:, msk:msk + P],
                              dta[:, :, 8 * d:8 * d + 8], start=True, stop=True)
            i = PE.matmul(psum[b][:, 192:288].rearrange("p (t h) -> p t h", h=16), ones, dta, start=True, stop=True)
            m = pe.mark(i)
            act.need(m)
            act.mark(ACTE.activation(ex, psum[b][:, 0:192].rearrange("p (k t h) -> p k t h", t=NT, h=8), ACT.Exp))
            m = act.mark(ACTE.activation(tot, psum[b][:, 192:288].rearrange("p (t h) -> p t h", h=16), ACT.Exp))
            bank_free[b] = m
            dve.need(m)
            for d in range(2):
                m_ex = dve.mark(DVE.tensor_tensor(ex[:, 2 + d, :, :], ex[:, 2 + d, :, :], dt[:, :, 8 * d:8 * d + 8], ALU.mult))

            def cst(c):
                return const[:, c:c + P]

            def per_head(x, n):
                return x.unsqueeze(2).to_broadcast([P, SH, n])

            for ts, which in full:
                for t in ts:
                    cols = slice(t * P, (t + 1) * P)
                    bs = bank()
                    for g in range(2):
                        i = PE.matmul(psum[bs][:, g * P:(g + 1) * P], xbc[:, 4 + g, cols], xbc[:, 6 + g, cols], start=True, stop=True)
                    m_s = pe.mark(i)
                    for d in range(2):
                        row, colm, keep = ((C_GT, C_LE, C_LE), (C_LT, C_GE, C_GE))[d]
                        pool.need(pe.last(), dve.last())
                        mg = pool.mark(POOL.tensor_tensor(grow, cst(row).unsqueeze(1).to_broadcast([P, SH, P]),
                                                          per_head(dta[:, t, 8 * d:8 * d + 8], P), ALU.mult))
                        mm = pool.mark(POOL.tensor_tensor(md, cst(keep).unsqueeze(1).to_broadcast([P, SH, P]),
                                                          per_head(dt_dir(t, d), P), ALU.mult))
                        pe.need(mg)
                        e = (ef, eb)[d]
                        for q in range(2):
                            b = bank()
                            for h in range(4):
                                i = PE.matmul(psum[b][:, h * P:(h + 1) * P], grow[:, 4 * q + h, :], cst(colm), start=True, stop=True)
                            m = pe.mark(i)
                            act.need(m, dve.last())
                            if d and q == 0:
                                hold = (b, m)
                                continue
                            if d:
                                bb, _ = hold
                                bank_free[bb] = act.mark(ACTE.activation(e[:, 0:4, :], psum[bb][:].rearrange("p (h l) -> p h l", l=P), ACT.Exp))
                            bank_free[b] = act.mark(ACTE.activation(e[:, 4 * q:4 * q + 4, :], psum[b][:].rearrange("p (h l) -> p h l", l=P), ACT.Exp))
                        dve.need(act.last(), mm)
                        m = dve.mark(DVE.tensor_tensor(e, e, md, ALU.mult))
                    dve.need(m)
                    m = dve.mark(DVE.tensor_tensor(ef, ef, eb, ALU.add))
                    dve.need(m, m_s)
                    for g in range(2):
                        m = dve.mark(DVE.tensor_tensor(ef[:, 4 * g:4 * g + 4, :], ef[:, 4 * g:4 * g + 4, :],
                                                       psum[bs][:, g * P:(g + 1) * P].unsqueeze(1).to_broadcast([P, 4, P]), ALU.mult))
                    bank_free[bs] = m
                    pool.mark(POOL.tensor_tensor(ys[:, t, :].rearrange("p (h n) -> p h n", n=HD), tk[:, t, 0:DS].rearrange("p (h n) -> p h n", n=HD),
                                                 per_head(bc[:, B_DS + 8 * l:B_DS + 8 * l + 8], HD), ALU.mult))
                    b = bank()
                    pe.need(m)
                    for h in range(SH):
                        i = PE.matmul(psum[b][:, h * HD:(h + 1) * HD], ef[:, h, :], tk[:, t, h * HD:(h + 1) * HD], start=True, stop=True)
                    m = pe.mark(i)
                    dve.need(m, pool.last())
                    bank_free[b] = dve.mark(DVE.tensor_tensor(ys[:, t, :], ys[:, t, :], psum[b][:], ALU.add))

            for d in range(2):
                dve.need(pe.last())
                m_h = dve.mark(DVE.memset(hst, 0.0))
                order = (ct + xt) if d == 0 else (ct[::-1] + xt[::-1])
                for t in order:
                    cols = slice(t * P, (t + 1) * P)
                    if t in [q for ts, _ in full for q in ts]:
                        b = bank()
                        pe.need(m_h)
                        for g in range(2):
                            i = PE.matmul(psum[b][:, g * 256:(g + 1) * 256], xbc[:, 6 + g, cols], hst[:, g * 256:(g + 1) * 256], start=True, stop=True)
                        m = pe.mark(i)
                        dve.need(m, m_ex)
                        m = dve.mark(DVE.tensor_tensor(yt.rearrange("p (h n) -> p h n", n=HD), psum[b][:].rearrange("p (h n) -> p h n", n=HD),
                                                       per_head(ex[:, d, t, :], HD), ALU.mult))
                        bank_free[b] = m
                        dve.need(m)
                        m = dve.mark(DVE.tensor_tensor(ys[:, t, :], ys[:, t, :], yt, ALU.add))
                    if t == order[-1]:
                        continue
                    pool.need(m_ex, pe.last())
                    mw = pool.mark(POOL.tensor_tensor(xw.rearrange("p (h n) -> p h n", n=HD), tk[:, t, 0:DS].rearrange("p (h n) -> p h n", n=HD),
                                                      per_head(ex[:, 2 + d, t, :], HD), ALU.mult))
                    b = bank()
                    pe.need(mw)
                    for g in range(2):
                        i = PE.matmul(psum[b][:, g * 256:(g + 1) * 256], tk[:, t, DS + g * P:DS + (g + 1) * P], xw[:, g * 256:(g + 1) * 256], start=True, stop=True)
                    m = pe.mark(i)
                    dve.need(m, m_h)
                    m = dve.mark(DVE.tensor_tensor(hst.rearrange("p (h n) -> p h n", n=HD), hst.rearrange("p (h n) -> p h n", n=HD),
                                                   per_head(tot[:, t, 8 * d:8 * d + 8], HD), ALU.mult))
                    dve.need(m)
                    m_h = dve.mark(DVE.tensor_tensor(hst, hst, psum[b][:], ALU.add))
                    bank_free[b] = m_h
            dve.need(dve.last())
            mt = [q for ts, _ in full for q in ts]
            m = dve.mark(DVE.tensor_tensor(ys[:, 0:len(mt), :], ys[:, 0:len(mt), :], zs[:, 0:len(mt), :], ALU.mult))
            act.need(m)
            m = rms_rows(mt, DS, lambda t: ys[:, t, :], yt)
            dve.need(m)
            m = dve.mark(DVE.tensor_tensor(ys[:, 0:len(mt), :], ys[:, 0:len(mt), :],
                                           stats[:, 0:len(mt)].unsqueeze(2).to_broadcast([P, len(mt), DS]), ALU.mult))
            phase()
            syT = view(xp_at, 4, TOK)
            for ts, _ in full:
                transposed(ys, ts, 4, syT, 0, lambda k: vec[:, V_SN + k:V_SN + k + 1])
            phase()
            prod = view(h_at, 4, 512)
            uses = [None] * 4
            for h in range(2):
                w, ready, s = fetch(ins["w_out_2"][l][:, h * 512:(h + 1) * 512], 512)
                pe.need(ready)
                for ts, which in full:
                    for t in ts:
                        b = bank()
                        for k in range(KC):
                            src = cy[:, k, t * P:(t + 1) * P] if k < 4 else syT[:, k - 4, t * P:(t + 1) * P]
                            i = PE.matmul(psum[b][:], src, w[:, k, :], start=k == 0, stop=k == KC - 1)
                        m = pe.mark(i)
                        u = t % 4
                        dve.need(m, uses[u])
                        m1 = dve.mark(DVE.tensor_tensor(prod[:, u, :], psum[b][:], gates[:, which, h * 512:(h + 1) * 512], ALU.mult))
                        bank_free[b] = m1
                        pool.need(m1)
                        r = resid[:, t, h * 512:(h + 1) * 512]
                        uses[u] = pool.mark(POOL.tensor_tensor(r, r, prod[:, u, :], ALU.add))
                slot_free[s] = m
            phase()

            z = zone
            tT = view(z, KC, TOK); z += KC * TOK
            acc = view(z, NT, D); acc_at = z; z += NT * D
            hid = [view(z + n * 2 * TOK, 2, TOK) for n in range(2)]; z += 4 * TOK
            silg = view(z, 2, 512); z += 1024
            prod = view(z, 4, 512); z += 2048
            lg_at = z; z += 2048
            assert z <= 53200, z
            normed_features(full, tT, acc, lambda k, w: effs[:, 1, k, w:w + 1], lambda k, w: mods[:, l, 24 + k, w:w + 1])
            phase()
            gate_rows(40)
            n_t = len(mt)
            lg = view(lg_at, n_t, 20)
            q = [lg_at + NT * 20]

            def tile(*dims):
                n = 1
                for x in dims:
                    n *= x
                v = view(q[0], *dims)
                q[0] += n
                return v
            b = bank()
            for t in mt:
                for k in range(KC):
                    i = PE.matmul(psum[b][:, 20 * t:20 * t + 20], tT[:, k, t * P:(t + 1) * P], router[:, l, k, :], start=k == 0, stop=k == KC - 1)
            m = pe.mark(i)

            def v_op(inst):
                m = dve.mark(inst)
                dve.need(m)
                return m
            dve.need(m)
            bank_free[b] = v_op(DVE.tensor_tensor(lg, psum[b][:, 0:20 * n_t].rearrange("p (t n) -> p t n", n=20),
                                                  bc[:, B_BR + 20 * l:B_BR + 20 * l + 20].unsqueeze(1).to_broadcast([P, n_t, 20]), ALU.add))

            def first_max(src, n, name):
                mx, oh, free = tile(n_t, 1), tile(n_t, n), tile(n_t, 1)
                v_op(DVE.tensor_reduce(mx.rearrange("p a b -> p (a b)"), src, AX.X, ALU.max))
                v_op(DVE.tensor_tensor(oh, src, mx.to_broadcast([P, n_t, n]), ALU.is_equal))
                v_op(DVE.tensor_scalar(free, oh[:, :, 0:1], -1.0, 1.0, ALU.mult, ALU.add))
                for j in range(1, n):
                    v_op(DVE.tensor_tensor(oh[:, :, j:j + 1], oh[:, :, j:j + 1], free, ALU.mult))
                    if j < n - 1:
                        v_op(DVE.tensor_tensor(free, free, oh[:, :, j:j + 1], ALU.subtract))
                return mx, oh
            gm, gsel = first_max(lg[:, :, 0:4], 4, "g")
            dif = tile(n_t, 4)
            m = v_op(DVE.tensor_tensor(dif, lg[:, :, 0:4], gm.to_broadcast([P, n_t, 4]), ALU.subtract))
            act.need(m)
            m = act.mark(ACTE.activation(dif, dif, ACT.Exp))
            dve.need(m)
            gp = tile(n_t, 1)
            v_op(DVE.tensor_reduce(gp.rearrange("p a b -> p (a b)"), dif, AX.X, ALU.add))
            el, pr = tile(n_t, 4), tile(n_t, 4)
            for g in range(NG):
                dst = el if g == 0 else pr
                v_op(DVE.tensor_tensor(dst, lg[:, :, 4 + 4 * g:8 + 4 * g], gsel[:, :, g:g + 1].to_broadcast([P, n_t, 4]), ALU.mult))
                if g:
                    v_op(DVE.tensor_tensor(el, el, pr, ALU.add))
            m1_, oh1 = first_max(el, 4, "1")
            v_op(DVE.scalar_tensor_tensor(el, oh1, -1e30, el, ALU.mult, ALU.add))
            m2_, oh2 = first_max(el, 4, "2")
            e2, w1 = tile(n_t, 1), tile(n_t, 1)
            m = v_op(DVE.tensor_tensor(e2, m2_, m1_, ALU.subtract))
            act.need(m)
            m = act.mark(ACTE.activation(e2, e2, ACT.Exp))
            dve.need(m)
            v_op(DVE.scalar_tensor_tensor(w1, e2, 1.0, gp, ALU.add, ALU.mult))
            v_op(DVE.reciprocal(w1, w1))
            v_op(DVE.tensor_tensor(e2, e2, w1, ALU.mult))
            v_op(DVE.tensor_tensor(oh1, oh1, w1.to_broadcast([P, n_t, 4]), ALU.mult))
            v_op(DVE.tensor_tensor(oh2, oh2, e2.to_broadcast([P, n_t, 4]), ALU.mult))
            v_op(DVE.tensor_tensor(oh1, oh1, oh2, ALU.add))
            cw = tile(NE, n_t)
            for g in range(NG):
                m_cw = v_op(DVE.tensor_tensor(cw[:, 4 * g:4 * g + 4, :].rearrange("p e t -> p t e"), oh1,
                                              gsel[:, :, g:g + 1].to_broadcast([P, n_t, 4]), ALU.mult))
            assert q[0] <= lg_at + 2048
            m = dve.mark(DVE.memset(acc[:, 0:n_t, :], 0.0))
            phase()
            for n in range(NSLOT):
                spl.need(slot_free[n])
            with loop_over(f"experts{l}", NE // 2) as lp:
                i = lp.i
                use = {}
                for u in range(2):
                    gu = sb[:, ring_at + 2 * u * SLOT:ring_at + (2 * u + 1) * SLOT].rearrange("p (g k n) -> p g k n", g=2, n=FF)
                    dn = sb[:, ring_at + (2 * u + 1) * SLOT:ring_at + (2 * u + 1) * SLOT + 2 * D].rearrange("p (k n) -> p k n", n=D)
                    spl.need(lp.prev(f"gu{u}"))
                    for j, name in enumerate(("w_gate_2", "w_up_2")):
                        sp.dma_start(gu[:, j, :, :], ins[name][l][bass.ts(i * 2 + u, 1), :, :].rearrange("e (k p) n -> p (e k) n", p=P)).then_inc(slot_full[2 * u], 16)
                    spl.need(lp.prev(f"dn{u}"))
                    sp.dma_start(dn, ins["w_down_2"][l][bass.ts(i * 2 + u, 1), :, :].rearrange("e (k p) n -> p (e k) n", p=P)).then_inc(slot_full[2 * u + 1], 16)
                    pe.eng.wait_ge(slot_full[2 * u], i * 32 + (slot_count[2 * u] + 32))
                    nb = [0]

                    def bk(fam):
                        key = (fam, u, nb[0])
                        n = (0, 1, 2, 3)[nb[0] % 4] if fam == "gu" else 4 + nb[0] % 4
                        nb[0] += 1
                        pe.need(use.get(("bank", n)) or lp.prev(f"bank{n}"))
                        return n
                    for f in range(2):
                        for ts, which in full:
                            n = len(ts) * P
                            c = slice(ts[0] * P, ts[0] * P + n)
                            bg, bu = bk("gu"), bk("gu")
                            for j, bj in ((0, bg), (1, bu)):
                                for k in range(KC):
                                    x = PE.matmul(psum[bj][:, 0:n], gu[:, j, k, f * P:(f + 1) * P], tT[:, k, c], start=k == 0, stop=k == KC - 1)
                                m = pe.mark(x)
                            w = f if which == 0 else f
                            act.need(m, use.get(("sil", f)) or lp.prev(f"sil{f}"))
                            ms = act.mark(ACTE.activation(silg[:, f, 0:n], psum[bg][:, 0:n], ACT.Silu))
                            use["bank", bg] = ms
                            dve.need(ms, m, use.get(("hid", u)) or lp.prev(f"hid{u}"))
                            mh = dve.mark(DVE.tensor_tensor(hid[u][:, f, c], silg[:, f, 0:n], psum[bu][:, 0:n], ALU.mult))
                            use["bank", bu] = mh
                            use["sil", f] = mh
                    lp.carry(f"gu{u}", pe.last())
                    pe.eng.wait_ge(slot_full[2 * u + 1], i * 16 + (slot_count[2 * u + 1] + 16))
                    pe.need(mh)
                    nb[0] = 0
                    for t in mt:
                        for h in range(2):
                            bd = bk("dn")
                            for k in range(2):
                                x = PE.matmul(psum[bd][:], hid[u][:, k, t * P:(t + 1) * P], dn[:, k, h * 512:(h + 1) * 512], start=k == 0, stop=k == 1)
                            m = pe.mark(x)
                            a = acc[:, t, h * 512:(h + 1) * 512]
                            dve.need(m, use.get(("acc", t, h)) or lp.prev(f"acc{t}{h}"))
                            wcol = cw[:, bass.ts(i * 2 + u, 1), t]
                            use["acc", t, h] = dve.mark(DVE.scalar_tensor_tensor(a, psum[bd][:], wcol, a, ALU.mult, ALU.add))
                            use["bank", bd] = use["acc", t, h]
                    use["hid", u] = m
                    lp.carry(f"hid{u}", m)
                    lp.carry(f"dn{u}", m)
                for key, mk in use.items():
                    if key[0] != "hid":
                        lp.carry(key[0] + "".join(str(x) for x in key[1:]), mk)
            for u in range(2):
                slot_count[2 * u] += 32 * (NE // 2)
                slot_count[2 * u + 1] += 16 * (NE // 2)
            for n in range(8):
                bank_free[n] = [dve.last(), act.last()]
            for n in range(NSLOT):
                slot_free[n] = pe.last()
            phase()
            uses = [None] * 4
            for h in range(2):
                for ts, which in full:
                    for t in ts:
                        a = acc[:, t, h * 512:(h + 1) * 512]
                        m1 = dve.mark(DVE.tensor_tensor(a, a, gates[:, which, h * 512:(h + 1) * 512], ALU.mult))
                        pool.need(m1)
                        r = resid[:, t, h * 512:(h + 1) * 512]
                        pool.mark(POOL.tensor_tensor(r, r, a, ALU.add))
            phase()

        yo = view(zone, NXT, D)
        m = rms_rows(list(range(NXT)), D, lambda t: resid[:, t, :], yo[:, 0, :])
        dve.need(m)
        s_out = sem("out_stored")
        for t in range(NXT):
            m = dve.mark(DVE.scalar_tensor_tensor(yo[:, t, :], resid[:, t, :], stats[:, t:t + 1], bc[:, B_GF:B_GF + D], ALU.mult, ALU.mult))
            spl.need(m)
            sp.dma_start(out[0, t * P:(t + 1) * P, :], yo[:, t, :]).then_inc(s_out, 16)
        sp.wait_ge(s_out, 16 * NXT)
    return book.found


_NAMES = ["x", "norm_gain", "w_in", "q_norm_a", "k_norm_a", "sinks_a", "q_norm_b", "k_norm_b", "w_out", "c_2", "ctx_2",
          "c_ctx_2", "w_ada_2", "b_ada_2", "g_mix_2", "g_ffn_2", "w_in_2", "conv_w_2", "conv_b_2", "conv_ln_g_2",
          "conv_ln_b_2", "ssd_conv_w_2", "ssd_conv_b_2", "dt_bias_2", "a_log_2", "d_skip_2", "ssd_norm_g_2",
          "w_out_2", "w_router_group_2", "b_router_group_2", "w_router_expert_2", "b_router_expert_2", "w_gate_2",
          "w_up_2", "w_down_2", "g_final_2"]


def _constants():
    import numpy as np
    r, s = np.arange(P)[:, None], np.arange(P)[None, :]
    c = np.zeros((P, NCONST), np.float32)
    c[:, C_ID:C_ID + P] = r == s
    c[:, C_LE:C_LE + P] = r <= s
    c[:, C_LT:C_LT + P] = r < s
    c[:, C_GE:C_GE + P] = r >= s
    c[:, C_GT:C_GT + P] = r > s
    c[:, C_ONE:C_ONE + P] = 1.0
    dist = r - np.arange(2 * P)[None, :] + P
    c[:, C_MA:C_MA + 2 * P] = np.where((dist >= 0) & (dist <= P - 1), 0.0, NEG)
    dist = r - np.arange(4 * P)[None, :] + 3 * P
    count = ((dist >= 0) & (dist <= 128)) * 1 + ((dist >= 0) & (dist % 4 == 0)) * 1 + ((dist >= 0) & (dist % 16 == 0)) * 1
    c[:, C_MB:C_MB + 4 * P] = np.where(count > 0, np.log(np.maximum(count, 1)) / SCALE, NEG)
    half = HD // 2
    inv = np.float32(10000.0) ** (-np.arange(half, dtype=np.float32) / np.float32(half))
    ang = (np.arange(SEQ, dtype=np.float32)[:, None] * inv[None, :]).astype(np.float32)
    tab = np.concatenate([np.cos(ang), np.sin(ang)], axis=1).reshape(NXT, P, HD)
    c[:, C_CS:] = tab.transpose(1, 0, 2).reshape(P, NXT * HD)
    return c


def kernel(**inputs):
    import numpy as np
    import concourse.bacc as bacc
    from concourse.bass_utils import run_bass_kernel_spmd as run
    arrays = {n: np.ascontiguousarray(inputs[n]) for n in _NAMES}
    arrays["consts"] = _constants()
    known = {}
    for _ in range(2):
        nc = bacc.Bacc("TRN2", target_bir_lowering=False, num_devices=1)
        ins = {n: nc.dram_tensor("in_" + n, a.shape, mybir.dt.from_np(a.dtype), kind="ExternalInput").ap()
               for n, a in arrays.items()}
        out = nc.dram_tensor("out", (1, SEQ, D), F32, kind="ExternalOutput").ap()
        known = program(nc, ins, out, known)
    r = run(nc, [{"in_" + n: a for n, a in arrays.items()}], core_ids=[0])
    return r.results[0]["out"]
```

```python
import concourse.bass as bass
from concourse import mybir
from contextlib import ExitStack

F32 = mybir.dt.float32
ALU = mybir.AluOpType
ACT = mybir.ActivationFunctionType
AX = mybir.AxisListType

P = 128
D = 1024
KC = D // P
SEQ, CTX = 512, 256
NXT, NCT = SEQ // P, CTX // P
NT = NXT + NCT
TOK = SEQ + CTX
EPS, LN_EPS = 1e-6, 1e-5
HD = 64
AH = BH = 8
AKV = 2
SCALE = HD ** -0.5
NEG = -1e30
LAYERS = 2
GRID_W = 64
ROWS = SEQ // GRID_W
CK, SK = 31, 5
DC = DS = 512
SH = 8
NS_ = 128
DIN = 2576
NG, NPG, NE = 4, 4, 16
FF = 256
BLOCKS = (2, 1)

C_ID, C_LE, C_LT, C_GE, C_GT, C_ONE = (P * n for n in range(6))
C_MA = 6 * P
C_MB = C_MA + 2 * P
C_CS = C_MB + 4 * P
C_IO = C_CS + 4 * HD
C_TOK = C_IO + 256
NCONST = C_TOK + 2 * NT
V_NG, V_C, V_CC = 0, 8, 16
V_L = 24
V_LN = 40
B_QK, B_SK, B_DTB, B_AL, B_DS, B_BR, B_GF = 0, 256, 264, 296, 328, 344, 384
NB = B_GF + D


NEVER = -1 << 30


class Mark:

    def __init__(self, sem, count, loop):
        self.sem, self.count, self.loop = sem, count, loop

    def value(self):
        if self.loop is None:
            return self.count
        return self.loop.value(self.sem, self.count)


class Loop:

    def __init__(self, book, name, n):
        self.book, self.name, self.n = book, name, n
        self.i = None
        self.base = {}
        self.local = {}
        self.per = book.known.get(name, {}).get("per", {})
        self.carried = book.known.get(name, {}).get("carry", {})
        self.out = {}

    def value(self, sem, count):
        k = sem.name
        if self.i is None:
            return self.base[k] + (self.n - 1) * self.local.get(k, 0) + count
        return self.base[k] + count + self.i * self.per.get(k, 0)

    def prev(self, name):
        if name not in self.carried:
            return None
        k, count = self.carried[name]
        return Prev(self, self.book.sems[k], count - self.per[k])

    def ahead(self, lane, less):
        return Mark(lane.sem, -less, self)

    def carry(self, name, mark):
        self.out[name] = (mark.sem.name, mark.count)


class Prev:
    def __init__(self, loop, sem, count):
        self.loop, self.sem, self.count = loop, sem, count

    def value(self):
        return self.loop.value(self.sem, self.count)


class Book:

    def __init__(self, known):
        self.known, self.sems, self.loop, self.found = known, {}, None, {}
        self.lanes = []


class Lane:

    def __init__(self, book, eng, sem, by=1):
        self.book, self.eng, self.sem, self.by, self.count = book, eng, sem, by, 0
        self.seen = {}
        book.sems[sem.name] = sem
        book.lanes.append(self)

    def mark(self, inst):
        inst.then_inc(self.sem, self.by)
        loop = self.book.loop
        if loop is None:
            self.count += self.by
            return Mark(self.sem, self.count, None)
        k = self.sem.name
        loop.local[k] = loop.local.get(k, 0) + self.by
        return Mark(self.sem, loop.local[k], loop)

    def last(self):
        loop = self.book.loop
        if loop is None:
            return Mark(self.sem, self.count, None)
        return Mark(self.sem, loop.local.get(self.sem.name, 0), loop)

    def need(self, *marks):
        best = {}
        todo = list(marks)
        while todo:
            m = todo.pop(0)
            if m is None:
                continue
            if isinstance(m, (list, tuple)):
                todo = list(m) + todo
                continue
            k = (m.sem.name, id(m.loop) if m.loop is not None and m.loop.i is not None else None)
            size = m.count if k[1] else m.value()
            if k not in best or best[k][0] < size:
                best[k] = (size, m)
        for (name, in_loop), (size, m) in best.items():
            if in_loop:
                if self.seen.get((name, in_loop), NEVER) >= size:
                    continue
                self.seen[name, in_loop] = size
            else:
                if self.seen.get(name, 0) >= size or size <= 0:
                    continue
                if self.book.loop is None:
                    self.seen[name] = size
            self.eng.wait_ge(m.sem, m.value())


def stage(nc, name):
    pass


def program(nc, ins, out, known):
    book = Book(known)
    ctx = ExitStack()
    with ctx:
        def sem(name):
            return ctx.enter_context(nc.semaphore(name))

        pe = Lane(book, nc.tensor, sem("pe_done"))
        dve = Lane(book, nc.vector, sem("dve_done"))
        act = Lane(book, nc.scalar, sem("act_done"))
        pool = Lane(book, nc.gpsimd, sem("pool_done"))
        sp = nc.sync
        PE, DVE, ACTE, POOL = nc.tensor, nc.vector, nc.scalar, nc.gpsimd
        lanes = [pe, dve, act, pool]

        spl = Lane(book, nc.sync, sem("sync_done"))

        class loop_over:

            def __init__(self, name, n):
                self.loop = Loop(book, name, n)

            def __enter__(self):
                lp = self.loop
                for x in book.lanes:
                    lp.base[x.sem.name] = x.count
                self.cm = nc.Fori(0, lp.n)
                lp.i = self.cm.__enter__()
                book.loop = lp
                return lp

            def __exit__(self, *a):
                lp = self.loop
                self.cm.__exit__(*a)
                book.loop, lp.i = None, None
                for x in book.lanes:
                    x.count += lp.n * lp.local.get(x.sem.name, 0)
                book.found[lp.name] = {"per": dict(lp.local), "carry": dict(lp.out)}

        def phase(name=""):
            stage(nc, name)
            marks = [x.last() for x in lanes]
            for x in lanes:
                x.need(*marks)

        sb = ctx.enter_context(nc.sbuf_tensor("arena", [P, 53200], F32))
        top = [0]

        def place(n):
            at = top[0]
            top[0] += n
            return at

        def view(at, *dims):
            n = 1
            for d in dims:
                n *= d
            v = sb[:, at:at + n]
            if len(dims) == 2:
                v = v.rearrange("p (a b) -> p a b", b=dims[1])
            elif len(dims) == 3:
                v = v.rearrange("p (a b c) -> p a b c", b=dims[1], c=dims[2])
            return v

        NSLOT = 4
        SLOT = KC * 512
        ring_at = place(NSLOT * SLOT)
        resid = view(place(NT * D), NT, D)
        const = view(place(NCONST), NCONST)
        vec = view(place(5 * P), 5 * P)
        bc = view(place(NB), NB)
        mods = view(place(LAYERS * 48 * 2), LAYERS, 48, 2)
        router = view(place(LAYERS * KC * 20), LAYERS, KC, 20)
        gate_at = place(2 * D)
        gates = view(gate_at, 2, D)
        stat_at = place(1024)
        zone = top[0]
        ident = const[:, C_ID:C_ID + P]
        ones = const[:, C_ONE:C_ONE + P]

        psum = [ctx.enter_context(nc.psum_tensor(f"psum{n}", [P, 512], F32)) for n in range(8)]
        bank_free = [None] * 8
        turn = [0]

        def bank():
            n = turn[0] % 8
            turn[0] += 1
            pe.need(bank_free[n])
            return n

        slot_full = [Lane(book, None, sem(f"slot_full{n}"), 16) for n in range(NSLOT)]
        slot_free = [None] * NSLOT
        slot_turn = [0]

        def slot_view(n, width):
            return sb[:, ring_at + n * SLOT:ring_at + n * SLOT + KC * width].rearrange("p (k n) -> p k n", n=width)

        def fetch(src, width):
            n = slot_turn[0] % NSLOT
            slot_turn[0] += 1
            spl.need(slot_free[n])
            dst = slot_view(n, width)
            return dst, slot_full[n].mark(sp.dma_start(dst, src.rearrange("(k p) n -> p k n", p=P))), n

        tok_dram = [nc.dram_tensor(f"tokens{l}", (SEQ if l == LAYERS - 1 else TOK, D), F32, kind="Internal").ap() for l in range(LAYERS)]
        out_dram = [nc.dram_tensor(f"expert_out{l}", (NE * BLOCKS[l] * P, D), F32, kind="Internal").ap() for l in range(LAYERS)]
        tok_stored = Lane(book, None, sem("tokens_stored"), 16)
        gx_full = [Lane(book, None, sem(f"gathered{n}"), 16) for n in range(4)]
        yg_full = [Lane(book, None, sem(f"collected{n}"), 16) for n in range(4)]
        y_stored = [Lane(book, None, sem(f"expert_out_stored{n}"), 16) for n in range(2)]

        s_small = sem("small_loaded")
        rows = view(zone, 5, P)
        small = [0]

        def load(dst, src):
            nc.scalar.dma_start(dst, src).then_inc(s_small, 16)
            small[0] += 16
        load(const, ins["consts"])
        load(resid[:, 0:NXT, :], ins["x"][0].rearrange("(t p) d -> p t d", p=P))

        def load_rows(g, r, src, n):
            load(rows[r:r + n, g, :], src)
        load_rows(0, V_NG, ins["norm_gain"].rearrange("a (k n) -> (a k) n", n=P), 8)
        load_rows(0, V_C, ins["c_2"].rearrange("a (k n) -> (a k) n", n=P), 8)
        load_rows(0, V_CC, ins["c_ctx_2"].rearrange("(k n) -> k n", n=P), 8)
        for l in range(LAYERS):
            at = V_L + l * V_LN
            for name, n in (("g_mix_2", 8), ("g_ffn_2", 8), ("conv_b_2", 4), ("conv_ln_g_2", 4),
                            ("conv_ln_b_2", 4), ("ssd_conv_b_2", 8), ("ssd_norm_g_2", 4)):
                load_rows(0, at, ins[name][l].rearrange("(k n) -> k n", n=P), n)
                at += n
            load_rows(1, l * 48, ins["b_ada_2"][l].rearrange("(k n) -> k n", n=P), 48)
            load_rows(2 + l, 0, ins["conv_w_2"][l].rearrange("t (k n) -> (t k) n", n=P), 4 * CK)
            load_rows(4, l * 40, ins["ssd_conv_w_2"][l].rearrange("t (k n) -> (t k) n", n=P), 8 * SK)

        def load_bc(at, src):
            n = src.shape[-1]
            load(bc[:, at:at + n], src.partition_broadcast(P))
        for n, name in enumerate(("q_norm_a", "k_norm_a", "q_norm_b", "k_norm_b")):
            load_bc(B_QK + n * HD, ins[name][0])
        load_bc(B_SK, ins["sinks_a"][0])
        for l in range(LAYERS):
            load_bc(B_DTB + l * 16, ins["dt_bias_2"][l].rearrange("a h -> (a h)"))
            load_bc(B_AL + l * 16, ins["a_log_2"][l].rearrange("a h -> (a h)"))
            load_bc(B_DS + l * 8, ins["d_skip_2"][l])
            load_bc(B_BR + l * 20, ins["b_router_group_2"][l])
            load_bc(B_BR + l * 20 + 4, ins["b_router_expert_2"][l])
            load(router[:, l, :, 0:4], ins["w_router_group_2"][l].rearrange("(k p) n -> p k n", p=P))
            load(router[:, l, :, 4:20], ins["w_router_expert_2"][l].rearrange("(k p) n -> p k n", p=P))
        load_bc(B_GF, ins["g_final_2"])
        load(resid[:, NXT:NT, :], ins["ctx_2"][0].rearrange("(t p) d -> p t d", p=P))
        m_small = Mark(s_small, small[0], None)

        for x in lanes:
            x.need(m_small)
        nrow = [V_L + 2 * V_LN, 96, 4 * CK, 4 * CK, 80]
        b = bank()
        for g in range(4):
            m = pe.mark(PE.transpose(psum[b][:, g * P:g * P + nrow[g]], rows[0:nrow[g], g, :], ident[0:nrow[g], 0:nrow[g]]))
        b2 = bank()
        m2 = pe.mark(PE.transpose(psum[b2][:, 0:nrow[4]], rows[0:nrow[4], 4, :], ident[0:nrow[4], 0:nrow[4]]))
        dve.need(m)
        for g in range(4):
            mv = dve.mark(DVE.tensor_copy(vec[:, g * P:g * P + nrow[g]], psum[b][:, g * P:g * P + nrow[g]]))
        dve.need(m2)
        mv = dve.mark(DVE.tensor_copy(vec[:, 4 * P:4 * P + nrow[4]], psum[b2][:, 0:nrow[4]]))
        bank_free[b] = bank_free[b2] = mv
        cvec = view(stat_at, KC, 2)
        act.need(mv)
        for j, at in enumerate((V_C, V_CC)):
            m_cvec = act.mark(ACTE.activation(cvec[:, :, j], vec[:, at:at + KC], ACT.Silu))
        phase()

        def ada_piece(l, n):
            w, ready, s = fetch(ins["w_ada_2"][l][:, n * 512:(n + 1) * 512], 512)
            pe.need(ready)
            b = bank()
            for f in range(4):
                for k in range(KC):
                    i = PE.matmul(psum[b][:, 2 * f:2 * f + 2], w[:, k, f * P:(f + 1) * P], cvec[:, k, :],
                                  start=k == 0, stop=k == KC - 1)
            m = pe.mark(i)
            slot_free[s] = m
            dve.need(m)
            bias = vec[:, P + l * 48 + 4 * n:P + l * 48 + 4 * n + 4].unsqueeze(2).to_broadcast([P, 4, 2])
            bank_free[b] = dve.mark(DVE.tensor_tensor(
                mods[:, l, 4 * n:4 * n + 4, :], psum[b][:, 0:8].rearrange("p (f j) -> p f j", j=2), bias, ALU.add))
        ada_todo = [(l, n) for l in range(LAYERS) for n in range(12)]

        def some_ada(n):
            for _ in range(n):
                if ada_todo:
                    ada_piece(*ada_todo.pop(0))

        stats = view(stat_at + 16, 96)
        def rms_rows(tiles, width, src, scratch, at=0, eps=EPS):
            for t in tiles:
                act.need(act.last())
                act.mark(ACTE.activation(scratch, src(t), ACT.Square, accum_out=stats[:, at + t:at + t + 1]))
            a, z = at + tiles[0], at + tiles[-1] + 1
            dve.need(act.last())
            m = dve.mark(DVE.tensor_scalar(stats[:, a:z], stats[:, a:z], 1.0 / width, eps, ALU.mult, ALU.add))
            act.need(m)
            m = act.mark(ACTE.activation(stats[:, a:z], stats[:, a:z], ACT.Sqrt))
            dve.need(m)
            return dve.mark(DVE.reciprocal(stats[:, a:z], stats[:, a:z]))

        def normed_features(tiles_of, dst, xn, scale_of, bias_of):
            tiles = [t for ts, _ in tiles_of for t in ts]
            m = rms_rows(tiles, D, lambda t: resid[:, t, :], xn[:, tiles[0], :])
            dve.need(m)
            ms = {}
            act.need(m)
            for t in tiles:
                if t % 2:
                    ms[t] = dve.mark(DVE.tensor_scalar(xn[:, t, :], resid[:, t, :], stats[:, t:t + 1], None, ALU.mult))
                else:
                    ms[t] = act.mark(ACTE.activation(xn[:, t, :], resid[:, t, :], ACT.Copy, scale=stats[:, t:t + 1]))
            for k in range(KC):
                for ts, which in tiles_of:
                    b = bank()
                    for j, t in enumerate(ts):
                        pe.need(ms[t])
                        i = PE.transpose(psum[b][:, j * P:(j + 1) * P], xn[:, t, k * P:(k + 1) * P], ident)
                    m = pe.mark(i)
                    n = len(ts) * P
                    o = dst[:, k, ts[0] * P:ts[0] * P + n]
                    sc, bi = scale_of(k, which), bias_of(k, which)
                    if k % 2:
                        dve.need(m)
                        if bi is None:
                            bank_free[b] = dve.mark(DVE.tensor_scalar(o, psum[b][:, 0:n], sc, None, ALU.mult))
                        else:
                            bank_free[b] = dve.mark(DVE.tensor_scalar(o, psum[b][:, 0:n], sc, bi, ALU.mult, ALU.add))
                    else:
                        act.need(m)
                        bank_free[b] = act.mark(ACTE.activation(o, psum[b][:, 0:n], ACT.Identity, scale=sc,
                                                                bias=0.0 if bi is None else bi))

        def tok_product(xT, t, w, width, cols=0, start=True, stop=True, kc=KC, b=None, off=0):
            if b is None:
                b = bank()
            for k in range(kc):
                i = PE.matmul(psum[b][:, off:off + width], xT[:, k, t * P:(t + 1) * P], w[:, k, cols:cols + width],
                              start=k == 0, stop=k == kc - 1)
            return b, pe.mark(i)

        z = zone
        hT = view(z, KC, SEQ); z += KC * SEQ
        qkT_at = z
        qTA = view(z, 4, SEQ); z += 4 * SEQ
        kTA = view(z, 4, SEQ); z += 4 * SEQ
        qTB = view(z, 4, SEQ); z += 4 * SEQ
        kTB = view(z, 4, SEQ); z += 4 * SEQ
        vA = view(z, NXT, 4, HD); z += NXT * 256
        vB = view(z, NXT, 4, P); z += NXT * 512
        mix = view(z, NXT, D); z += NXT * D
        tmp_at = z; z += 2048
        cosg = view(gate_at, 4, NXT, HD)
        sing = view(gate_at + 1024, 4, NXT, HD)
        assert z <= 53200
        tabs = const[:, C_CS:C_CS + 4 * HD].rearrange("p (t n) -> p t n", n=HD)
        for n in range(4):
            g = bc[:, B_QK + n * HD:B_QK + (n + 1) * HD]
            gl, gh = (g[:, o:o + 32].unsqueeze(1).to_broadcast([P, NXT, 32]) for o in (0, 32))
            pool.mark(POOL.tensor_tensor(cosg[:, n, :, 0:32], tabs[:, :, 0:32], gl, ALU.mult))
            pool.mark(POOL.tensor_tensor(cosg[:, n, :, 32:64], tabs[:, :, 0:32], gh, ALU.mult))
            pool.mark(POOL.tensor_tensor(sing[:, n, :, 32:64], tabs[:, :, 32:64], gl, ALU.mult))
            m = pool.mark(POOL.tensor_tensor(sing[:, n, :, 0:32], tabs[:, :, 32:64], gh, ALU.mult))
            pool.need(m)
            m_tab = pool.mark(POOL.tensor_scalar(sing[:, n, :, 0:32], sing[:, n, :, 0:32], -1.0, None, ALU.mult))

        xn = view(qkT_at, NXT, D)
        normed_features([(list(range(NXT)), 0)], hT, xn,
                        lambda k, w: vec[:, V_NG + k:V_NG + k + 1], lambda k, w: None)
        phase()

        sq = view(tmp_at, 512)
        qn = view(tmp_at + 512, 512)
        rot = view(tmp_at + 1024, 512)
        crs = view(tmp_at + 1536, 512)
        dve.need(m_tab)
        pool.need(m_tab)
        reads = {"qn": None, "rot": None}

        def rotary(b, m, kind, heads, t, dst, dup):
            n = heads * HD
            act.need(m, dve.last())
            ma = act.mark(ACTE.activation(sq[:, 0:n], psum[b][:, 0:n], ACT.Square))
            hs = stats[:, 0:heads]
            dve.need(ma)
            m1 = dve.mark(DVE.tensor_reduce(hs, sq[:, 0:n].rearrange("p (h d) -> p h d", d=HD), AX.X, ALU.add))
            dve.need(m1)
            m1 = dve.mark(DVE.tensor_scalar(hs, hs, 1.0 / HD, EPS, ALU.mult, ALU.add))
            act.need(m1)
            m1 = act.mark(ACTE.activation(hs, hs, ACT.Sqrt))
            dve.need(m1)
            m1 = dve.mark(DVE.reciprocal(hs, hs))
            dve.need(m1, reads["qn"])
            q3 = qn[:, 0:n].rearrange("p (h d) -> p h d", d=HD)
            r3 = rot[:, 0:n].rearrange("p (h d) -> p h d", d=HD)
            c3 = crs[:, 0:n].rearrange("p (h d) -> p h d", d=HD)
            m1 = dve.mark(DVE.tensor_tensor(q3, psum[b][:, 0:n].rearrange("p (h d) -> p h d", d=HD),
                                            hs.unsqueeze(2).to_broadcast([P, heads, HD]), ALU.mult))
            bank_free[b] = m1
            pool.need(m1, dve.last())
            pool.mark(POOL.tensor_tensor(c3[:, :, 0:32], q3[:, :, 32:64],
                                         sing[:, kind, t:t + 1, 0:32].to_broadcast([P, heads, 32]), ALU.mult))
            m2 = pool.mark(POOL.tensor_tensor(c3[:, :, 32:64], q3[:, :, 0:32],
                                              sing[:, kind, t:t + 1, 32:64].to_broadcast([P, heads, 32]), ALU.mult))
            reads["qn"] = m2
            dve.need(m1, reads["rot"])
            m3 = dve.mark(DVE.tensor_tensor(r3, q3, cosg[:, kind, t:t + 1, :].to_broadcast([P, heads, HD]), ALU.mult))
            dve.need(m2, m3)
            m3 = dve.mark(DVE.tensor_tensor(r3, r3, c3, ALU.add))
            if dup:
                d4 = qn[:, 0:4 * HD].rearrange("p (h c d) -> p h c d", c=2, d=HD)
                dve.need(m3)
                for c in range(2):
                    m3 = dve.mark(DVE.tensor_copy(d4[:, :, c, :], r3))
                src, pairs = qn, 2
            else:
                src, pairs = rot, 4
            b = bank()
            pe.need(m3)
            for j in range(pairs):
                i = PE.transpose(psum[b][:, j * P:(j + 1) * P], src[:, j * P:(j + 1) * P], ident)
            m4 = pe.mark(i)
            reads["rot"] = m4
            if dup:
                reads["qn"] = m4
            act.need(m4)
            got = psum[b][:, 0:pairs * P].rearrange("p (j t) -> p j t", t=P)
            if dup:
                for kv in range(2):
                    o = dst[:, 2 * kv:2 * kv + 2, t * P:(t + 1) * P]
                    m5 = act.mark(ACTE.activation(o, got[:, kv:kv + 1, :].to_broadcast([P, 2, P]), ACT.Copy))
            else:
                m5 = act.mark(ACTE.activation(dst[:, :, t * P:(t + 1) * P], got, ACT.Copy))
            bank_free[b] = m5

        def in_piece(c0, width, use):
            w, ready, s = fetch(ins["w_in"][0][:, c0:c0 + width], width)
            pe.need(ready)
            late = []
            for t in range(NXT):
                b, m = tok_product(hT, t, w, width)
                late.append((b, m, t))
                if len(late) > 1:
                    use(*late.pop(0))
            slot_free[s] = m
            use(*late.pop(0))

        def use_q(kind, dst):
            return lambda b, m, t: rotary(b, m, kind, 8, t, dst, False)

        def use_kv_a(b, m, t):
            act.need(m)
            v = psum[b][:, 128:256].rearrange("p (h d) -> p h d", d=HD)
            for kv in range(2):
                act.mark(ACTE.activation(vA[:, t, 2 * kv:2 * kv + 2, :], v[:, kv:kv + 1, :].to_broadcast([P, 2, HD]), ACT.Copy))
            rotary(b, m, 1, 2, t, kTA, True)

        def use_v_b(b, m, t):
            act.need(m)
            bank_free[b] = act.mark(ACTE.activation(vB[:, t, :, :].rearrange("p a b -> p (a b)"), psum[b][:], ACT.Copy))

        def use_gate(off):
            def f(b, m, t):
                act.need(m)
                bank_free[b] = act.mark(ACTE.activation(mix[:, t, off:off + 512], psum[b][:], ACT.Silu))
            return f
        in_piece(0, 512, use_q(0, qTA)); some_ada(2)
        in_piece(512, 256, use_kv_a); some_ada(1)
        in_piece(1280, 512, use_q(2, qTB)); some_ada(2)
        in_piece(1792, 512, use_q(3, kTB)); some_ada(2)
        in_piece(2304, 512, use_v_b); some_ada(2)
        in_piece(768, 512, use_gate(0)); some_ada(2)
        in_piece(2816, 512, use_gate(512)); some_ada(2)
        phase()

        NPB = 3
        pb = [view(zone + n * 512, 512) for n in range(NPB)]
        pT = [view(zone + (NPB + n) * 512, 512) for n in range(NPB)]
        qs = [view(zone + 2 * NPB * 512 + n * SEQ, SEQ) for n in range(2)]
        ks = [view(gate_at + n * SEQ, SEQ) for n in range(2)]
        st = view(stat_at + 128, 16, 8)
        S_B, T_B, O_B = (0, 1, 2), (3, 4, 5), (6, 7)
        maskA = const[:, C_MA:C_MA + 256]
        maskB = const[:, C_MB:C_MB + 512]
        with loop_over("attention", 4) as lp:
            i = lp.i
            def pair(x):
                return x[:, bass.ts(i, 1), :].rearrange("p a b -> p (a b)")
            pe_all = lp.prev("pe")
            dve.need(pe_all)
            pool.need(pe_all)
            mq = [dve.mark(DVE.tensor_copy(qs[0], pair(qTA))), dve.mark(DVE.tensor_copy(qs[1], pair(qTB)))]
            mk = [pool.mark(POOL.tensor_copy(ks[0], pair(kTA))), pool.mark(POOL.tensor_copy(ks[1], pair(kTB)))]
            units = [(k, par, t) for par in range(2) for k in range(2) for t in range(NXT)]
            state = {}

            def keys(k, t):
                return range(max(0, t - 1), t + 1) if k == 0 else range(t + 1)

            def scores(u):
                k, par, t = units[u]
                kt = keys(k, t)
                pe.need(mq[k], mk[k], state.get(("max", u - 3)) or lp.prev(f"max{(u - 3) % 16}"))
                half = slice(par * HD, par * HD + HD)
                kT = ks[k][half, kt[0] * P:(kt[-1] + 1) * P]
                state["s", u] = pe.mark(PE.matmul(psum[S_B[u % 3]][:, 0:len(kt) * P], qs[k][half, t * P:(t + 1) * P], kT,
                                                  start=True, stop=True))

            def softmax(u):
                k, par, t = units[u]
                n = len(keys(k, t)) * P
                mask = maskA[:, 256 - n:256] if k == 0 else maskB[:, 512 - n:512]
                c = st[:, u, :]
                dve.need(state["s", u], state.get(("tr", u - NPB)) or lp.prev(f"tr{(u - NPB) % 16}"))
                dve.mark(DVE.memset(c[:, 7:8], 0.0))
                m = dve.mark(DVE.tensor_tensor_reduce(pb[u % NPB][:, 0:n], psum[S_B[u % 3]][:, 0:n], mask, SCALE, NEG,
                                                      ALU.add, ALU.max, c[:, 0:1]))
                state["max", u] = m
                dve.need(m)
                if k == 0:
                    sk = bc[:, B_SK:B_SK + 8].rearrange("p (i h) -> p i h", h=2)[:, bass.ts(i, 1), par]
                    m = dve.mark(DVE.tensor_tensor(c[:, 0:1], c[:, 0:1], sk, ALU.max))
                    dve.need(m)
                m = dve.mark(DVE.tensor_scalar(c[:, 1:2], c[:, 0:1], -1.0, None, ALU.mult))
                act.need(m)
                m2 = act.mark(ACTE.activation(pb[u % NPB][:, 0:n], pb[u % NPB][:, 0:n], ACT.Exp, bias=c[:, 1:2],
                                              accum_out=c[:, 2:3]))
                if k == 0:
                    m2 = act.mark(ACTE.activation(c[:, 3:4], sk, ACT.Exp, bias=c[:, 1:2]))
                state["exp", u] = m2
                dve.need(m2)
                if k == 0:
                    m = dve.mark(DVE.tensor_tensor(c[:, 2:3], c[:, 2:3], c[:, 3:4], ALU.add))
                    dve.need(m)
                state["rec", u] = dve.mark(DVE.reciprocal(c[:, 4:5], c[:, 2:3]))

            def turn_p(u):
                k, par, t = units[u]
                n = len(keys(k, t))
                pe.need(state["exp", u], state.get(("pT", u - 3)) or lp.prev(f"pT{(u - 3) % 16}"))
                for j in range(n):
                    x = PE.transpose(psum[T_B[u % 3]][:, j * P:(j + 1) * P], pb[u % NPB][:, j * P:(j + 1) * P], ident)
                m = pe.mark(x)
                state["tr", u] = m
                act.need(m, state.get(("pv", u - NPB)) or lp.prev(f"pv{(u - NPB) % 16}"))
                state["pT", u] = act.mark(ACTE.activation(pT[u % NPB][:, 0:n * P], psum[T_B[u % 3]][:, 0:n * P], ACT.Copy))

            def value(u):
                k, par, t = units[u]
                kt_ = keys(k, t)
                pe.need(state["pT", u], state.get(("o", u - 2)) or lp.prev(f"o{(u - 2) % 16}"))
                o = psum[O_B[u % 2]][:, 0:HD]
                for j, kt in enumerate(kt_):
                    if k == 0:
                        v = vA[:, kt, bass.ts(i, 1), :].rearrange("p a b -> p (a b)")
                    else:
                        v = vB[:, kt, bass.ts(i, 1), par * HD:(par + 1) * HD].rearrange("p a b -> p (a b)")
                    x = PE.matmul(o, pT[u % NPB][:, j * P:(j + 1) * P], v, start=j == 0, stop=j == len(kt_) - 1)
                state["pv", u] = pe.mark(x)
                dve.need(state["pv", u], state["rec", u])
                g = mix[:, t, k * 512:(k + 1) * 512].rearrange("p (i n) -> p i n", n=P)[:, bass.ts(i, 1), par * HD:(par + 1) * HD]
                g = g.rearrange("p a b -> p (a b)")
                state["o", u] = dve.mark(DVE.scalar_tensor_tensor(g, o, st[:, u, 4:5], g, ALU.mult, ALU.mult))

            n = len(units)
            for u in range(n + 3):
                if u < n:
                    scores(u)
                    softmax(u)
                if u >= 1 and u - 1 < n:
                    turn_p(u - 1)
                if u >= 2 and u - 2 < n:
                    value(u - 2)
            for u in range(n - 3, n):
                for key in ("max", "tr", "pT", "pv", "o"):
                    lp.carry(f"{key}{u}", state[key, u])
            lp.carry("pe", pe.last())
        for n in range(8):
            bank_free[n] = [dve.last(), act.last()]
        phase()

        mT = view(qkT_at, KC, SEQ)

        def transposed(src, tiles, k_of, dst, dst_k, scale=None):
            for k in range(k_of):
                for ts in (tiles[i:i + 4] for i in range(0, len(tiles), 4)):
                    b = bank()
                    for j, t in enumerate(ts):
                        i = PE.transpose(psum[b][:, j * P:(j + 1) * P], src[:, t, k * P:(k + 1) * P], ident)
                    m = pe.mark(i)
                    o = dst[:, dst_k + k, ts[0] * P:(ts[-1] + 1) * P]
                    n = len(ts) * P
                    if k % 2:
                        dve.need(m)
                        if scale is None:
                            mo = dve.mark(DVE.tensor_copy(o, psum[b][:, 0:n]))
                        else:
                            mo = dve.mark(DVE.tensor_scalar(o, psum[b][:, 0:n], scale(k), None, ALU.mult))
                    else:
                        act.need(m)
                        mo = act.mark(ACTE.activation(o, psum[b][:, 0:n], ACT.Copy, scale=1.0 if scale is None else scale(k)))
                    bank_free[b] = mo
        transposed(mix, list(range(NXT)), KC, mT, 0)
        some_ada(3)
        phase()
        for h in range(2):
            w, ready, s = fetch(ins["w_out"][0][:, h * 512:(h + 1) * 512], 512)
            pe.need(ready)
            for t in range(NXT):
                b, m = tok_product(mT, t, w, 512)
                dve.need(m)
                r = resid[:, t, h * 512:(h + 1) * 512]
                bank_free[b] = dve.mark(DVE.tensor_tensor(r, r, psum[b][:], ALU.add))
            slot_free[s] = m
            some_ada(2)
        some_ada(24)
        phase()

        for l in range(LAYERS):
            last = l == LAYERS - 1
            xt, ct = list(range(NXT)), list(range(NXT, NT))
            streams = [(xt, 0), (ct, 1)]
            full = [(xt, 0)] if last else streams
            vl = V_L + l * V_LN
            V_GM, V_GF, V_CB, V_LG, V_LB, V_SB, V_SN = vl, vl + 8, vl + 16, vl + 20, vl + 24, vl + 28, vl + 36

            effs = view(stat_at + 256, 2, KC, 2)
            for n, (vg, sc) in enumerate(((V_GM, 8), (V_GF, 32))):
                m = dve.mark(DVE.tensor_scalar(effs[:, n, :, :], mods[:, l, sc:sc + 8, :], 1.0, None, ALU.add))
                dve.need(m)
                m = dve.mark(DVE.tensor_tensor(effs[:, n, :, :], effs[:, n, :, :],
                                               vec[:, vg:vg + 8].unsqueeze(2).to_broadcast([P, KC, 2]), ALU.mult))
            phase()

            def gate_rows(g0):
                for _, which in full:
                    for h in range(2):
                        b = bank()
                        for k in range(4):
                            col = mods[:, l, g0 + 4 * h + k, which:which + 1].to_broadcast([P, P])
                            i = PE.matmul(psum[b][:, k * P:(k + 1) * P], col, ident, start=True, stop=True)
                        m = pe.mark(i)
                        act.need(m)
                        bank_free[b] = act.mark(ACTE.activation(gates[:, which, h * 512:(h + 1) * 512], psum[b][:], ACT.Copy))

            z = zone
            hT = view(z, KC, TOK); h_at = z; z += KC * TOK
            sg_at = z; sg = view(z, 4, TOK); z += 4 * TOK
            vc_at = z; z += 3672
            zs_at = z; zs = view(z, NT, DS); z += NT * DS
            xp_at = z; z += KC * (TOK + 2 * (SK - 1))
            assert z <= 53200, z
            xn = view(sg_at, NT, D)
            normed_features(streams, hT, xn,
                            lambda k, w: effs[:, 0, k, w:w + 1], lambda k, w: mods[:, l, k, w:w + 1])
            phase()
            gate_rows(16)

            v1 = view(vc_at, 2, ROWS, GRID_W + CK - 1)
            v2 = view(vc_at + 2 * ROWS * (GRID_W + CK - 1), 2, SEQ)
            v3 = view(vc_at + 2 * ROWS * (GRID_W + CK - 1) + 2 * SEQ, 4, CTX + CK - 1)
            xbcx = view(xp_at, KC, SEQ + SK - 1)
            xbcc = view(xp_at + KC * (SEQ + SK - 1), KC, CTX + SK - 1)
            mz = pool.mark(POOL.memset(view(vc_at, 3672), 0.0))
            mz = pool.mark(POOL.memset(view(xp_at, KC * (TOK + 2 * (SK - 1))), 0.0))
            H2 = CK // 2
            H5 = SK // 2

            def feature_piece(c0, which_streams, use, nf=4):
                w, ready, s = fetch(ins["w_in_2"][l][:, c0:c0 + 128 * nf], 128 * nf)
                pe.need(ready)
                for f in range(nf):
                    for ts, which in which_streams:
                        b = bank()
                        n = len(ts) * P
                        for k in range(KC):
                            i = PE.matmul(psum[b][:, 0:n], w[:, k, f * P:(f + 1) * P], hT[:, k, ts[0] * P:ts[0] * P + n],
                                          start=k == 0, stop=k == KC - 1)
                        m = pe.mark(i)
                        use(b, m, f, ts, which, n)
                slot_free[s] = m

            def use_sig(b, m, f, ts, which, n):
                act.need(m)
                bank_free[b] = act.mark(ACTE.activation(sg[:, f, ts[0] * P:ts[0] * P + n], psum[b][:, 0:n], ACT.Sigmoid))

            def use_u(b, m, f, ts, which, n):
                dve.need(m, mz, act.last())
                s3 = sg[:, f, ts[0] * P:ts[0] * P + n]
                p3 = psum[b][:, 0:n]
                if which == 1:
                    o = v3[:, f, H2:H2 + CTX]
                elif f < 2:
                    o = v1[:, f, :, H2:H2 + GRID_W]
                    s3 = s3.rearrange("p (r c) -> p r c", c=GRID_W)
                    p3 = p3.rearrange("p (r c) -> p r c", c=GRID_W)
                else:
                    o = v2[:, f - 2, :]
                bank_free[b] = dve.mark(DVE.tensor_tensor(o, p3, s3, ALU.mult))

            def use_xbc(c):
                def f_(b, m, f, ts, which, n):
                    act.need(m, mz)
                    dst = (xbcx, xbcc)[which][:, c + f, H5:H5 + n]
                    bank_free[b] = act.mark(ACTE.activation(dst, psum[b][:, 0:n], ACT.Copy))
                return f_
            feature_piece(512, full, use_sig)
            feature_piece(0, full, use_u)
            w, ready, s = fetch(ins["w_in_2"][l][:, 1024:1536], 512)
            pe.need(ready)
            for ts, which in full:
                for t in ts:
                    b, m = tok_product(hT, t, w, 512)
                    act.need(m)
                    bank_free[b] = act.mark(ACTE.activation(zs[:, t, :], psum[b][:], ACT.Silu))
            slot_free[s] = m
            feature_piece(1536, streams, use_xbc(0))
            if last:
                feature_piece(2048, streams, use_xbc(4), nf=2)
                feature_piece(2304, full, use_xbc(6), nf=2)
            else:
                feature_piece(2048, streams, use_xbc(4))
            w, ready, s = fetch(ins["w_in_2"][l][:, 2560:2576], 16)
            pe.need(ready)
            dt = view(stat_at + 320, NT, 16)
            dta = view(stat_at + 416, NT, 16)
            e1 = view(stat_at + 512, NT, 16)
            av = view(stat_at + 608, 16)
            b = bank()
            for t in range(NT):
                for k in range(KC):
                    i = PE.matmul(psum[b][:, 16 * t:16 * t + 16], hT[:, k, t * P:(t + 1) * P], w[:, k, :],
                                  start=k == 0, stop=k == KC - 1)
            m = pe.mark(i)
            slot_free[s] = m
            dve.need(m)
            m = dve.mark(DVE.tensor_tensor(dt, psum[b][:, 0:16 * NT].rearrange("p (t n) -> p t n", n=16),
                                           bc[:, B_DTB + 16 * l:B_DTB + 16 * l + 16].unsqueeze(1).to_broadcast([P, NT, 16]), ALU.add))
            bank_free[b] = m
            act.need(m)
            m = act.mark(ACTE.activation(e1, dt, ACT.Abs))
            act.need(m)
            m = act.mark(ACTE.activation(e1, e1, ACT.Exp, scale=-1.0))
            act.need(m)
            m = act.mark(ACTE.activation(e1, e1, ACT.Ln, bias=1.0))
            ma = act.mark(ACTE.activation(av, bc[:, B_AL + 16 * l:B_AL + 16 * l + 16], ACT.Exp))
            dve.need(m)
            m = dve.mark(DVE.scalar_tensor_tensor(dt, dt, 0.0, e1, ALU.max, ALU.add))
            dve.need(m, ma)
            m = dve.mark(DVE.scalar_tensor_tensor(dta, dt, -1.0, av.unsqueeze(1).to_broadcast([P, NT, 16]), ALU.mult, ALU.mult))
            phase()

            xbc = view(h_at, KC, TOK)
            def taps5(src, c, n, o):
                cw = lambda j: vec[:, 4 * P + 40 * l + 8 * j + c:4 * P + 40 * l + 8 * j + c + 1]
                m = dve.mark(DVE.tensor_scalar(o, src[:, c, 0:n], cw(0), vec[:, V_SB + c:V_SB + c + 1], ALU.mult, ALU.add))
                for j in range(1, SK):
                    dve.need(m)
                    m = dve.mark(DVE.scalar_tensor_tensor(o, src[:, c, j:j + n], cw(j), o, ALU.mult, ALU.add))
                act.need(m)
                return act.mark(ACTE.activation(o, o, ACT.Silu))
            for c in range(KC):
                taps5(xbcx, c, SEQ, xbc[:, c, 0:SEQ])
                if c < 6 or not last:
                    taps5(xbcc, c, CTX, xbc[:, c, SEQ:TOK])
            cy = view(sg_at, 4, TOK)
            def wide(j, c):
                return vec[:, (2 + l) * P + 4 * j + c:(2 + l) * P + 4 * j + c + 1]
            for c in range(2):
                o = cy[:, c, 0:SEQ].rearrange("p (r w) -> p r w", w=GRID_W)
                m = dve.mark(DVE.tensor_scalar(o, v1[:, c, :, 0:GRID_W], wide(0, c), vec[:, V_CB + c:V_CB + c + 1], ALU.mult, ALU.add))
                for j in range(1, CK):
                    dve.need(m)
                    m = dve.mark(DVE.scalar_tensor_tensor(o, v1[:, c, :, j:j + GRID_W], wide(j, c), o, ALU.mult, ALU.add))
            for c in range(2):
                o = cy[:, 2 + c, 0:SEQ]
                m = dve.mark(DVE.tensor_scalar(o, v2[:, c, :], wide(H2, 2 + c), vec[:, V_CB + 2 + c:V_CB + 3 + c], ALU.mult, ALU.add))
                for d in range(1 - ROWS, ROWS):
                    if d == 0:
                        continue
                    r0, r1 = max(0, -d) * GRID_W, (ROWS - max(0, d)) * GRID_W
                    dve.need(m)
                    m = dve.mark(DVE.scalar_tensor_tensor(o[:, r0:r1], v2[:, c, r0 + d * GRID_W:r1 + d * GRID_W],
                                                          wide(H2 + d, 2 + c), o[:, r0:r1], ALU.mult, ALU.add))
            if not last:
                for c in range(4):
                    o = cy[:, c, SEQ:TOK]
                    m = dve.mark(DVE.tensor_scalar(o, v3[:, c, 0:CTX], wide(0, c), vec[:, V_CB + c:V_CB + c + 1], ALU.mult, ALU.add))
                    for j in range(1, CK):
                        dve.need(m)
                        m = dve.mark(DVE.scalar_tensor_tensor(o, v3[:, c, j:j + CTX], wide(j, c), o, ALU.mult, ALU.add))
            phase()

            sqv = view(vc_at, 4, 512)
            mu = view(vc_at + 2048, 512)
            rs = view(vc_at + 2560, 512)
            for ts, which in full:
                a, n = ts[0] * P, len(ts) * P
                b = bank()
                for c in range(4):
                    i = PE.matmul(psum[b][:, 0:n], ones, cy[:, c, a:a + n], start=c == 0, stop=c == 3)
                m = pe.mark(i)
                act.need(m, dve.last())
                m = act.mark(ACTE.activation(mu[:, 0:n], psum[b][:, 0:n], ACT.Copy, scale=1.0 / DC))
                bank_free[b] = m
                dve.need(m)
                m = dve.mark(DVE.tensor_tensor(cy[:, :, a:a + n], cy[:, :, a:a + n],
                                               mu[:, 0:n].unsqueeze(1).to_broadcast([P, 4, n]), ALU.subtract))
                act.need(m, pe.last())
                m = act.mark(ACTE.activation(sqv[:, :, 0:n], cy[:, :, a:a + n], ACT.Square))
                b = bank()
                pe.need(m)
                for c in range(4):
                    i = PE.matmul(psum[b][:, 0:n], ones, sqv[:, c, 0:n], start=c == 0, stop=c == 3)
                m = pe.mark(i)
                dve.need(m)
                m = dve.mark(DVE.tensor_scalar(rs[:, 0:n], psum[b][:, 0:n], 1.0 / DC, LN_EPS, ALU.mult, ALU.add))
                bank_free[b] = m
                act.need(m)
                m = act.mark(ACTE.activation(rs[:, 0:n], rs[:, 0:n], ACT.Sqrt))
                dve.need(m)
                m = dve.mark(DVE.reciprocal(rs[:, 0:n], rs[:, 0:n]))
                dve.need(m)
                m = dve.mark(DVE.tensor_tensor(cy[:, :, a:a + n], cy[:, :, a:a + n],
                                               rs[:, 0:n].unsqueeze(1).to_broadcast([P, 4, n]), ALU.mult))
                act.need(m)
                for c in range(4):
                    m = act.mark(ACTE.activation(cy[:, c, a:a + n], cy[:, c, a:a + n], ACT.Silu,
                                                 scale=vec[:, V_LG + c:V_LG + c + 1], bias=vec[:, V_LB + c:V_LB + c + 1]))
            tk = view(xp_at, NT, 6 * P)
            for t in range(NT):
                for c0, n in ((0, 4), (4, 2)):
                    b = bank()
                    for j in range(n):
                        i = PE.transpose(psum[b][:, j * P:(j + 1) * P], xbc[:, c0 + j, t * P:(t + 1) * P], ident)
                    m = pe.mark(i)
                    x = (dve, act)[t % 2]
                    x.need(m)
                    o, q = tk[:, t, c0 * P:(c0 + n) * P], psum[b][:, 0:n * P]
                    bank_free[b] = x.mark(DVE.tensor_copy(o, q) if t % 2 == 0 else ACTE.activation(o, q, ACT.Copy))
            phase()

            za = h_at
            ex = view(za, 4, NT, SH); za += 4 * NT * SH
            tot = view(za, NT, 16); za += NT * 16
            grow = view(za, SH, P); za += SH * P
            xw = view(za, DS); za += DS
            hst = view(za, DS); za += DS
            yt = view(za, DS); za += DS
            assert za <= h_at + 4 * TOK
            za = xp_at + NT * 6 * P
            md = view(za, SH, P); za += SH * P
            assert za <= 53200
            ef = view(vc_at + 3072 - 3072, 8)
            za = xp_at + NT * 6 * P + SH * P
            ys_at = vc_at
            ys = view(ys_at, NT, DS)
            E_at = za
            ef = view(za, SH, P); za += SH * P
            assert za <= 53200 + 0, za
            eb = grow
            dt_dir = lambda t, d: dt[:, t, 8 * d:8 * d + 8]
            b = bank()
            for n, (msk, d) in enumerate(((C_LE, 0), (C_GE, 1), (C_GT, 0), (C_LT, 1))):
                i = PE.matmul(psum[b][:, 48 * n:48 * n + 48].rearrange("p (t h) -> p t h", h=8), const[:, msk:msk + P],
                              dta[:, :, 8 * d:8 * d + 8], start=True, stop=True)
            i = PE.matmul(psum[b][:, 192:288].rearrange("p (t h) -> p t h", h=16), ones, dta, start=True, stop=True)
            m = pe.mark(i)
            act.need(m)
            act.mark(ACTE.activation(ex, psum[b][:, 0:192].rearrange("p (k t h) -> p k t h", t=NT, h=8), ACT.Exp))
            m = act.mark(ACTE.activation(tot, psum[b][:, 192:288].rearrange("p (t h) -> p t h", h=16), ACT.Exp))
            bank_free[b] = m
            dve.need(m)
            for d in range(2):
                m_ex = dve.mark(DVE.tensor_tensor(ex[:, 2 + d, :, :], ex[:, 2 + d, :, :], dt[:, :, 8 * d:8 * d + 8], ALU.mult))

            def cst(c):
                return const[:, c:c + P]

            def per_head(x, n):
                return x.unsqueeze(2).to_broadcast([P, SH, n])

            for ts, which in full:
                for t in ts:
                    cols = slice(t * P, (t + 1) * P)
                    bs = bank()
                    for g in range(2):
                        i = PE.matmul(psum[bs][:, g * P:(g + 1) * P], xbc[:, 4 + g, cols], xbc[:, 6 + g, cols], start=True, stop=True)
                    m_s = pe.mark(i)
                    for d in range(2):
                        row, colm, keep = ((C_GT, C_LE, C_LE), (C_LT, C_GE, C_GE))[d]
                        pool.need(pe.last(), dve.last())
                        mg = pool.mark(POOL.tensor_tensor(grow, cst(row).unsqueeze(1).to_broadcast([P, SH, P]),
                                                          per_head(dta[:, t, 8 * d:8 * d + 8], P), ALU.mult))
                        mm = pool.mark(POOL.tensor_tensor(md, cst(keep).unsqueeze(1).to_broadcast([P, SH, P]),
                                                          per_head(dt_dir(t, d), P), ALU.mult))
                        pe.need(mg)
                        e = (ef, eb)[d]
                        for q in range(2):
                            b = bank()
                            for h in range(4):
                                i = PE.matmul(psum[b][:, h * P:(h + 1) * P], grow[:, 4 * q + h, :], cst(colm), start=True, stop=True)
                            m = pe.mark(i)
                            act.need(m, dve.last())
                            if d and q == 0:
                                hold = (b, m)
                                continue
                            if d:
                                bb, _ = hold
                                bank_free[bb] = act.mark(ACTE.activation(e[:, 0:4, :], psum[bb][:].rearrange("p (h l) -> p h l", l=P), ACT.Exp))
                            bank_free[b] = act.mark(ACTE.activation(e[:, 4 * q:4 * q + 4, :], psum[b][:].rearrange("p (h l) -> p h l", l=P), ACT.Exp))
                        dve.need(act.last(), mm)
                        m = dve.mark(DVE.tensor_tensor(e, e, md, ALU.mult))
                    dve.need(m)
                    m = dve.mark(DVE.tensor_tensor(ef, ef, eb, ALU.add))
                    dve.need(m, m_s)
                    for g in range(2):
                        m = dve.mark(DVE.tensor_tensor(ef[:, 4 * g:4 * g + 4, :], ef[:, 4 * g:4 * g + 4, :],
                                                       psum[bs][:, g * P:(g + 1) * P].unsqueeze(1).to_broadcast([P, 4, P]), ALU.mult))
                    bank_free[bs] = m
                    pool.mark(POOL.tensor_tensor(ys[:, t, :].rearrange("p (h n) -> p h n", n=HD), tk[:, t, 0:DS].rearrange("p (h n) -> p h n", n=HD),
                                                 per_head(bc[:, B_DS + 8 * l:B_DS + 8 * l + 8], HD), ALU.mult))
                    b = bank()
                    pe.need(m)
                    for h in range(SH):
                        i = PE.matmul(psum[b][:, h * HD:(h + 1) * HD], ef[:, h, :], tk[:, t, h * HD:(h + 1) * HD], start=True, stop=True)
                    m = pe.mark(i)
                    dve.need(m, pool.last())
                    bank_free[b] = dve.mark(DVE.tensor_tensor(ys[:, t, :], ys[:, t, :], psum[b][:], ALU.add))

            for d in range(2):
                dve.need(pe.last())
                m_h = dve.mark(DVE.memset(hst, 0.0))
                order = (ct + xt) if d == 0 else (ct[::-1] + xt[::-1])
                for t in order:
                    cols = slice(t * P, (t + 1) * P)
                    if t in [q for ts, _ in full for q in ts]:
                        b = bank()
                        pe.need(m_h)
                        for g in range(2):
                            i = PE.matmul(psum[b][:, g * 256:(g + 1) * 256], xbc[:, 6 + g, cols], hst[:, g * 256:(g + 1) * 256], start=True, stop=True)
                        m = pe.mark(i)
                        dve.need(m, m_ex)
                        m = dve.mark(DVE.tensor_tensor(yt.rearrange("p (h n) -> p h n", n=HD), psum[b][:].rearrange("p (h n) -> p h n", n=HD),
                                                       per_head(ex[:, d, t, :], HD), ALU.mult))
                        bank_free[b] = m
                        dve.need(m)
                        m = dve.mark(DVE.tensor_tensor(ys[:, t, :], ys[:, t, :], yt, ALU.add))
                    if t == order[-1]:
                        continue
                    pool.need(m_ex, pe.last())
                    mw = pool.mark(POOL.tensor_tensor(xw.rearrange("p (h n) -> p h n", n=HD), tk[:, t, 0:DS].rearrange("p (h n) -> p h n", n=HD),
                                                      per_head(ex[:, 2 + d, t, :], HD), ALU.mult))
                    b = bank()
                    pe.need(mw)
                    for g in range(2):
                        i = PE.matmul(psum[b][:, g * 256:(g + 1) * 256], tk[:, t, DS + g * P:DS + (g + 1) * P], xw[:, g * 256:(g + 1) * 256], start=True, stop=True)
                    m = pe.mark(i)
                    dve.need(m, m_h)
                    m = dve.mark(DVE.tensor_tensor(hst.rearrange("p (h n) -> p h n", n=HD), hst.rearrange("p (h n) -> p h n", n=HD),
                                                   per_head(tot[:, t, 8 * d:8 * d + 8], HD), ALU.mult))
                    dve.need(m)
                    m_h = dve.mark(DVE.tensor_tensor(hst, hst, psum[b][:], ALU.add))
                    bank_free[b] = m_h
            dve.need(dve.last())
            mt = [q for ts, _ in full for q in ts]
            m = dve.mark(DVE.tensor_tensor(ys[:, 0:len(mt), :], ys[:, 0:len(mt), :], zs[:, 0:len(mt), :], ALU.mult))
            act.need(m)
            m = rms_rows(mt, DS, lambda t: ys[:, t, :], yt)
            dve.need(m)
            m = dve.mark(DVE.tensor_tensor(ys[:, 0:len(mt), :], ys[:, 0:len(mt), :],
                                           stats[:, 0:len(mt)].unsqueeze(2).to_broadcast([P, len(mt), DS]), ALU.mult))
            phase()
            syT = view(xp_at, 4, TOK)
            for ts, _ in full:
                transposed(ys, ts, 4, syT, 0, lambda k: vec[:, V_SN + k:V_SN + k + 1])
            phase()
            prod = view(h_at, 4, 512)
            uses = [None] * 4
            for h in range(2):
                w, ready, s = fetch(ins["w_out_2"][l][:, h * 512:(h + 1) * 512], 512)
                pe.need(ready)
                for ts, which in full:
                    for t in ts:
                        b = bank()
                        for k in range(KC):
                            src = cy[:, k, t * P:(t + 1) * P] if k < 4 else syT[:, k - 4, t * P:(t + 1) * P]
                            i = PE.matmul(psum[b][:], src, w[:, k, :], start=k == 0, stop=k == KC - 1)
                        m = pe.mark(i)
                        u = t % 4
                        dve.need(m, uses[u])
                        m1 = dve.mark(DVE.tensor_tensor(prod[:, u, :], psum[b][:], gates[:, which, h * 512:(h + 1) * 512], ALU.mult))
                        bank_free[b] = m1
                        pool.need(m1)
                        r = resid[:, t, h * 512:(h + 1) * 512]
                        uses[u] = pool.mark(POOL.tensor_tensor(r, r, prod[:, u, :], ALU.add))
                slot_free[s] = m
            phase()

            NB_ = BLOCKS[l]
            CAP = NB_ * P
            n_t = len(mt)
            z = zone
            tT = view(z, KC, TOK); z += KC * TOK
            xm = view(z, NT, D); xm_at = z; z += NT * D
            sb_rows = view(z, 4, D); z += 4 * D
            lg_at = z; z += 3200
            assert z <= 53200, z
            w_gu = [sb[:, ring_at + 2 * u * SLOT:ring_at + (2 * u + 1) * SLOT].rearrange("p (k n) -> p k n", n=2 * FF) for u in range(2)]
            w_dn = [sb[:, ring_at + (2 * u + 1) * SLOT:ring_at + (2 * u + 1) * SLOT + 2 * D].rearrange("p (k n) -> p k n", n=D) for u in range(2)]

            def load_gu(e, u):
                for j, name in enumerate(("w_gate_2", "w_up_2")):
                    m = slot_full[2 * u].mark(sp.dma_start(w_gu[u][:, :, j * FF:(j + 1) * FF],
                                                           ins[name][l][e, :, :].rearrange("e (k p) n -> p (e k) n", p=P)))
                return m

            def load_dn(e, u):
                return slot_full[2 * u + 1].mark(sp.dma_start(w_dn[u], ins["w_down_2"][l][e, :, :].rearrange("e (k p) n -> p (e k) n", p=P)))
            ready_gu, ready_dn = [None] * 2, [None] * 2
            for n in range(NSLOT):
                spl.need(slot_free[n])
            for u in range(2):
                ready_gu[u] = load_gu(slice(u, u + 1), u)
                ready_dn[u] = load_dn(slice(u, u + 1), u)

            for _, which in full:
                for n, col in ((0, lambda k: effs[:, 1, k, which:which + 1]), (1, lambda k: mods[:, l, 24 + k, which:which + 1])):
                    for h in range(2):
                        b = bank()
                        for k in range(4):
                            i = PE.matmul(psum[b][:, k * P:(k + 1) * P], col(4 * h + k).to_broadcast([P, P]), ident, start=True, stop=True)
                        m = pe.mark(i)
                        act.need(m)
                        m_rows = bank_free[b] = act.mark(ACTE.activation(sb_rows[:, 2 * which + n, h * 512:(h + 1) * 512], psum[b][:], ACT.Copy))
            m = rms_rows(mt, D, lambda t: resid[:, t, :], xm[:, 0, :])
            dve.need(m, m_rows)
            ms = {}
            for t in mt:
                which = 0 if t < NXT else 1
                m = dve.mark(DVE.scalar_tensor_tensor(xm[:, t, :], resid[:, t, :], stats[:, t:t + 1], sb_rows[:, 2 * which, :], ALU.mult, ALU.mult))
                pool.need(m)
                ms[t] = pool.mark(POOL.tensor_tensor(xm[:, t, :], xm[:, t, :], sb_rows[:, 2 * which + 1, :], ALU.add))
                act.need(ms[t])
                m_xd = tok_stored.mark(nc.scalar.dma_start(tok_dram[l][t * P:(t + 1) * P, :], xm[:, t, :]))
            for k in range(KC):
                for ts, which in full:
                    b = bank()
                    for j, t in enumerate(ts):
                        pe.need(ms[t])
                        i = PE.transpose(psum[b][:, j * P:(j + 1) * P], xm[:, t, k * P:(k + 1) * P], ident)
                    m = pe.mark(i)
                    o, n = tT[:, k, ts[0] * P:(ts[-1] + 1) * P], len(ts) * P
                    x = (dve, act)[k % 2]
                    x.need(m)
                    bank_free[b] = x.mark(DVE.tensor_copy(o, psum[b][:, 0:n]) if k % 2 == 0 else ACTE.activation(o, psum[b][:, 0:n], ACT.Copy))
            gate_rows(40)
            lg = view(lg_at, n_t, 20)
            q = [lg_at + NT * 20]

            def tile(*dims):
                n = 1
                for x in dims:
                    n *= x
                v = view(q[0], *dims)
                q[0] += n
                return v
            b = bank()
            pe.need(dve.last(), act.last())
            for t in mt:
                for k in range(KC):
                    i = PE.matmul(psum[b][:, 20 * t:20 * t + 20], tT[:, k, t * P:(t + 1) * P], router[:, l, k, :], start=k == 0, stop=k == KC - 1)
            m = pe.mark(i)

            def v_op(inst):
                m = dve.mark(inst)
                dve.need(m)
                return m
            dve.need(m)
            bank_free[b] = v_op(DVE.tensor_tensor(lg, psum[b][:, 0:20 * n_t].rearrange("p (t n) -> p t n", n=20),
                                                  bc[:, B_BR + 20 * l:B_BR + 20 * l + 20].unsqueeze(1).to_broadcast([P, n_t, 20]), ALU.add))

            def first_max(src, n):
                mx, oh, free = tile(n_t, 1), tile(n_t, n), tile(n_t, 1)
                v_op(DVE.tensor_reduce(mx.rearrange("p a b -> p (a b)"), src, AX.X, ALU.max))
                v_op(DVE.tensor_tensor(oh, src, mx.to_broadcast([P, n_t, n]), ALU.is_equal))
                v_op(DVE.tensor_scalar(free, oh[:, :, 0:1], -1.0, 1.0, ALU.mult, ALU.add))
                for j in range(1, n):
                    v_op(DVE.tensor_tensor(oh[:, :, j:j + 1], oh[:, :, j:j + 1], free, ALU.mult))
                    if j < n - 1:
                        v_op(DVE.tensor_tensor(free, free, oh[:, :, j:j + 1], ALU.subtract))
                return mx, oh
            gm, gsel = first_max(lg[:, :, 0:4], 4)
            dif = tile(n_t, 4)
            m = v_op(DVE.tensor_tensor(dif, lg[:, :, 0:4], gm.to_broadcast([P, n_t, 4]), ALU.subtract))
            act.need(m)
            m = act.mark(ACTE.activation(dif, dif, ACT.Exp))
            dve.need(m)
            gp = tile(n_t, 1)
            v_op(DVE.tensor_reduce(gp.rearrange("p a b -> p (a b)"), dif, AX.X, ALU.add))
            el, pr = tile(n_t, 4), tile(n_t, 4)
            for g in range(NG):
                dst = el if g == 0 else pr
                v_op(DVE.tensor_tensor(dst, lg[:, :, 4 + 4 * g:8 + 4 * g], gsel[:, :, g:g + 1].to_broadcast([P, n_t, 4]), ALU.mult))
                if g:
                    v_op(DVE.tensor_tensor(el, el, pr, ALU.add))
            m1_, oh1 = first_max(el, 4)
            v_op(DVE.scalar_tensor_tensor(el, oh1, -1e30, el, ALU.mult, ALU.add))
            m2_, oh2 = first_max(el, 4)
            wt = tile(2, n_t)
            w1, e2 = wt[:, 0, :].unsqueeze(2), wt[:, 1, :].unsqueeze(2)
            m = v_op(DVE.tensor_tensor(e2, m2_, m1_, ALU.subtract))
            act.need(m)
            m = act.mark(ACTE.activation(e2, e2, ACT.Exp))
            dve.need(m)
            v_op(DVE.scalar_tensor_tensor(w1, e2, 1.0, gp, ALU.add, ALU.mult))
            v_op(DVE.reciprocal(w1, w1))
            v_op(DVE.tensor_tensor(e2, e2, w1, ALU.mult))
            ch = [tile(n_t, NE) for _ in range(2)]
            for c, oh in enumerate((oh1, oh2)):
                for g in range(NG):
                    m = dve.mark(DVE.tensor_tensor(ch[c][:, :, 4 * g:4 * g + 4], oh, gsel[:, :, g:g + 1].to_broadcast([P, n_t, 4]), ALU.mult))
            dve.need(m)
            both, before, rank, tmp = tile(n_t, NE), tile(n_t + 1, NE), tile(n_t, NE), tile(n_t, NE)
            v_op(DVE.tensor_tensor(both, ch[0], ch[1], ALU.add))
            v_op(DVE.memset(before[:, 0, :], 0.0))
            for t in range(n_t):
                m = v_op(DVE.tensor_tensor(before[:, t + 1, :], before[:, t, :], both[:, t, :], ALU.add))
            b = bank()
            pe.need(m)
            r_ps = psum[b][:, 0:NE * n_t].rearrange("p (t e) -> p t e", e=NE)
            PE.matmul(r_ps, const[:, C_LT:C_LT + P], both, start=True, stop=False)
            PE.matmul(r_ps, ones, before[:, 0:n_t, :], start=False, stop=True)
            i = PE.matmul(psum[b][:, NE * n_t:NE * n_t + NE], ones, before[:, n_t, :], start=True, stop=True)
            m = pe.mark(i)
            dve.need(m)
            v_op(DVE.tensor_copy(rank, r_ps))
            most = tile(1)
            bank_free[b] = v_op(DVE.tensor_reduce(most, psum[b][:, NE * n_t:NE * n_t + NE], AX.X, ALU.max))
            most_i = view(stat_at + 700 + l, 1).bitcast(mybir.dt.int32)
            m_most = v_op(DVE.tensor_copy(most_i, most))
            place_i = tile(2, n_t).bitcast(mybir.dt.int32)
            fits = tile(2, n_t)
            rk, ei = tile(n_t), tile(n_t)
            for c in range(2):
                v_op(DVE.tensor_tensor(tmp, rank, ch[c], ALU.mult))
                v_op(DVE.tensor_reduce(rk, tmp, AX.X, ALU.add))
                v_op(DVE.tensor_tensor(tmp, ch[c], const[:, C_IO:C_IO + NE].unsqueeze(1).to_broadcast([P, n_t, NE]), ALU.mult))
                v_op(DVE.tensor_reduce(ei, tmp, AX.X, ALU.add))
                v_op(DVE.tensor_scalar(fits[:, c, :], rk, float(CAP), None, ALU.is_lt))
                v_op(DVE.tensor_scalar(rk, rk, float(CAP - 1), None, ALU.min))
                m_place = v_op(DVE.scalar_tensor_tensor(place_i[:, c, :], ei, float(CAP), rk, ALU.mult, ALU.add))
            wfit = tile(2, n_t)
            m_w = v_op(DVE.tensor_tensor(wfit, wt, fits, ALU.mult))
            v_op(DVE.tensor_scalar(rank, rank, 1.0, None, ALU.add))
            v_op(DVE.tensor_tensor(rank, rank, both, ALU.mult))
            v_op(DVE.tensor_scalar(rank, rank, -1.0, None, ALU.add))
            BF = mybir.dt.bfloat16
            tokb = tile(NT).bitcast(BF)
            v_op(DVE.tensor_copy(tokb, const[:, C_TOK:C_TOK + 2 * NT]))
            hot = [tile(P).bitcast(BF) for _ in range(3)]
            b = bank()
            seen = [None] * 3
            nh = 0
            for e in range(NE):
                for t in range(n_t):
                    hv = hot[nh % 3][:, 0:CAP]
                    dve.need(seen[nh % 3])
                    m = dve.mark(DVE.tensor_scalar(hv, const[:, C_IO:C_IO + CAP], rank[:, t, e:e + 1], None, ALU.is_equal))
                    pe.need(m)
                    for k in range(NB_):
                        o = (e * NB_ + k) * n_t + t
                        i = PE.matmul(psum[b][:, 2 * o:2 * o + 2], hv[:, k * P:(k + 1) * P], tokb[:, 2 * t:2 * t + 2],
                                      start=True, stop=True)
                    seen[nh % 3] = pe.mark(i)
                    nh += 1
            dve.need(seen[(nh - 1) % 3])
            tab = tile(NE * NB_, 2)
            tabi = tile(NE * NB_).bitcast(mybir.dt.int32)
            v_op(DVE.tensor_reduce(tab, psum[b][:, 0:2 * NE * NB_ * n_t].rearrange("p (e t j) -> p e j t", t=n_t, j=2), AX.X, ALU.add))
            bank_free[b] = m
            v_op(DVE.scalar_tensor_tensor(tabi, tab[:, :, 1], float(P), tab[:, :, 0], ALU.mult, ALU.add))
            assert q[0] <= lg_at + 3200, q[0] - lg_at
            act.need(m_xd)
            phase("experts")
            pool.need(m_xd)
            bank_free[b] = None
            z = xm_at
            gx = [view(z + n * D, D) for n in range(2 * NB_)]; z += 4 * D
            gxT = [view(z + n * D, KC, P) for n in range(2)]; z += 2 * D
            z = xm_at + NT * D
            yb = [view(z + n * D, D) for n in range(2)]; z += 2 * D
            silg = [view(z + n * FF, FF) for n in range(2)]; z += 2 * FF
            hidb = [view(z + n * FF, FF) for n in range(2)]; z += 2 * FF
            hidT = [view(z + n * FF, 2, P) for n in range(2)]; z += 2 * FF
            idx = view(z, 2 * NB_).bitcast(mybir.dt.int32); z += 2 * NB_
            spare = view(z, 1); z += 1
            pool.need(pool.mark(POOL.memset(spare, 0.0)))
            assert z <= lg_at
            use = {}

            def pair_of_experts(lp, i, more):
                def old(key):
                    return use.get(key) or (lp.prev(key) if lp else None)
                def slc(j):
                    return bass.ts(j, 1) if lp else slice(j, j + 1)
                gathered = {}
                for u in range(2):
                    for k in range(NB_):
                        g = u * NB_ + k
                        pool.need(old(f"turned{g}"))
                        m = pool.mark(POOL.tensor_copy(idx[:, g:g + 1], tabi[:, slc(2 * NB_ * i + g)]))
                        pool.need(m)
                        pool.mark(POOL.tensor_tensor(spare, spare, spare, ALU.add))
                        gathered[g] = gx_full[g].mark(nc.gpsimd.indirect_dma_start(
                            out=gx[g], out_offset=None, in_=tok_dram[l][:, :],
                            in_offset=bass.IndirectOffsetOnAxis(ap=idx[:, g:g + 1], axis=0)))
                blocks = [(u, k) for u in range(2) for k in range(NB_)]
                nb_ = [0]

                def bk(*marks, n=1):
                    got = [(nb_[0] + j) % 8 for j in range(n)]
                    nb_[0] += n
                    pe.need(*marks, *(old(f"bank{b}") for b in got))
                    return got if n > 1 else got[0]

                def turn(n):
                    u, k = blocks[n]
                    g, s = u * NB_ + k, n % 2
                    bs = bk(gathered[g], n=2)
                    for h in range(2):
                        b = bs[h]
                        for j in range(4):
                            x = PE.transpose(psum[b][:, j * P:(j + 1) * P], gx[g][:, (4 * h + j) * P:(4 * h + j + 1) * P], ident)
                        m = pe.mark(x)
                        o = gxT[s][:, 4 * h:4 * h + 4, :].rearrange("p a b -> p (a b)")
                        y = (dve, act)[h]
                        y.need(m, old(f"gate{s}"))
                        use[f"bank{b}"] = y.mark(DVE.tensor_copy(o, psum[b][:]) if h == 0 else ACTE.activation(o, psum[b][:], ACT.Copy))
                        use[f"gxT{s}{h}"] = use[f"bank{b}"]
                    use[f"turned{g}"] = m

                def gate_up(n):
                    u, k = blocks[n]
                    s = n % 2
                    b = bk(ready_gu[u], use[f"gxT{s}0"], use[f"gxT{s}1"])
                    for c in range(KC):
                        x = PE.matmul(psum[b][:], gxT[s][:, c, :], w_gu[u][:, c, :], start=c == 0, stop=c == KC - 1)
                    m = pe.mark(x)
                    use[f"gate{s}"] = m
                    use[f"gu{u}"] = m
                    act.need(m, old(f"hid{s}"))
                    m = act.mark(ACTE.activation(silg[s], psum[b][:, 0:FF], ACT.Silu))
                    dve.need(m, old(f"hT{s}"))
                    m = dve.mark(DVE.tensor_tensor(hidb[s], silg[s], psum[b][:, FF:2 * FF], ALU.mult))
                    use[f"bank{b}"] = use[f"hid{s}"] = m

                def down(n):
                    u, k = blocks[n]
                    s = n % 2
                    b = bk(use[f"hid{s}"])
                    for c in range(2):
                        x = PE.transpose(psum[b][:, c * P:(c + 1) * P], hidb[s][:, c * P:(c + 1) * P], ident)
                    m = pe.mark(x)
                    use[f"hT{s}"] = m
                    dve.need(m, old(f"down{s}"))
                    m = dve.mark(DVE.tensor_copy(hidT[s].rearrange("p a b -> p (a b)"), psum[b][:, 0:2 * P]))
                    use[f"bank{b}"] = m
                    b0, b1 = bk(m, ready_dn[u], n=2)
                    for h, b in ((0, b0), (1, b1)):
                        for c in range(2):
                            x = PE.matmul(psum[b][:], hidT[s][:, c, :], w_dn[u][:, c, h * 512:(h + 1) * 512], start=c == 0, stop=c == 1)
                    m = pe.mark(x)
                    use[f"down{s}"] = m
                    use[f"dn{u}"] = m
                    act.need(m, old(f"stored{s}"))
                    dve.need(m, old(f"stored{s}"))
                    m0 = use[f"bank{b0}"] = act.mark(ACTE.activation(yb[s][:, 0:512], psum[b0][:], ACT.Copy))
                    m1 = use[f"bank{b1}"] = dve.mark(DVE.tensor_copy(yb[s][:, 512:1024], psum[b1][:]))
                    use[f"y{s}"] = (m0, m1)

                def store(n):
                    s = n % 2
                    act.need(*use[f"y{s}"])
                    dst = out_dram[l].rearrange("(b p) d -> b p d", p=P)[slc(2 * NB_ * i + n), :, :].rearrange("b p d -> (b p) d")
                    use[f"stored{s}"] = y_stored[s].mark(nc.scalar.dma_start(dst, yb[s]))
                nblk = len(blocks)
                turn(0)
                for n in range(nblk):
                    gate_up(n)
                    if n + 1 < nblk:
                        turn(n + 1)
                    down(n)
                    store(n)
                    u, k = blocks[n]
                    if k == NB_ - 1 and more:
                        e = slc(2 * i + 2 + u)
                        spl.need(use[f"gu{u}"])
                        r1 = load_gu(e, u)
                        spl.need(use[f"dn{u}"])
                        r2 = load_dn(e, u)
                        use[f"next{u}"] = (r1, r2)
                return use

            for x in (pe, dve, act, pool):
                x.need(dve.last(), pool.last())
            NPAIR = NE // 2
            with loop_over(f"experts{l}", NPAIR - 1) as lp:
                ready_gu = [lp.ahead(slot_full[2 * u], 0) for u in range(2)]
                ready_dn = [lp.ahead(slot_full[2 * u + 1], 0) for u in range(2)]
                use = {}
                pair_of_experts(lp, lp.i, True)
                for key, mk in use.items():
                    if isinstance(mk, tuple):
                        continue
                    lp.carry(key, mk)
                last_use = dict(use)
            ready_gu = [slot_full[2 * u].last() for u in range(2)]
            ready_dn = [slot_full[2 * u + 1].last() for u in range(2)]
            use = last_use
            pair_of_experts(None, NPAIR - 1, False)
            for n in range(8):
                bank_free[n] = [dve.last(), act.last()]
            for n in range(NSLOT):
                slot_free[n] = pe.last()
            phase("combine")
            pool.need(use["stored0"], use["stored1"])
            z = xm_at
            yg = [view(z + n * D, D) for n in range(4)]; z += 4 * D
            free = [None] * 4
            for n, t in enumerate(mt):
                which = 0 if t < NXT else 1
                got = []
                for c in range(2):
                    s = 2 * (n % 2) + c
                    pool.need(free[s])
                    got.append(yg_full[s].mark(nc.gpsimd.indirect_dma_start(
                        out=yg[s], out_offset=None, in_=out_dram[l][:, :],
                        in_offset=bass.IndirectOffsetOnAxis(ap=place_i[:, c, t:t + 1], axis=0))))
                a, c_ = yg[2 * (n % 2)], yg[2 * (n % 2) + 1]
                act.need(got[0])
                m = act.mark(ACTE.activation(a, a, ACT.Copy, scale=wfit[:, 0, t:t + 1]))
                dve.need(m, got[1])
                m = dve.mark(DVE.scalar_tensor_tensor(a, c_, wfit[:, 1, t:t + 1], a, ALU.mult, ALU.add))
                dve.need(m)
                m = dve.mark(DVE.tensor_tensor(a, a, gates[:, which, :], ALU.mult))
                dve.need(m)
                m = dve.mark(DVE.tensor_tensor(resid[:, t, :], resid[:, t, :], a, ALU.add))
                free[2 * (n % 2)] = free[2 * (n % 2) + 1] = m
            phase("overflow")

            for x in (pe, dve, act, pool, spl):
                x.need(m_most)
            busiest = nc.values_load(most_i[0:1, 0:1], min_val=0, max_val=TOK)
            kept = [(x, x.sem, x.count, x.seen) for x in (pe, dve, act, pool, spl)]
            spl.need(*slot_free)
            with nc.If(busiest > CAP):
                for x, nm in zip((pe, dve, act, pool, spl), ("pe", "dve", "act", "pool", "sync")):
                    x.sem, x.count, x.seen = sem(f"overflow{l}_{nm}_done"), 0, {}
                    book.sems[x.sem.name] = x.sem
                o_full = [Lane(book, None, sem(f"overflow{l}_{nm}_full"), 16) for nm in ("gu", "down")]
                for n in range(8):
                    bank_free[n] = None
                acc = view(xm_at, NT, D)
                z = xm_at + NT * D
                hidn = view(z, 2, 512); z += 1024
                silo = view(z, 512); z += 512
                cwl = view(z, NE, n_t); z += NE * NT
                wl, tw = view(z, 2, n_t), view(z + 2 * NT, n_t, NE); z += 2 * NT + NE * NT
                m = dve.mark(DVE.tensor_tensor(wl, wt, wfit, ALU.subtract))
                dve.need(m)
                ce = cwl.rearrange("p e t -> p t e")
                m = dve.mark(DVE.tensor_tensor(ce, ch[0], wl[:, 0, :].unsqueeze(2).to_broadcast([P, n_t, NE]), ALU.mult))
                m = dve.mark(DVE.tensor_tensor(tw, ch[1], wl[:, 1, :].unsqueeze(2).to_broadcast([P, n_t, NE]), ALU.mult))
                dve.need(m)
                m = dve.mark(DVE.tensor_tensor(ce, ce, tw, ALU.add))
                m = dve.mark(DVE.memset(acc[:, 0:n_t, :], 0.0))
                dve.need(m)
                with loop_over(f"overflow{l}", NE) as lp:
                    i = lp.i
                    spl.need(lp.prev("down"))
                    for j, name in enumerate(("w_gate_2", "w_up_2")):
                        r1 = o_full[0].mark(sp.dma_start(w_gu[0][:, :, j * FF:(j + 1) * FF],
                                                         ins[name][l][bass.ts(i, 1), :, :].rearrange("e (k p) n -> p (e k) n", p=P)))
                    r2 = o_full[1].mark(sp.dma_start(w_dn[0], ins["w_down_2"][l][bass.ts(i, 1), :, :].rearrange("e (k p) n -> p (e k) n", p=P)))
                    pe.need(lp.prev("acc"))
                    pe.need(r1, r2)
                    ma = lp.prev("acc")
                    for ts, which in full:
                        c, n = slice(ts[0] * P, (ts[-1] + 1) * P), len(ts) * P
                        for f in range(2):
                            pe.need(ma)
                            for j in range(2):
                                for k in range(KC):
                                    x = PE.matmul(psum[j][:, 0:n], w_gu[0][:, k, j * FF + f * P:j * FF + (f + 1) * P], tT[:, k, c], start=k == 0, stop=k == KC - 1)
                            m = pe.mark(x)
                            act.need(m, ma)
                            m = act.mark(ACTE.activation(silo[:, 0:n], psum[0][:, 0:n], ACT.Silu))
                            dve.need(m, ma)
                            ma = dve.mark(DVE.tensor_tensor(hidn[:, f, 0:n], silo[:, 0:n], psum[1][:, 0:n], ALU.mult))
                        for j, t in enumerate(ts):
                            for h in range(2):
                                pe.need(ma)
                                for k in range(2):
                                    x = PE.matmul(psum[2][:], hidn[:, k, j * P:(j + 1) * P], w_dn[0][:, k, h * 512:(h + 1) * 512], start=k == 0, stop=k == 1)
                                m = pe.mark(x)
                                dve.need(m, ma)
                                a = acc[:, t, h * 512:(h + 1) * 512]
                                ma = dve.mark(DVE.scalar_tensor_tensor(a, psum[2][:], cwl[:, bass.ts(i, 1), t], a, ALU.mult, ALU.add))
                    lp.carry("acc", ma)
                    lp.carry("down", m)
                dve.need(dve.last())
                for t in mt:
                    which = 0 if t < NXT else 1
                    m = dve.mark(DVE.tensor_tensor(acc[:, t, :], acc[:, t, :], gates[:, which, :], ALU.mult))
                    dve.need(m)
                    m = dve.mark(DVE.tensor_tensor(resid[:, t, :], resid[:, t, :], acc[:, t, :], ALU.add))
                phase("overflow end")
                spl.need(pe.last())
            for n in range(8):
                bank_free[n] = None
            for x, s_, c_, n_ in kept:
                x.sem, x.count, x.seen = s_, c_, n_
            assert all(x.last().value() == x.count for x in lanes)

        yo = view(zone, NXT, D)
        m = rms_rows(list(range(NXT)), D, lambda t: resid[:, t, :], yo[:, 0, :])
        dve.need(m)
        s_out = sem("out_stored")
        for t in range(NXT):
            m = dve.mark(DVE.scalar_tensor_tensor(yo[:, t, :], resid[:, t, :], stats[:, t:t + 1], bc[:, B_GF:B_GF + D], ALU.mult, ALU.mult))
            spl.need(m)
            sp.dma_start(out[0, t * P:(t + 1) * P, :], yo[:, t, :]).then_inc(s_out, 16)
        sp.wait_ge(s_out, 16 * NXT)
    return book.found


_NAMES = ["x", "norm_gain", "w_in", "q_norm_a", "k_norm_a", "sinks_a", "q_norm_b", "k_norm_b", "w_out", "c_2", "ctx_2",
          "c_ctx_2", "w_ada_2", "b_ada_2", "g_mix_2", "g_ffn_2", "w_in_2", "conv_w_2", "conv_b_2", "conv_ln_g_2",
          "conv_ln_b_2", "ssd_conv_w_2", "ssd_conv_b_2", "dt_bias_2", "a_log_2", "d_skip_2", "ssd_norm_g_2",
          "w_out_2", "w_router_group_2", "b_router_group_2", "w_router_expert_2", "b_router_expert_2", "w_gate_2",
          "w_up_2", "w_down_2", "g_final_2"]


def _constants():
    import numpy as np
    r, s = np.arange(P)[:, None], np.arange(P)[None, :]
    c = np.zeros((P, NCONST), np.float32)
    c[:, C_ID:C_ID + P] = r == s
    c[:, C_LE:C_LE + P] = r <= s
    c[:, C_LT:C_LT + P] = r < s
    c[:, C_GE:C_GE + P] = r >= s
    c[:, C_GT:C_GT + P] = r > s
    c[:, C_ONE:C_ONE + P] = 1.0
    dist = r - np.arange(2 * P)[None, :] + P
    c[:, C_MA:C_MA + 2 * P] = np.where((dist >= 0) & (dist <= P - 1), 0.0, NEG)
    dist = r - np.arange(4 * P)[None, :] + 3 * P
    count = ((dist >= 0) & (dist <= 128)) * 1 + ((dist >= 0) & (dist % 4 == 0)) * 1 + ((dist >= 0) & (dist % 16 == 0)) * 1
    c[:, C_MB:C_MB + 4 * P] = np.where(count > 0, np.log(np.maximum(count, 1)) / SCALE, NEG)
    half = HD // 2
    inv = np.float32(10000.0) ** (-np.arange(half, dtype=np.float32) / np.float32(half))
    ang = (np.arange(SEQ, dtype=np.float32)[:, None] * inv[None, :]).astype(np.float32)
    tab = np.concatenate([np.cos(ang), np.sin(ang)], axis=1).reshape(NXT, P, HD)
    c[:, C_IO:C_IO + 256] = np.arange(256)
    c[:, C_TOK:C_TOK + 2 * NT:2] = np.arange(P)[:, None]
    c[:, C_TOK + 1:C_TOK + 2 * NT:2] = np.arange(NT)
    c[:, C_CS:C_CS + NXT * HD] = tab.transpose(1, 0, 2).reshape(P, NXT * HD)
    return c


def kernel(**inputs):
    import numpy as np
    import concourse.bacc as bacc
    from concourse.bass_utils import run_bass_kernel_spmd as run
    arrays = {n: np.ascontiguousarray(inputs[n]) for n in _NAMES}
    arrays["consts"] = _constants()
    known = {}
    for _ in range(2):
        nc = bacc.Bacc("TRN2", target_bir_lowering=False, num_devices=1)
        ins = {n: nc.dram_tensor("in_" + n, a.shape, mybir.dt.from_np(a.dtype), kind="ExternalInput").ap()
               for n, a in arrays.items()}
        out = nc.dram_tensor("out", (1, SEQ, D), F32, kind="ExternalOutput").ap()
        known = program(nc, ins, out, known)
    r = run(nc, [{"in_" + n: a for n, a in arrays.items()}], core_ids=[0])
    return r.results[0]["out"]
```

```python
import concourse.bass as bass
from concourse import mybir
from contextlib import ExitStack

F32 = mybir.dt.float32
ALU = mybir.AluOpType
ACT = mybir.ActivationFunctionType
AX = mybir.AxisListType

P = 128
D = 1024
KC = D // P
SEQ, CTX = 512, 256
NXT, NCT = SEQ // P, CTX // P
NT = NXT + NCT
TOK = SEQ + CTX
EPS, LN_EPS = 1e-6, 1e-5
HD = 64
AH = BH = 8
AKV = 2
SCALE = HD ** -0.5
NEG = -1e30
LAYERS = 2
GRID_W = 64
ROWS = SEQ // GRID_W
CK, SK = 31, 5
DC = DS = 512
SH = 8
NS_ = 128
DIN = 2576
NG, NPG, NE = 4, 4, 16
FF = 256
EXTRA = (4, 0)

C_ID, C_LE, C_LT, C_GE, C_GT, C_ONE = (P * n for n in range(6))
C_MA = 6 * P
C_MB = C_MA + 2 * P
C_CS = C_MB + 4 * P
C_IO = C_CS + 4 * HD
C_TOK = C_IO + 256
NCONST = C_TOK + 2 * NT
V_NG, V_C, V_CC = 0, 8, 16
V_L = 24
V_LN = 40
B_QK, B_SK, B_DTB, B_AL, B_DS, B_BR, B_GF = 0, 256, 264, 296, 328, 344, 384
NB = B_GF + D


NEVER = -1 << 30


class Mark:

    def __init__(self, sem, count, loop):
        self.sem, self.count, self.loop = sem, count, loop

    def value(self):
        if self.loop is None:
            return self.count
        return self.loop.value(self.sem, self.count)


class Loop:

    def __init__(self, book, name, n):
        self.book, self.name, self.n = book, name, n
        self.i = None
        self.base = {}
        self.local = {}
        self.per = book.known.get(name, {}).get("per", {})
        self.carried = book.known.get(name, {}).get("carry", {})
        self.out = {}

    def value(self, sem, count):
        k = sem.name
        if self.i is None:
            return self.base[k] + (self.n - 1) * self.local.get(k, 0) + count
        return self.base[k] + count + self.i * self.per.get(k, 0)

    def prev(self, name):
        if name not in self.carried:
            return None
        k, count = self.carried[name]
        return Prev(self, self.book.sems[k], count - self.per[k])

    def ahead(self, lane, less):
        return Mark(lane.sem, -less, self)

    def carry(self, name, mark):
        self.out[name] = (mark.sem.name, mark.count)


class Prev:
    def __init__(self, loop, sem, count):
        self.loop, self.sem, self.count = loop, sem, count

    def value(self):
        return self.loop.value(self.sem, self.count)


class Book:

    def __init__(self, known):
        self.known, self.sems, self.loop, self.found = known, {}, None, {}
        self.lanes = []


class Lane:

    def __init__(self, book, eng, sem, by=1):
        self.book, self.eng, self.sem, self.by, self.count = book, eng, sem, by, 0
        self.seen = {}
        book.sems[sem.name] = sem
        book.lanes.append(self)

    def mark(self, inst):
        inst.then_inc(self.sem, self.by)
        loop = self.book.loop
        if loop is None:
            self.count += self.by
            return Mark(self.sem, self.count, None)
        k = self.sem.name
        loop.local[k] = loop.local.get(k, 0) + self.by
        return Mark(self.sem, loop.local[k], loop)

    def last(self):
        loop = self.book.loop
        if loop is None:
            return Mark(self.sem, self.count, None)
        return Mark(self.sem, loop.local.get(self.sem.name, 0), loop)

    def need(self, *marks):
        best = {}
        todo = list(marks)
        while todo:
            m = todo.pop(0)
            if m is None:
                continue
            if isinstance(m, (list, tuple)):
                todo = list(m) + todo
                continue
            k = (m.sem.name, id(m.loop) if m.loop is not None and m.loop.i is not None else None)
            size = m.count if k[1] else m.value()
            if k not in best or best[k][0] < size:
                best[k] = (size, m)
        for (name, in_loop), (size, m) in best.items():
            if in_loop:
                if self.seen.get((name, in_loop), NEVER) >= size:
                    continue
                self.seen[name, in_loop] = size
            else:
                if self.seen.get(name, 0) >= size or size <= 0:
                    continue
                if self.book.loop is None:
                    self.seen[name] = size
            self.eng.wait_ge(m.sem, m.value())


def stage(nc, name):
    pass


def program(nc, ins, out, known):
    book = Book(known)
    ctx = ExitStack()
    with ctx:
        def sem(name):
            return ctx.enter_context(nc.semaphore(name))

        pe = Lane(book, nc.tensor, sem("pe_done"))
        dve = Lane(book, nc.vector, sem("dve_done"))
        act = Lane(book, nc.scalar, sem("act_done"))
        pool = Lane(book, nc.gpsimd, sem("pool_done"))
        sp = nc.sync
        PE, DVE, ACTE, POOL = nc.tensor, nc.vector, nc.scalar, nc.gpsimd
        lanes = [pe, dve, act, pool]

        spl = Lane(book, nc.sync, sem("sync_done"))

        class loop_over:

            def __init__(self, name, n):
                self.loop = Loop(book, name, n)

            def __enter__(self):
                lp = self.loop
                for x in book.lanes:
                    lp.base[x.sem.name] = x.count
                self.cm = nc.Fori(0, lp.n)
                lp.i = self.cm.__enter__()
                book.loop = lp
                return lp

            def __exit__(self, *a):
                lp = self.loop
                self.cm.__exit__(*a)
                book.loop, lp.i = None, None
                for x in book.lanes:
                    x.count += lp.n * lp.local.get(x.sem.name, 0)
                book.found[lp.name] = {"per": dict(lp.local), "carry": dict(lp.out)}

        def phase(name=""):
            stage(nc, name)
            marks = [x.last() for x in lanes]
            for x in lanes:
                x.need(*marks)

        sb = ctx.enter_context(nc.sbuf_tensor("arena", [P, 53200], F32))
        top = [0]

        def place(n):
            at = top[0]
            top[0] += n
            return at

        def view(at, *dims):
            n = 1
            for d in dims:
                n *= d
            v = sb[:, at:at + n]
            if len(dims) == 2:
                v = v.rearrange("p (a b) -> p a b", b=dims[1])
            elif len(dims) == 3:
                v = v.rearrange("p (a b c) -> p a b c", b=dims[1], c=dims[2])
            return v

        NSLOT = 4
        SLOT = KC * 512
        ring_at = place(NSLOT * SLOT)
        resid_at = place(NT * D)
        ctx_at = resid_at + NXT * D
        resid = view(resid_at, NT, D)
        const = view(place(NCONST), NCONST)
        vec = view(place(5 * P), 5 * P)
        bc = view(place(NB), NB)
        mods = view(place(LAYERS * 48 * 2), LAYERS, 48, 2)
        router = view(place(LAYERS * KC * 20), LAYERS, KC, 20)
        gate_at = place(2 * D)
        gates = view(gate_at, 2, D)
        stat_at = place(1024)
        zone = top[0]
        ident = const[:, C_ID:C_ID + P]
        ones = const[:, C_ONE:C_ONE + P]

        psum = [ctx.enter_context(nc.psum_tensor(f"psum{n}", [P, 512], F32)) for n in range(8)]
        bank_free = [None] * 8
        turn = [0]
        banks_held = set()

        def bank():
            while turn[0] % 8 in banks_held:
                turn[0] += 1
            n = turn[0] % 8
            turn[0] += 1
            pe.need(bank_free[n])
            return n

        slot_full = [Lane(book, None, sem(f"slot_full{n}"), 16) for n in range(NSLOT)]
        slot_free = [None] * NSLOT
        slot_turn = [0]
        held = set()

        ctx_full = Lane(book, None, sem("context_loaded"), 16)

        def slot_view(n, width):
            return sb[:, ring_at + n * SLOT:ring_at + n * SLOT + KC * width].rearrange("p (k n) -> p k n", n=width)

        def fetch(src, width):
            while slot_turn[0] % NSLOT in held:
                slot_turn[0] += 1
            n = slot_turn[0] % NSLOT
            slot_turn[0] += 1
            spl.need(slot_free[n])
            if slot_turn[0] == 2:
                spl.need(m_small)
            dst = slot_view(n, width)
            return dst, slot_full[n].mark(sp.dma_start(dst, src.rearrange("(k p) n -> p k n", p=P))), n

        tok_dram = [nc.dram_tensor(f"tokens{l}", (SEQ if l == LAYERS - 1 else TOK, D), F32, kind="Internal").ap() for l in range(LAYERS)]
        out_dram = [nc.dram_tensor(f"expert_out{l}", ((NE + EXTRA[l]) * P, D), F32, kind="Internal").ap() for l in range(LAYERS)]
        tok_stored = Lane(book, None, sem("tokens_stored"), 16)
        gx_full = [Lane(book, None, sem(f"gathered{n}"), 16) for n in range(4)]
        yg_full = [Lane(book, None, sem(f"collected{n}"), 16) for n in range(4)]
        y_stored = [Lane(book, None, sem(f"expert_out_stored{n}"), 16) for n in range(2)]

        s_small = sem("small_loaded")
        rows = view(zone, 5, P)
        small = [0]

        def load(dst, src):
            nc.scalar.dma_start(dst, src).then_inc(s_small, 16)
            small[0] += 16
        load(const, ins["consts"])
        load(resid[:, 0:NXT, :], ins["x"][0].rearrange("(t p) d -> p t d", p=P))

        def load_rows(g, r, src, n):
            load(rows[r:r + n, g, :], src)
        load_rows(0, V_NG, ins["norm_gain"].rearrange("a (k n) -> (a k) n", n=P), 8)
        load_rows(0, V_C, ins["c_2"].rearrange("a (k n) -> (a k) n", n=P), 8)
        load_rows(0, V_CC, ins["c_ctx_2"].rearrange("(k n) -> k n", n=P), 8)
        for l in range(LAYERS):
            at = V_L + l * V_LN
            for name, n in (("g_mix_2", 8), ("g_ffn_2", 8), ("conv_b_2", 4), ("conv_ln_g_2", 4),
                            ("conv_ln_b_2", 4), ("ssd_conv_b_2", 8), ("ssd_norm_g_2", 4)):
                load_rows(0, at, ins[name][l].rearrange("(k n) -> k n", n=P), n)
                at += n
            load_rows(1, l * 48, ins["b_ada_2"][l].rearrange("(k n) -> k n", n=P), 48)
            load_rows(2 + l, 0, ins["conv_w_2"][l].rearrange("t (k n) -> (t k) n", n=P), 4 * CK)
            load_rows(4, l * 40, ins["ssd_conv_w_2"][l].rearrange("t (k n) -> (t k) n", n=P), 8 * SK)

        def load_bc(at, src):
            n = src.shape[-1]
            load(bc[:, at:at + n], src.partition_broadcast(P))
        for n, name in enumerate(("q_norm_a", "k_norm_a", "q_norm_b", "k_norm_b")):
            load_bc(B_QK + n * HD, ins[name][0])
        load_bc(B_SK, ins["sinks_a"][0])
        m_small = Mark(s_small, small[0], None)
        s_small, small[0] = sem("second_block_loaded"), 0
        for l in range(LAYERS):
            load_bc(B_DTB + l * 16, ins["dt_bias_2"][l].rearrange("a h -> (a h)"))
            load_bc(B_AL + l * 16, ins["a_log_2"][l].rearrange("a h -> (a h)"))
            load_bc(B_DS + l * 8, ins["d_skip_2"][l])
            load_bc(B_BR + l * 20, ins["b_router_group_2"][l])
            load_bc(B_BR + l * 20 + 4, ins["b_router_expert_2"][l])
            load(router[:, l, :, 0:4], ins["w_router_group_2"][l].rearrange("(k p) n -> p k n", p=P))
            load(router[:, l, :, 4:20], ins["w_router_expert_2"][l].rearrange("(k p) n -> p k n", p=P))
        m_second = Mark(s_small, small[0], None)

        for x in lanes:
            x.need(m_small)
        nrow = [V_L + 2 * V_LN, 96, 4 * CK, 4 * CK, 80]
        b = bank()
        for g in range(4):
            m = pe.mark(PE.transpose(psum[b][:, g * P:g * P + nrow[g]], rows[0:nrow[g], g, :], ident[0:nrow[g], 0:nrow[g]]))
        b2 = bank()
        m2 = pe.mark(PE.transpose(psum[b2][:, 0:nrow[4]], rows[0:nrow[4], 4, :], ident[0:nrow[4], 0:nrow[4]]))
        dve.need(m)
        for g in range(4):
            mv = dve.mark(DVE.tensor_copy(vec[:, g * P:g * P + nrow[g]], psum[b][:, g * P:g * P + nrow[g]]))
        dve.need(m2)
        mv = dve.mark(DVE.tensor_copy(vec[:, 4 * P:4 * P + nrow[4]], psum[b2][:, 0:nrow[4]]))
        bank_free[b] = bank_free[b2] = mv
        cvec = view(stat_at, KC, 2)
        act.need(mv)
        for j, at in enumerate((V_C, V_CC)):
            m_cvec = act.mark(ACTE.activation(cvec[:, :, j], vec[:, at:at + KC], ACT.Silu))
        phase()

        arow = [bc[:, B_GF + n * 512:B_GF + (n + 1) * 512] for n in range(2)]
        arow_free = [None] * 2
        ada_late = []

        def ada_turn():
            l, n, s, m = ada_late.pop(0)
            b = bank()
            pe.need(m)
            for f in range(4):
                i = PE.transpose(psum[b][:, 2 * f:2 * f + 2], arow[s][0:2, f * P:(f + 1) * P], ident[0:2, 0:2])
            arow_free[s] = pe.mark(i)
            dve.need(arow_free[s])
            bias = vec[:, P + l * 48 + 4 * n:P + l * 48 + 4 * n + 4].unsqueeze(2).to_broadcast([P, 4, 2])
            bank_free[b] = dve.mark(DVE.tensor_tensor(
                mods[:, l, 4 * n:4 * n + 4, :], psum[b][:, 0:8].rearrange("p (f j) -> p f j", j=2), bias, ALU.add))

        def ada_piece(l, n):
            w, ready, slot = fetch(ins["w_ada_2"][l][:, n * 512:(n + 1) * 512], 512)
            pe.need(ready)
            b = bank()
            for k in range(KC):
                i = PE.matmul(psum[b][0:2, :], cvec[:, k, :], w[:, k, :], start=k == 0, stop=k == KC - 1)
            m = pe.mark(i)
            slot_free[slot] = m
            s = n % 2
            act.need(m, arow_free[s])
            m = act.mark(ACTE.activation(arow[s][0:2, :], psum[b][0:2, :], ACT.Copy))
            bank_free[b] = m
            if ada_late:
                ada_turn()
            ada_late.append((l, n, s, m))
        ada_todo = [(l, n) for l in range(LAYERS) for n in range(12)]

        pick = view(stat_at + 1016, 2, 2)
        m_pick = [pool.mark(POOL.memset(pick, 0.0))]
        pool.need(m_pick[0])
        for j in range(2):
            m_pick.append(pool.mark(POOL.memset(pick[:, j, j:j + 1], 1.0)))

        def ada_on_dve(todo, at):
            acc = [view(at + n * 1024, 2, 512) for n in range(2)]
            acc_free = [None] * 2
            summed = []

            def over_partitions():
                if ada_late:
                    ada_turn()
                if summed:
                    l, n, u, js, m = summed.pop(0)
                    b = bank()
                    pe.need(m, m_pick)
                    for j in js:
                        i = PE.matmul(psum[b][0:2, :], pick[:, j, :], acc[u][:, j, :], start=j == 0, stop=j == js[-1])
                    m = acc_free[u] = pe.mark(i)
                    act.need(m, arow_free[n % 2])
                    m = bank_free[b] = act.mark(ACTE.activation(arow[n % 2][0:2, :], psum[b][0:2, :], ACT.Copy))
                    ada_late.append((l, n, n % 2, m))
            for turn_, (l, n) in enumerate(todo):
                js = (0,) if l == LAYERS - 1 and n >= 4 else (0, 1)
                w, ready, slot = fetch(ins["w_ada_2"][l][:, n * 512:(n + 1) * 512], 512)
                u = turn_ % 2
                dve.need(ready, acc_free[u])
                ms = [None, None]
                for k in range(KC):
                    for j in js:
                        o, c = acc[u][:, j, :], cvec[:, k, j:j + 1]
                        dve.need(ms[j])
                        ms[j] = dve.mark(DVE.tensor_scalar(o, w[:, k, :], c, None, ALU.mult) if k == 0 else
                                         DVE.scalar_tensor_tensor(o, w[:, k, :], c, o, ALU.mult, ALU.add))
                    if k == 3:
                        over_partitions()
                    yield
                slot_free[slot] = list(ms)
                summed.append((l, n, u, js, list(ms)))
            while summed or ada_late:
                over_partitions()
                yield

        def steps_of(gen, n):
            for _ in range(n):
                next(gen, None)

        def some_ada(n):
            for _ in range(n):
                if ada_todo:
                    ada_piece(*ada_todo.pop(0))
                    if not ada_todo or ada_todo[0][1] == 0:
                        ada_turn()

        stats = view(stat_at + 16, 96)
        def sum_squares(t, row, scratch):
            act.need(act.last())
            return act.mark(ACTE.activation(scratch, row, ACT.Square, accum_out=stats[:, t:t + 1]))

        def rms_rows(tiles, width, src=None, scratch=None, at=0, eps=EPS):
            for t in tiles if scratch is not None else ():
                sum_squares(t, src(t), scratch)
            a, z = at + tiles[0], at + tiles[-1] + 1
            dve.need(act.last())
            m = dve.mark(DVE.tensor_scalar(stats[:, a:z], stats[:, a:z], 1.0 / width, eps, ALU.mult, ALU.add))
            act.need(m)
            m = act.mark(ACTE.activation(stats[:, a:z], stats[:, a:z], ACT.Sqrt))
            dve.need(m)
            return dve.mark(DVE.reciprocal(stats[:, a:z], stats[:, a:z]))

        def normed_features(tiles_of, dst, xn, scale_of, bias_of, summed=False):
            tiles = [t for ts, _ in tiles_of for t in ts]
            m = rms_rows(tiles, D) if summed else rms_rows(tiles, D, lambda t: resid[:, t, :], xn[:, tiles[0], :])
            dve.need(m)
            ms = {}
            act.need(m)
            for t in tiles:
                if t % 2:
                    ms[t] = dve.mark(DVE.tensor_scalar(xn[:, t, :], resid[:, t, :], stats[:, t:t + 1], None, ALU.mult))
                else:
                    ms[t] = act.mark(ACTE.activation(xn[:, t, :], resid[:, t, :], ACT.Copy, scale=stats[:, t:t + 1]))
            for k in range(KC):
                for ts, which in tiles_of:
                    b = bank()
                    for j, t in enumerate(ts):
                        pe.need(ms[t])
                        i = PE.transpose(psum[b][:, j * P:(j + 1) * P], xn[:, t, k * P:(k + 1) * P], ident)
                    m = pe.mark(i)
                    n = len(ts) * P
                    o = dst[:, k, ts[0] * P:ts[0] * P + n]
                    sc, bi = scale_of(k, which), bias_of(k, which)
                    if k % 2:
                        dve.need(m)
                        if bi is None:
                            bank_free[b] = dve.mark(DVE.tensor_scalar(o, psum[b][:, 0:n], sc, None, ALU.mult))
                        else:
                            bank_free[b] = dve.mark(DVE.tensor_scalar(o, psum[b][:, 0:n], sc, bi, ALU.mult, ALU.add))
                    else:
                        act.need(m)
                        bank_free[b] = act.mark(ACTE.activation(o, psum[b][:, 0:n], ACT.Identity, scale=sc,
                                                                bias=0.0 if bi is None else bi))

        def tok_product(xT, t, w, width, cols=0, start=True, stop=True, kc=KC, b=None, off=0):
            if b is None:
                b = bank()
            for k in range(kc):
                i = PE.matmul(psum[b][:, off:off + width], xT[:, k, t * P:(t + 1) * P], w[:, k, cols:cols + width],
                              start=k == 0, stop=k == kc - 1)
            return b, pe.mark(i)

        z = zone
        hT = view(z, KC, SEQ); z += KC * SEQ
        qkT_at = z
        qTA = view(z, 4, SEQ); z += 4 * SEQ
        kTA = view(z, 4, SEQ); z += 4 * SEQ
        qTB = view(z, 4, SEQ); z += 4 * SEQ
        kTB = view(z, 4, SEQ); z += 4 * SEQ
        vA = view(z, NXT, 4, HD); z += NXT * 256
        vB = view(z, NXT, 4, P); z += NXT * 512
        mix = view(z, NXT, D); z += NXT * D
        tmp_at = z; z += 2048
        cosg = view(gate_at, 4, NXT, HD)
        sing = view(gate_at + 1024, 4, NXT, HD)
        assert z <= 53200
        tabs = const[:, C_CS:C_CS + 4 * HD].rearrange("p (t n) -> p t n", n=HD)
        for n in range(4):
            g = bc[:, B_QK + n * HD:B_QK + (n + 1) * HD]
            gl, gh = (g[:, o:o + 32].unsqueeze(1).to_broadcast([P, NXT, 32]) for o in (0, 32))
            pool.mark(POOL.tensor_tensor(cosg[:, n, :, 0:32], tabs[:, :, 0:32], gl, ALU.mult))
            pool.mark(POOL.tensor_tensor(cosg[:, n, :, 32:64], tabs[:, :, 0:32], gh, ALU.mult))
            pool.mark(POOL.tensor_tensor(sing[:, n, :, 32:64], tabs[:, :, 32:64], gl, ALU.mult))
            m = pool.mark(POOL.tensor_tensor(sing[:, n, :, 0:32], tabs[:, :, 32:64], gh, ALU.mult))
            pool.need(m)
            m_tab = pool.mark(POOL.tensor_scalar(sing[:, n, :, 0:32], sing[:, n, :, 0:32], -1.0, None, ALU.mult))

        xn = view(qkT_at, NXT, D)
        normed_features([(list(range(NXT)), 0)], hT, xn,
                        lambda k, w: vec[:, V_NG + k:V_NG + k + 1], lambda k, w: None)
        phase()

        sq = view(tmp_at, 512)
        qn = view(tmp_at + 512, 512)
        crs = view(tmp_at + 1024, 512)
        rots = [view(tmp_at + 1536 + n * 512, 512) for n in range(3)]
        assert tmp_at + 1536 + 1536 <= 53200
        dve.need(m_tab)
        pool.need(m_tab)
        reads = {"qn": None, "rot": [None] * 3}
        turns = []
        unit = [0]

        def rotary(b, m, kind, heads, t, dst, dup):
            n = heads * HD
            slot = unit[0] % 3
            unit[0] += 1
            rot = rots[slot]
            act.need(m, reads.get("sq"))
            ma = act.mark(ACTE.activation(sq[:, 0:n], psum[b][:, 0:n], ACT.Square))
            hs = stats[:, 0:heads]
            dve.need(ma)
            m1 = dve.mark(DVE.tensor_reduce(hs, sq[:, 0:n].rearrange("p (h d) -> p h d", d=HD), AX.X, ALU.add))
            reads["sq"] = m1
            dve.need(m1)
            m1 = dve.mark(DVE.tensor_scalar(hs, hs, 1.0 / HD, EPS, ALU.mult, ALU.add))
            act.need(m1)
            m1 = act.mark(ACTE.activation(hs, hs, ACT.Sqrt))
            dve.need(m1)
            m1 = dve.mark(DVE.reciprocal(hs, hs))
            dve.need(m1, reads["qn"])
            q3 = qn[:, 0:n].rearrange("p (h d) -> p h d", d=HD)
            r3 = rot[:, 0:n].rearrange("p (h d) -> p h d", d=HD)
            c3 = crs[:, 0:n].rearrange("p (h d) -> p h d", d=HD)
            m1 = dve.mark(DVE.tensor_tensor(q3, psum[b][:, 0:n].rearrange("p (h d) -> p h d", d=HD),
                                            hs.unsqueeze(2).to_broadcast([P, heads, HD]), ALU.mult))
            bank_free[b] = m1
            pool.need(m1, reads.get("crs"))
            pool.mark(POOL.tensor_tensor(c3[:, :, 0:32], q3[:, :, 32:64],
                                         sing[:, kind, t:t + 1, 0:32].to_broadcast([P, heads, 32]), ALU.mult))
            m2 = pool.mark(POOL.tensor_tensor(c3[:, :, 32:64], q3[:, :, 0:32],
                                              sing[:, kind, t:t + 1, 32:64].to_broadcast([P, heads, 32]), ALU.mult))
            reads["qn"] = m2
            dve.need(m1, reads["rot"][slot])
            m3 = dve.mark(DVE.tensor_tensor(r3, q3, cosg[:, kind, t:t + 1, :].to_broadcast([P, heads, HD]), ALU.mult))
            dve.need(m2, m3)
            if dup:
                m3 = dve.mark(DVE.tensor_tensor(r3, r3, c3, ALU.add))
                d4 = rot[:, n:3 * n].rearrange("p (h c d) -> p h c d", c=2, d=HD)
                dve.need(m3)
                for c in range(2):
                    m3 = dve.mark(DVE.tensor_copy(d4[:, :, c, :], r3))
                rot = rot[:, n:3 * n]
            else:
                m3 = dve.mark(DVE.tensor_tensor(r3, r3, c3, ALU.add))
            reads["crs"] = m3
            turns.append((rot, slot, m3, heads, t, dst, dup))

        def turn_heads():
            rot, slot, m3, heads, t, dst, dup = turns.pop(0)
            pairs = 2 if dup else 4
            b = bank()
            pe.need(m3)
            for j in range(pairs):
                i = PE.transpose(psum[b][:, j * P:(j + 1) * P], rot[:, j * P:(j + 1) * P], ident)
            m4 = pe.mark(i)
            reads["rot"][slot] = m4
            act.need(m4)
            got = psum[b][:, 0:pairs * P].rearrange("p (j t) -> p j t", t=P)
            if dup:
                for kv in range(2):
                    o = dst[:, 2 * kv:2 * kv + 2, t * P:(t + 1) * P]
                    m5 = act.mark(ACTE.activation(o, got[:, kv:kv + 1, :].to_broadcast([P, 2, P]), ACT.Copy))
            else:
                m5 = act.mark(ACTE.activation(dst[:, :, t * P:(t + 1) * P], got, ACT.Copy))
            bank_free[b] = m5

        def in_piece(c0, width, use):
            w, ready, s = fetch(ins["w_in"][0][:, c0:c0 + width], width)
            pe.need(ready)
            for t in range(NXT):
                b, m = tok_product(hT, t, w, width)
                use(b, m, t)
                if len(turns) > 2:
                    turn_heads()
                steps_of(ada_gen, 4)
            slot_free[s] = m

        def use_q(kind, dst):
            return lambda b, m, t: rotary(b, m, kind, 8, t, dst, False)

        def use_kv_a(b, m, t):
            act.need(m)
            v = psum[b][:, 128:256].rearrange("p (h d) -> p h d", d=HD)
            for kv in range(2):
                act.mark(ACTE.activation(vA[:, t, 2 * kv:2 * kv + 2, :], v[:, kv:kv + 1, :].to_broadcast([P, 2, HD]), ACT.Copy))
            rotary(b, m, 1, 2, t, kTA, True)

        def use_v_b(b, m, t):
            act.need(m)
            bank_free[b] = act.mark(ACTE.activation(vB[:, t, :, :].rearrange("p a b -> p (a b)"), psum[b][:], ACT.Copy))

        def use_gate(off):
            def f(b, m, t):
                act.need(m)
                bank_free[b] = act.mark(ACTE.activation(mix[:, t, off:off + 512], psum[b][:], ACT.Silu))
            return f
        ada_gen = ada_on_dve([ada_todo.pop(0) for _ in range(12)], ctx_at)
        in_piece(0, 512, use_q(0, qTA))
        in_piece(2304, 512, use_v_b)
        in_piece(1280, 512, use_q(2, qTB))
        in_piece(768, 512, use_gate(0))
        in_piece(1792, 512, use_q(3, kTB))
        in_piece(512, 256, use_kv_a)
        in_piece(2816, 512, use_gate(512))
        while turns:
            turn_heads()
        for _ in ada_gen:
            pass
        spl.need(pe.last())
        m_ctx = ctx_full.mark(sp.dma_start(resid[:, NXT:NT, :], ins["ctx_2"][0].rearrange("(t p) d -> p t d", p=P)))
        phase()

        NPB = 3
        pb = [view(zone + n * 512, 512) for n in range(NPB)]
        pT = [view(zone + (NPB + n) * 512, 512) for n in range(NPB)]
        qs = [view(zone + 2 * NPB * 512 + n * SEQ, SEQ) for n in range(2)]
        ks = [view(gate_at + n * SEQ, SEQ) for n in range(2)]
        st = view(stat_at + 128, 16, 8)
        on = view(tmp_at, 4, HD)
        nsink = view(stat_at + 256, AH)
        dve.need(dve.mark(DVE.tensor_scalar(nsink, bc[:, B_SK:B_SK + AH], -1.0, None, ALU.mult)))
        S_B, T_B, O_B = (0, 1, 2), (3, 4, 5), (6, 7)
        maskA = const[:, C_MA:C_MA + 256]
        maskB = const[:, C_MB:C_MB + 512]
        with loop_over("attention", 4) as lp:
            i = lp.i
            def pair(x):
                return x[:, bass.ts(i, 1), :].rearrange("p a b -> p (a b)")
            pe_all = lp.prev("pe")
            dve.need(pe_all)
            pool.need(pe_all)
            mq = [dve.mark(DVE.tensor_copy(qs[0], pair(qTA))), dve.mark(DVE.tensor_copy(qs[1], pair(qTB)))]
            mk = [pool.mark(POOL.tensor_copy(ks[0], pair(kTA))), pool.mark(POOL.tensor_copy(ks[1], pair(kTB)))]
            act.need(dve.last())
            units = [(k, par, t) for par in range(2) for k in range(2) for t in range(NXT)]
            state = {}

            def keys(k, t):
                return range(max(0, t - 1), t + 1) if k == 0 else range(t + 1)

            def scores(u):
                k, par, t = units[u]
                kt = keys(k, t)
                pe.need(mq[k], mk[k], state.get(("max", u - 3)) or lp.prev(f"max{(u - 3) % 16}"))
                half = slice(par * HD, par * HD + HD)
                kT = ks[k][half, kt[0] * P:(kt[-1] + 1) * P]
                state["s", u] = pe.mark(PE.matmul(psum[S_B[u % 3]][:, 0:len(kt) * P], qs[k][half, t * P:(t + 1) * P], kT,
                                                  start=True, stop=True))

            def softmax(u):
                k, par, t = units[u]
                n = len(keys(k, t)) * P
                mask = maskA[:, 256 - n:256] if k == 0 else maskB[:, 512 - n:512]
                c = st[:, u, :]
                dve.need(state["s", u], state.get(("tr", u - NPB)) or lp.prev(f"tr{(u - NPB) % 16}"))
                dve.mark(DVE.memset(c[:, 7:8], 0.0))
                m = dve.mark(DVE.tensor_tensor_reduce(pb[u % NPB][:, 0:n], psum[S_B[u % 3]][:, 0:n], mask, -SCALE, -NEG,
                                                      ALU.add, ALU.min, c[:, 0:1]))
                state["max", u] = m
                if k == 0:
                    sk = nsink.rearrange("p (i h) -> p i h", h=2)[:, bass.ts(i, 1), par]
                    dve.need(m)
                    m = dve.mark(DVE.tensor_tensor(c[:, 0:1], c[:, 0:1], sk, ALU.min))
                act.need(m)
                m2 = act.mark(ACTE.activation(pb[u % NPB][:, 0:n], pb[u % NPB][:, 0:n], ACT.Exp, bias=c[:, 0:1], scale=-1.0,
                                              accum_out=c[:, 2:3]))
                if k == 0:
                    m2 = act.mark(ACTE.activation(c[:, 3:4], sk, ACT.Exp, bias=c[:, 0:1], scale=-1.0))
                state["exp", u] = m2

            def turn_p(u):
                k, par, t = units[u]
                n = len(keys(k, t))
                pe.need(state["exp", u], state.get(("pT", u - 3)) or lp.prev(f"pT{(u - 3) % 16}"))
                for j in range(n):
                    x = PE.transpose(psum[T_B[u % 3]][:, j * P:(j + 1) * P], pb[u % NPB][:, j * P:(j + 1) * P], ident)
                m = pe.mark(x)
                state["tr", u] = m
                act.need(m, state.get(("pv", u - NPB)) or lp.prev(f"pv{(u - NPB) % 16}"))
                state["pT", u] = act.mark(ACTE.activation(pT[u % NPB][:, 0:n * P], psum[T_B[u % 3]][:, 0:n * P], ACT.Copy))

            def value(u):
                k, par, t = units[u]
                kt_ = keys(k, t)
                q = u // 4
                pe.need(state["pT", u], state.get(("o", q - 2)) or lp.prev(f"o{(q - 2) % 4}"))
                o = psum[O_B[q % 2]][:, t * HD:(t + 1) * HD]
                for j, kt in enumerate(kt_):
                    if k == 0:
                        v = vA[:, kt, bass.ts(i, 1), :].rearrange("p a b -> p (a b)")
                    else:
                        v = vB[:, kt, bass.ts(i, 1), par * HD:(par + 1) * HD].rearrange("p a b -> p (a b)")
                    x = PE.matmul(o, pT[u % NPB][:, j * P:(j + 1) * P], v, start=j == 0, stop=j == len(kt_) - 1)
                state["pv", u] = pe.mark(x)
                if t < NXT - 1:
                    return
                dve.need(state["pv", u], state["exp", u])
                c = st[:, 4 * q:4 * q + 4, :]
                if k == 0:
                    m = dve.mark(DVE.tensor_tensor(c[:, :, 2], c[:, :, 2], c[:, :, 3], ALU.add))
                    dve.need(m)
                m = dve.mark(DVE.reciprocal(c[:, :, 4], c[:, :, 2]))
                dve.need(m)
                m = dve.mark(DVE.tensor_tensor(on, psum[O_B[q % 2]][:, 0:4 * HD].rearrange("p (t d) -> p t d", d=HD),
                                               c[:, :, 4:5].to_broadcast([P, 4, HD]), ALU.mult))
                state["o", q] = m
                g = mix[:, :, k * 512:(k + 1) * 512].rearrange("p t (i n) -> p t i n", n=P)[:, :, bass.ts(i, 1), par * HD:(par + 1) * HD]
                g = g.rearrange("p t a b -> p t (a b)")
                dve.need(m)
                dve.mark(DVE.tensor_tensor(g, on, g, ALU.mult))

            n = len(units)
            for u in range(n + 3):
                if u < n:
                    scores(u)
                    softmax(u)
                if u >= 1 and u - 1 < n:
                    turn_p(u - 1)
                if u >= 2 and u - 2 < n:
                    value(u - 2)
            for u in range(n - 3, n):
                for key in ("max", "tr", "pT", "pv"):
                    lp.carry(f"{key}{u}", state[key, u])
            for q in (2, 3):
                lp.carry(f"o{q}", state["o", q])
            lp.carry("pe", pe.last())
        for n in range(8):
            bank_free[n] = [dve.last(), act.last()]
        phase()

        mT = view(qkT_at, KC, SEQ)

        def transposed(src, tiles, k_of, dst, dst_k, scale=None):
            for k in range(k_of):
                for ts in (tiles[i:i + 4] for i in range(0, len(tiles), 4)):
                    b = bank()
                    for j, t in enumerate(ts):
                        i = PE.transpose(psum[b][:, j * P:(j + 1) * P], src[:, t, k * P:(k + 1) * P], ident)
                    m = pe.mark(i)
                    o = dst[:, dst_k + k, ts[0] * P:(ts[-1] + 1) * P]
                    n = len(ts) * P
                    if k % 2:
                        dve.need(m)
                        if scale is None:
                            mo = dve.mark(DVE.tensor_copy(o, psum[b][:, 0:n]))
                        else:
                            mo = dve.mark(DVE.tensor_scalar(o, psum[b][:, 0:n], scale(k), None, ALU.mult))
                    else:
                        act.need(m)
                        mo = act.mark(ACTE.activation(o, psum[b][:, 0:n], ACT.Copy, scale=1.0 if scale is None else scale(k)))
                    bank_free[b] = mo
        transposed(mix, list(range(NXT)), KC, mT, 0)
        phase()
        for h in range(2):
            w, ready, s = fetch(ins["w_out"][0][:, h * 512:(h + 1) * 512], 512)
            pe.need(ready)
            for t in range(NXT):
                b, m = tok_product(mT, t, w, 512)
                dve.need(m)
                r = resid[:, t, h * 512:(h + 1) * 512]
                bank_free[b] = dve.mark(DVE.tensor_tensor(r, r, psum[b][:], ALU.add))
            slot_free[s] = m
        phase()

        for x in lanes:
            x.need(m_ctx, m_second)
        for l in range(LAYERS):
            last = l == LAYERS - 1
            xt, ct = list(range(NXT)), list(range(NXT, NT))
            streams = [(xt, 0), (ct, 1)]
            full = [(xt, 0)] if last else streams
            vl = V_L + l * V_LN
            V_GM, V_GF, V_CB, V_LG, V_LB, V_SB, V_SN = vl, vl + 8, vl + 16, vl + 20, vl + 24, vl + 28, vl + 36

            effs = view(stat_at + 256, 2, KC, 2)
            for n, (vg, sc) in enumerate(((V_GM, 8), (V_GF, 32))):
                m = dve.mark(DVE.tensor_scalar(effs[:, n, :, :], mods[:, l, sc:sc + 8, :], 1.0, None, ALU.add))
                dve.need(m)
                m = dve.mark(DVE.tensor_tensor(effs[:, n, :, :], effs[:, n, :, :],
                                               vec[:, vg:vg + 8].unsqueeze(2).to_broadcast([P, KC, 2]), ALU.mult))
            phase()

            def gate_rows(g0):
                for _, which in full:
                    for h in range(2):
                        b = bank()
                        for k in range(4):
                            col = mods[:, l, g0 + 4 * h + k, which:which + 1].to_broadcast([P, P])
                            i = PE.matmul(psum[b][:, k * P:(k + 1) * P], col, ident, start=True, stop=True)
                        m = pe.mark(i)
                        act.need(m)
                        bank_free[b] = act.mark(ACTE.activation(gates[:, which, h * 512:(h + 1) * 512], psum[b][:], ACT.Copy))

            z = zone
            hT = view(z, KC, TOK); h_at = z; z += KC * TOK
            sg_at = z; sg = view(z, 4, TOK); z += 4 * TOK
            vc_at = z; z += 3672
            zs_at = z; zs = view(z, NT, DS); z += NT * DS
            xp_at = z; z += KC * (TOK + 2 * (SK - 1))
            t5_at = z; z += TOK
            assert z <= 53200, z
            xn = view(sg_at, NT, D)
            normed_features(streams, hT, xn,
                            lambda k, w: effs[:, 0, k, w:w + 1], lambda k, w: mods[:, l, k, w:w + 1])
            phase("inproj")

            v1 = view(vc_at, 2, ROWS, GRID_W + CK - 1)
            v2 = view(vc_at + 2 * ROWS * (GRID_W + CK - 1), 2, SEQ)
            v3 = view(vc_at + 2 * ROWS * (GRID_W + CK - 1) + 2 * SEQ, 4, CTX + CK - 1)
            xbcx = view(xp_at, KC, SEQ + SK - 1)
            xbcc = view(xp_at + KC * (SEQ + SK - 1), KC, CTX + SK - 1)
            mz = pool.mark(POOL.memset(view(vc_at, 3672), 0.0))
            mz = pool.mark(POOL.memset(view(xp_at, KC * (TOK + 2 * (SK - 1))), 0.0))
            H2 = CK // 2
            H5 = SK // 2

            def feature_piece(c0, which_streams, use, nf=4):
                w, ready, s = fetch(ins["w_in_2"][l][:, c0:c0 + 128 * nf], 128 * nf)
                pe.need(ready)
                for f in range(nf):
                    for ts, which in which_streams:
                        b = bank()
                        n = len(ts) * P
                        for k in range(KC):
                            i = PE.matmul(psum[b][:, 0:n], w[:, k, f * P:(f + 1) * P], hT[:, k, ts[0] * P:ts[0] * P + n],
                                          start=k == 0, stop=k == KC - 1)
                        m = pe.mark(i)
                        use(b, m, f, ts, which, n)
                slot_free[s] = m

            def use_sig(b, m, f, ts, which, n):
                act.need(m)
                bank_free[b] = act.mark(ACTE.activation(sg[:, f, ts[0] * P:ts[0] * P + n], psum[b][:, 0:n], ACT.Sigmoid))

            def use_u(b, m, f, ts, which, n):
                dve.need(m, mz, act.last())
                s3 = sg[:, f, ts[0] * P:ts[0] * P + n]
                p3 = psum[b][:, 0:n]
                if which == 1:
                    o = v3[:, f, H2:H2 + CTX]
                elif f < 2:
                    o = v1[:, f, :, H2:H2 + GRID_W]
                    s3 = s3.rearrange("p (r c) -> p r c", c=GRID_W)
                    p3 = p3.rearrange("p (r c) -> p r c", c=GRID_W)
                else:
                    o = v2[:, f - 2, :]
                bank_free[b] = dve.mark(DVE.tensor_tensor(o, p3, s3, ALU.mult))
                u_done.append(bank_free[b])

            def use_xbc(c):
                def f_(b, m, f, ts, which, n):
                    act.need(m, mz)
                    dst = (xbcx, xbcc)[which][:, c + f, H5:H5 + n]
                    bank_free[b] = xbc_in[c + f, which] = act.mark(ACTE.activation(dst, psum[b][:, 0:n], ACT.Copy))
                return f_
            w, ready, s = fetch(ins["w_in_2"][l][:, 2560:2576], 16)
            pe.need(ready)
            dt = view(stat_at + 320, NT, 16)
            dta = view(stat_at + 416, NT, 16)
            e1 = view(stat_at + 512, NT, 16)
            av = view(stat_at + 608, 16)
            b = bank()
            for t in range(NT):
                for k in range(KC):
                    i = PE.matmul(psum[b][:, 16 * t:16 * t + 16], hT[:, k, t * P:(t + 1) * P], w[:, k, :],
                                  start=k == 0, stop=k == KC - 1)
            m = pe.mark(i)
            slot_free[s] = m
            dve.need(m)
            m = dve.mark(DVE.tensor_tensor(dt, psum[b][:, 0:16 * NT].rearrange("p (t n) -> p t n", n=16),
                                           bc[:, B_DTB + 16 * l:B_DTB + 16 * l + 16].unsqueeze(1).to_broadcast([P, NT, 16]), ALU.add))
            bank_free[b] = m
            act.need(m)
            m = act.mark(ACTE.activation(e1, dt, ACT.Abs))
            act.need(m)
            m = act.mark(ACTE.activation(e1, e1, ACT.Exp, scale=-1.0))
            act.need(m)
            m = act.mark(ACTE.activation(e1, e1, ACT.Ln, bias=1.0))
            ma = act.mark(ACTE.activation(av, bc[:, B_AL + 16 * l:B_AL + 16 * l + 16], ACT.Exp))
            dve.need(m)
            m = dve.mark(DVE.scalar_tensor_tensor(dt, dt, 0.0, e1, ALU.max, ALU.add))
            dve.need(m, ma)
            m = dve.mark(DVE.scalar_tensor_tensor(dta, dt, -1.0, av.unsqueeze(1).to_broadcast([P, NT, 16]), ALU.mult, ALU.mult))

            xbc_in, u_done = {}, []
            t5 = (view(t5_at, SEQ), view(t5_at + SEQ, CTX))
            t5_free = [None, None]
            m_xbc = {}

            def short_conv(c):
                for which in range(2):
                    if which and last and c >= 6:
                        continue
                    src, n = (xbcx, xbcc)[which], (SEQ, CTX)[which]
                    cw = lambda j: vec[:, 4 * P + 40 * l + 8 * j + c:4 * P + 40 * l + 8 * j + c + 1]
                    o = t5[which]
                    dve.need(xbc_in[c, which], t5_free[which])
                    m = dve.mark(DVE.tensor_scalar(o, src[:, c, 0:n], cw(0), vec[:, V_SB + c:V_SB + c + 1], ALU.mult, ALU.add))
                    for j in range(1, SK):
                        dve.need(m)
                        m = dve.mark(DVE.scalar_tensor_tensor(o, src[:, c, j:j + n], cw(j), o, ALU.mult, ALU.add))
                    act.need(m)
                    t5_free[which] = m_xbc[c, which] = act.mark(ACTE.activation(src[:, c, 0:n], o, ACT.Silu))
            feature_piece(1536, streams, use_xbc(0))
            feature_piece(512, full, use_sig)
            for c in range(4):
                short_conv(c)
            feature_piece(0, full, use_u)
            m_u = u_done[-1]
            cy = view(sg_at, 4, TOK)
            NPC = 3
            def wide(j, c):
                return vec[:, (2 + l) * P + 4 * j + c:(2 + l) * P + 4 * j + c + 1]
            if not last:
                pool.need(m_u, act.last())
                o, by_tap = cy[:, 0:NPC, SEQ:TOK], view(gate_at, NPC, CTX)
                def taps(at):
                    return vec[:, at:at + NPC].unsqueeze(2).to_broadcast([P, NPC, CTX])
                for j in range(CK):
                    mp = pool.mark(POOL.tensor_tensor(by_tap if j else o, v3[:, 0:NPC, j:j + CTX], taps((2 + l) * P + 4 * j), ALU.mult))
                    pool.need(mp)
                    mp = pool.mark(POOL.tensor_tensor(o, o, by_tap if j else taps(V_CB), ALU.add))
                    pool.need(mp)
            dve.need(m_u)
            for c in range(2):
                o = cy[:, c, 0:SEQ].rearrange("p (r w) -> p r w", w=GRID_W)
                m = dve.mark(DVE.tensor_scalar(o, v1[:, c, :, 0:GRID_W], wide(0, c), vec[:, V_CB + c:V_CB + c + 1], ALU.mult, ALU.add))
                for j in range(1, CK):
                    dve.need(m)
                    m = dve.mark(DVE.scalar_tensor_tensor(o, v1[:, c, :, j:j + GRID_W], wide(j, c), o, ALU.mult, ALU.add))
            for c in range(2):
                o = cy[:, 2 + c, 0:SEQ]
                m = dve.mark(DVE.tensor_scalar(o, v2[:, c, :], wide(H2, 2 + c), vec[:, V_CB + 2 + c:V_CB + 3 + c], ALU.mult, ALU.add))
                for d in range(1 - ROWS, ROWS):
                    if d == 0:
                        continue
                    r0, r1 = max(0, -d) * GRID_W, (ROWS - max(0, d)) * GRID_W
                    dve.need(m)
                    m = dve.mark(DVE.scalar_tensor_tensor(o[:, r0:r1], v2[:, c, r0 + d * GRID_W:r1 + d * GRID_W],
                                                          wide(H2 + d, 2 + c), o[:, r0:r1], ALU.mult, ALU.add))
            if not last:
                for c in range(NPC, 4):
                    o = cy[:, c, SEQ:TOK]
                    m = dve.mark(DVE.tensor_scalar(o, v3[:, c, 0:CTX], wide(0, c), vec[:, V_CB + c:V_CB + c + 1], ALU.mult, ALU.add))
                    for j in range(1, CK):
                        dve.need(m)
                        m = dve.mark(DVE.scalar_tensor_tensor(o, v3[:, c, j:j + CTX], wide(j, c), o, ALU.mult, ALU.add))
            w, ready, s = fetch(ins["w_in_2"][l][:, 1024:1536], 512)
            pe.need(ready)
            for ts, which in full:
                for t in ts:
                    b, m = tok_product(hT, t, w, 512)
                    act.need(m)
                    bank_free[b] = act.mark(ACTE.activation(zs[:, t, :], psum[b][:], ACT.Silu))
            slot_free[s] = m
            if last:
                feature_piece(2048, streams, use_xbc(4), nf=2)
                feature_piece(2304, full, use_xbc(6), nf=2)
            else:
                feature_piece(2048, streams, use_xbc(4))
            m_in = pe.last()
            for c in range(4, 8):
                short_conv(c)

            def xb(c, t):
                src, a = (xbcx, t * P) if t < NXT else (xbcc, (t - NXT) * P)
                return src[:, c, a:a + P]
            tk = view(h_at, NT, 6 * P)
            pe.need(pe.last())
            act.need(pe.last())
            for c0, n in ((0, 4), (4, 2)):
                for t in range(NT):
                    b = bank()
                    for j in range(n):
                        pe.need(m_xbc[c0 + j, 0 if t < NXT else 1])
                        i = PE.transpose(psum[b][:, j * P:(j + 1) * P], xb(c0 + j, t), ident)
                    m = pe.mark(i)
                    act.need(m, m_in)
                    bank_free[b] = m_tk = act.mark(ACTE.activation(tk[:, t, c0 * P:(c0 + n) * P], psum[b][:, 0:n * P], ACT.Copy))
            phase("layernorm")

            sqv = view(vc_at, 4, 512)
            mu = view(vc_at + 2048, 512)
            rs = view(vc_at + 2560, 512)
            for ts, which in full:
                a, n = ts[0] * P, len(ts) * P
                b = bank()
                for c in range(4):
                    i = PE.matmul(psum[b][:, 0:n], ones, cy[:, c, a:a + n], start=c == 0, stop=c == 3)
                m = pe.mark(i)
                act.need(m, dve.last())
                m = act.mark(ACTE.activation(mu[:, 0:n], psum[b][:, 0:n], ACT.Copy, scale=1.0 / DC))
                bank_free[b] = m
                dve.need(m)
                m = dve.mark(DVE.tensor_tensor(cy[:, :, a:a + n], cy[:, :, a:a + n],
                                               mu[:, 0:n].unsqueeze(1).to_broadcast([P, 4, n]), ALU.subtract))
                act.need(m, pe.last())
                m = act.mark(ACTE.activation(sqv[:, :, 0:n], cy[:, :, a:a + n], ACT.Square))
                b = bank()
                pe.need(m)
                for c in range(4):
                    i = PE.matmul(psum[b][:, 0:n], ones, sqv[:, c, 0:n], start=c == 0, stop=c == 3)
                m = pe.mark(i)
                dve.need(m)
                m = dve.mark(DVE.tensor_scalar(rs[:, 0:n], psum[b][:, 0:n], 1.0 / DC, LN_EPS, ALU.mult, ALU.add))
                bank_free[b] = m
                act.need(m)
                m = act.mark(ACTE.activation(rs[:, 0:n], rs[:, 0:n], ACT.Sqrt))
                dve.need(m)
                m = dve.mark(DVE.reciprocal(rs[:, 0:n], rs[:, 0:n]))
                dve.need(m)
                m = dve.mark(DVE.tensor_tensor(cy[:, :, a:a + n], cy[:, :, a:a + n],
                                               rs[:, 0:n].unsqueeze(1).to_broadcast([P, 4, n]), ALU.mult))
                act.need(m)
                for c in range(4):
                    m = act.mark(ACTE.activation(cy[:, c, a:a + n], cy[:, c, a:a + n], ACT.Silu,
                                                 scale=vec[:, V_LG + c:V_LG + c + 1], bias=vec[:, V_LB + c:V_LB + c + 1]))
            phase("ssd")

            def borrow():
                n = slot_turn[0] % NSLOT
                slot_turn[0] += 1
                for x in (pool, act, dve):
                    x.need(slot_free[n])
                held.add(n)
                return n
            sets = [borrow(), borrow()]
            def part(j, at, *dims):
                return view(ring_at + sets[j] * SLOT + at, *dims)
            rowf = [part(j, 0, SH, P) for j in range(2)]
            rowb = [part(j, SH * P, SH, P) for j in range(2)]
            em = [part(j, 2 * SH * P, SH, P) for j in range(2)]
            xd = [part(j, 3 * SH * P, 2, DS) for j in range(2)]
            za = h_at + NT * 6 * P
            ex = view(za, 4, NT, SH); za += 4 * NT * SH
            tot = view(za, NT, 16); za += NT * 16
            sm = view(za, 2, 2, P); za += 4 * P
            yt0 = view(za, DS); za += DS
            assert za <= h_at + KC * TOK
            yts = [yt0, view(t5_at, DS)]
            hs_ = [[view(xp_at + (2 * d + j) * DS, DS) for j in range(2)] for d in range(2)]
            assert 4 * DS <= 4 * (SEQ + SK - 1)
            xws = [view(xp_at + KC * (SEQ + SK - 1) + d * DS, DS) for d in range(2)]
            ys = view(vc_at, NT, DS)
            mt = [q for ts, _ in full for q in ts]
            h3 = lambda x: x.rearrange("p (h n) -> p h n", n=HD)
            b = bank()
            for n, (msk, d) in enumerate(((C_LE, 0), (C_GE, 1), (C_GT, 0), (C_LT, 1))):
                i = PE.matmul(psum[b][:, 48 * n:48 * n + 48].rearrange("p (t h) -> p t h", h=8), const[:, msk:msk + P],
                              dta[:, :, 8 * d:8 * d + 8], start=True, stop=True)
            i = PE.matmul(psum[b][:, 192:288].rearrange("p (t h) -> p t h", h=16), ones, dta, start=True, stop=True)
            m = pe.mark(i)
            act.need(m)
            act.mark(ACTE.activation(ex, psum[b][:, 0:192].rearrange("p (k t h) -> p k t h", t=NT, h=8), ACT.Exp))
            m = act.mark(ACTE.activation(tot, psum[b][:, 192:288].rearrange("p (t h) -> p t h", h=16), ACT.Exp))
            bank_free[b] = m
            dve.need(m)
            for d in range(2):
                m_ex = dve.mark(DVE.tensor_tensor(ex[:, 2 + d, :, :], ex[:, 2 + d, :, :], dt[:, :, 8 * d:8 * d + 8], ALU.mult))
            m_h = [dve.mark(DVE.memset(hs_[d][0], 0.0)) for d in range(2)]
            y_at = {}

            def cst(c):
                return const[:, c:c + P]

            def per_head(x, n):
                return x.unsqueeze(2).to_broadcast([P, SH, n])
            set_free, seg = [None, None], {}

            def within_1(n):
                t, j = mt[n], n % 2
                pool.need(set_free[j])
                for o, msk, d in ((rowf[j], C_GT, 0), (rowb[j], C_LT, 1)):
                    mg = pool.mark(POOL.tensor_tensor(o, cst(msk).unsqueeze(1).to_broadcast([P, SH, P]),
                                                      per_head(dta[:, t, 8 * d:8 * d + 8], P), ALU.mult))
                for d in range(2):
                    mx = pool.mark(POOL.tensor_tensor(h3(xd[j][:, d, :]), h3(tk[:, t, 0:DS]), per_head(dt[:, t, 8 * d:8 * d + 8], HD), ALU.mult))
                y_at[t] = pool.mark(POOL.tensor_tensor(h3(ys[:, t, :]), h3(tk[:, t, 0:DS]), per_head(bc[:, B_DS + 8 * l:B_DS + 8 * l + 8], HD), ALU.mult))
                bs = bank()
                for g in range(2):
                    i = PE.matmul(psum[bs][:, g * P:(g + 1) * P], xb(4 + g, t), xb(6 + g, t), start=True, stop=True)
                m_s = pe.mark(i)
                pe.need(mg)
                es = []
                for q in range(2):
                    b = bank()
                    for h in range(4):
                        o = psum[b][:, h * P:(h + 1) * P]
                        PE.matmul(o, rowf[j][:, 4 * q + h, :], cst(C_LE), start=True, stop=False)
                        i = PE.matmul(o, rowb[j][:, 4 * q + h, :], cst(C_GE), start=False, stop=True)
                    m = pe.mark(i)
                    act.need(m, set_free[j])
                    bank_free[b] = act.mark(ACTE.activation(em[j][:, 4 * q:4 * q + 4, :], psum[b][:].rearrange("p (h l) -> p h l", l=P), ACT.Exp))
                banks_held.add(bs)
                seg[n] = (bs, m_s, act.last(), mx)

            def within_2(n):
                t, j = mt[n], n % 2
                bs, m_s, m_e, mx = seg[n]
                dve.need(m_s)
                for d, keep in ((0, C_LE), (1, C_GE)):
                    m = dve.mark(DVE.tensor_tensor(sm[:, d, :, :], psum[bs][:, 0:2 * P].rearrange("p (g l) -> p g l", l=P),
                                                   cst(keep).unsqueeze(1).to_broadcast([P, 2, P]), ALU.mult))
                bank_free[bs] = m
                banks_held.discard(bs)
                dve.need(m, m_e)
                for d, o in ((0, rowf[j]), (1, rowb[j])):
                    m = dve.mark(DVE.tensor_tensor(o.rearrange("p (g h) l -> p g h l", g=2), em[j].rearrange("p (g h) l -> p g h l", g=2),
                                                   sm[:, d, :, :].unsqueeze(2).to_broadcast([P, 2, 4, P]), ALU.mult))
                b = bank()
                pe.need(m, mx)
                for h in range(SH):
                    o = psum[b][:, h * HD:(h + 1) * HD]
                    PE.matmul(o, rowf[j][:, h, :], xd[j][:, 0, h * HD:(h + 1) * HD], start=True, stop=False)
                    i = PE.matmul(o, rowb[j][:, h, :], xd[j][:, 1, h * HD:(h + 1) * HD], start=False, stop=True)
                m = pe.mark(i)
                set_free[j] = m
                dve.need(m, y_at[t])
                bank_free[b] = y_at[t] = dve.mark(DVE.tensor_tensor(ys[:, t, :], ys[:, t, :], psum[b][:], ALU.add))

            order = [ct + xt, ct[::-1] + xt[::-1]]
            xw_free, yt_free = [None, None], [None, None]
            h_read = [[None, None], [None, None]]

            def across(n):
                for d in range(2):
                    t = order[d][n]
                    old, new = hs_[d][n % 2], hs_[d][1 - n % 2]
                    b2 = None
                    if n < NT - 1:
                        pool.need(m_ex, xw_free[d])
                        mw = pool.mark(POOL.tensor_tensor(h3(xws[d]), h3(tk[:, t, 0:DS]), per_head(ex[:, 2 + d, t, :], HD), ALU.mult))
                        b2 = bank()
                        pe.need(mw)
                        for g in range(2):
                            i = PE.matmul(psum[b2][:, g * 256:(g + 1) * 256], tk[:, t, DS + g * P:DS + (g + 1) * P], xws[d][:, g * 256:(g + 1) * 256], start=True, stop=True)
                        m_st = xw_free[d] = pe.mark(i)
                    if t in mt:
                        b = bank()
                        pe.need(m_h[d])
                        for g in range(2):
                            i = PE.matmul(psum[b][:, g * 256:(g + 1) * 256], xb(6 + g, t), old[:, g * 256:(g + 1) * 256], start=True, stop=True)
                        m = pe.mark(i)
                        h_read[d][n % 2] = m
                        dve.need(m, m_ex, yt_free[d])
                        m = dve.mark(DVE.tensor_tensor(h3(yts[d]), h3(psum[b][:]), per_head(ex[:, d, t, :], HD), ALU.mult))
                        bank_free[b] = m
                        later.append((d, t, m))
                    if n < NT - 1:
                        dve.need(m_h[d], h_read[d][1 - n % 2])
                        m = dve.mark(DVE.tensor_tensor(h3(new), h3(old), per_head(tot[:, t, 8 * d:8 * d + 8], HD), ALU.mult))
                        dve.need(m, m_st)
                        m_h[d] = bank_free[b2] = dve.mark(DVE.tensor_tensor(new, new, psum[b2][:], ALU.add))
                        later.append((d, -1, None))
                for d, t, m in later:
                    if t < 0:
                        continue
                    pool.need(m, y_at[t])
                    y_at[t] = yt_free[d] = pool.mark(POOL.tensor_tensor(ys[:, t, :], ys[:, t, :], yts[d], ALU.add))
                later.clear()
            later = []
            steps = max(len(mt) + 1, NT)
            for n in range(len(mt) + 1):
                if n < len(mt):
                    within_1(n)
                if n >= 1:
                    within_2(n - 1)
                if not last and n < len(mt) and len(ada_todo) > 7:
                    some_ada(1)
            for n in range(NT):
                across(n)
                if not last and len(ada_todo) > 7:
                    some_ada(1)
            for n in range(2):
                slot_free[sets[n]] = pe.last()
            held.clear()
            while ada_late:
                ada_turn()
            act.need(act.last())
            gate_rows(16)
            phase("ssd out")
            yt = yt0
            m = dve.mark(DVE.tensor_tensor(ys[:, 0:len(mt), :], ys[:, 0:len(mt), :], zs[:, 0:len(mt), :], ALU.mult))
            act.need(m)
            m = rms_rows(mt, DS, lambda t: ys[:, t, :], yt)
            dve.need(m)
            m = dve.mark(DVE.tensor_tensor(ys[:, 0:len(mt), :], ys[:, 0:len(mt), :],
                                           stats[:, 0:len(mt)].unsqueeze(2).to_broadcast([P, len(mt), DS]), ALU.mult))
            phase()
            syT = view(xp_at, 4, TOK)
            for ts, _ in full:
                transposed(ys, ts, 4, syT, 0, lambda k: vec[:, V_SN + k:V_SN + k + 1])
            phase()
            prod = view(h_at, 4, 512)
            uses = [None] * 4
            ada_gen = ada_on_dve([] if last else ada_todo, h_at + 2048)
            halves = [fetch(ins["w_out_2"][l][:, h * 512:(h + 1) * 512], 512) for h in range(2)]
            held.update(s for _, _, s in halves)
            for h in range(2):
                w, ready, s = halves[h]
                pe.need(ready)
                for ts, which in full:
                    for t in ts:
                        b = bank()
                        for k in range(KC):
                            src = cy[:, k, t * P:(t + 1) * P] if k < 4 else syT[:, k - 4, t * P:(t + 1) * P]
                            i = PE.matmul(psum[b][:], src, w[:, k, :], start=k == 0, stop=k == KC - 1)
                        m = pe.mark(i)
                        u = t % 4
                        dve.need(m, uses[u])
                        m1 = dve.mark(DVE.tensor_tensor(prod[:, u, :], psum[b][:], gates[:, which, h * 512:(h + 1) * 512], ALU.mult))
                        bank_free[b] = m1
                        pool.need(m1)
                        r = resid[:, t, h * 512:(h + 1) * 512]
                        uses[u] = pool.mark(POOL.tensor_tensor(r, r, prod[:, u, :], ALU.add))
                        if h == 1:
                            act.need(uses[u])
                            sum_squares(t, resid[:, t, :], view(vc_at, D))
                        steps_of(ada_gen, 5)
                slot_free[s] = m
                held.discard(s)
            for _ in ada_gen:
                pass
            phase()

            NX = EXTRA[l]
            NSL = NE + NX
            CAP = P * (2 if NX else 1)
            n_t = len(mt)
            z = zone
            tT = view(z, KC, TOK); z += KC * TOK
            xm = view(z, NT, D); xm_at = z; z += NT * D
            sb_rows = view(z, 4, D); z += 4 * D
            lg_at = z; z += 3200
            eid_at = stat_at + 704 + 64 * l
            assert z <= 53200, z
            w_gu = [sb[:, ring_at + 2 * u * SLOT:ring_at + (2 * u + 1) * SLOT].rearrange("p (k n) -> p k n", n=2 * FF) for u in range(2)]
            w_dn = [sb[:, ring_at + (2 * u + 1) * SLOT:ring_at + (2 * u + 1) * SLOT + 2 * D].rearrange("p (k n) -> p k n", n=D) for u in range(2)]

            def load_gu(e, u):
                for j, name in enumerate(("w_gate_2", "w_up_2")):
                    m = slot_full[2 * u].mark(sp.dma_start(w_gu[u][:, :, j * FF:(j + 1) * FF],
                                                           ins[name][l][e, :, :].rearrange("e (k p) n -> p (e k) n", p=P)))
                return m

            def load_dn(e, u):
                return slot_full[2 * u + 1].mark(sp.dma_start(w_dn[u], ins["w_down_2"][l][e, :, :].rearrange("e (k p) n -> p (e k) n", p=P)))
            ready_gu, ready_dn = [None] * 2, [None] * 2
            for n in range(NSLOT):
                spl.need(slot_free[n])
            for u in range(2):
                ready_gu[u] = load_gu(slice(u, u + 1), u)
                ready_dn[u] = load_dn(slice(u, u + 1), u)

            for _, which in full:
                for n, col in ((0, lambda k: effs[:, 1, k, which:which + 1]), (1, lambda k: mods[:, l, 24 + k, which:which + 1])):
                    for h in range(2):
                        b = bank()
                        for k in range(4):
                            i = PE.matmul(psum[b][:, k * P:(k + 1) * P], col(4 * h + k).to_broadcast([P, P]), ident, start=True, stop=True)
                        m = pe.mark(i)
                        act.need(m)
                        m_rows = bank_free[b] = act.mark(ACTE.activation(sb_rows[:, 2 * which + n, h * 512:(h + 1) * 512], psum[b][:], ACT.Copy))
            m = rms_rows(mt, D)
            dve.need(m, m_rows)
            ms = {}
            for t in mt:
                which = 0 if t < NXT else 1
                m = dve.mark(DVE.scalar_tensor_tensor(xm[:, t, :], resid[:, t, :], stats[:, t:t + 1], sb_rows[:, 2 * which, :], ALU.mult, ALU.mult))
                adds = dve if t % 3 == 2 else pool
                adds.need(m)
                ms[t] = adds.mark((DVE if adds is dve else POOL).tensor_tensor(xm[:, t, :], xm[:, t, :], sb_rows[:, 2 * which + 1, :], ALU.add))
                act.need(ms[t])
                m_xd = tok_stored.mark(nc.scalar.dma_start(tok_dram[l][t * P:(t + 1) * P, :], xm[:, t, :]))
            for k in range(KC):
                for ts, which in full:
                    b = bank()
                    for j, t in enumerate(ts):
                        pe.need(ms[t])
                        i = PE.transpose(psum[b][:, j * P:(j + 1) * P], xm[:, t, k * P:(k + 1) * P], ident)
                    m = pe.mark(i)
                    o, n = tT[:, k, ts[0] * P:(ts[-1] + 1) * P], len(ts) * P
                    x = (dve, act)[k % 2]
                    x.need(m)
                    bank_free[b] = x.mark(DVE.tensor_copy(o, psum[b][:, 0:n]) if k % 2 == 0 else ACTE.activation(o, psum[b][:, 0:n], ACT.Copy))
            lg = view(lg_at, n_t, 20)
            q = [lg_at + NT * 20]

            def tile(*dims):
                n = 1
                for x in dims:
                    n *= x
                v = view(q[0], *dims)
                q[0] += n
                return v
            b = bank()
            pe.need(dve.last(), act.last())
            for t in mt:
                for k in range(KC):
                    i = PE.matmul(psum[b][:, 20 * t:20 * t + 20], tT[:, k, t * P:(t + 1) * P], router[:, l, k, :], start=k == 0, stop=k == KC - 1)
            m = pe.mark(i)

            def v_op(inst):
                m = dve.mark(inst)
                dve.need(m)
                return m
            dve.need(m)
            bank_free[b] = v_op(DVE.tensor_tensor(lg, psum[b][:, 0:20 * n_t].rearrange("p (t n) -> p t n", n=20),
                                                  bc[:, B_BR + 20 * l:B_BR + 20 * l + 20].unsqueeze(1).to_broadcast([P, n_t, 20]), ALU.add))

            def first_max(src, n):
                mx, oh, free = tile(n_t, 1), tile(n_t, n), tile(n_t, 1)
                v_op(DVE.tensor_reduce(mx.rearrange("p a b -> p (a b)"), src, AX.X, ALU.max))
                v_op(DVE.tensor_tensor(oh, src, mx.to_broadcast([P, n_t, n]), ALU.is_equal))
                v_op(DVE.tensor_scalar(free, oh[:, :, 0:1], -1.0, 1.0, ALU.mult, ALU.add))
                for j in range(1, n):
                    v_op(DVE.tensor_tensor(oh[:, :, j:j + 1], oh[:, :, j:j + 1], free, ALU.mult))
                    if j < n - 1:
                        v_op(DVE.tensor_tensor(free, free, oh[:, :, j:j + 1], ALU.subtract))
                return mx, oh
            gm, gsel = first_max(lg[:, :, 0:4], 4)
            dif = tile(n_t, 4)
            m = v_op(DVE.tensor_tensor(dif, lg[:, :, 0:4], gm.to_broadcast([P, n_t, 4]), ALU.subtract))
            act.need(m)
            m = act.mark(ACTE.activation(dif, dif, ACT.Exp))
            dve.need(m)
            gp = tile(n_t, 1)
            v_op(DVE.tensor_reduce(gp.rearrange("p a b -> p (a b)"), dif, AX.X, ALU.add))
            el, pr = tile(n_t, 4), tile(n_t, 4)
            for g in range(NG):
                dst = el if g == 0 else pr
                v_op(DVE.tensor_tensor(dst, lg[:, :, 4 + 4 * g:8 + 4 * g], gsel[:, :, g:g + 1].to_broadcast([P, n_t, 4]), ALU.mult))
                if g:
                    v_op(DVE.tensor_tensor(el, el, pr, ALU.add))
            m1_, oh1 = first_max(el, 4)
            v_op(DVE.scalar_tensor_tensor(el, oh1, -1e30, el, ALU.mult, ALU.add))
            m2_, oh2 = first_max(el, 4)
            wt = tile(2, n_t)
            w1, e2 = wt[:, 0, :].unsqueeze(2), wt[:, 1, :].unsqueeze(2)
            m = v_op(DVE.tensor_tensor(e2, m2_, m1_, ALU.subtract))
            act.need(m)
            m = act.mark(ACTE.activation(e2, e2, ACT.Exp))
            dve.need(m)
            gate_rows(40)
            v_op(DVE.scalar_tensor_tensor(w1, e2, 1.0, gp, ALU.add, ALU.mult))
            v_op(DVE.reciprocal(w1, w1))
            v_op(DVE.tensor_tensor(e2, e2, w1, ALU.mult))
            ch = [tile(n_t, NE) for _ in range(2)]
            for c, oh in enumerate((oh1, oh2)):
                for g in range(NG):
                    m = dve.mark(DVE.tensor_tensor(ch[c][:, :, 4 * g:4 * g + 4], oh, gsel[:, :, g:g + 1].to_broadcast([P, n_t, 4]), ALU.mult))
            dve.need(m)
            both, before, rank, tmp = tile(n_t, NE), tile(n_t + 1, NE), tile(n_t, NE), tile(n_t, NE)
            v_op(DVE.tensor_tensor(both, ch[0], ch[1], ALU.add))
            v_op(DVE.memset(before[:, 0, :], 0.0))
            for t in range(n_t):
                m = v_op(DVE.tensor_tensor(before[:, t + 1, :], before[:, t, :], both[:, t, :], ALU.add))
            b = bank()
            pe.need(m)
            r_ps = psum[b][:, 0:NE * n_t].rearrange("p (t e) -> p t e", e=NE)
            PE.matmul(r_ps, const[:, C_LT:C_LT + P], both, start=True, stop=False)
            PE.matmul(r_ps, ones, before[:, 0:n_t, :], start=False, stop=True)
            i = PE.matmul(psum[b][:, NE * n_t:NE * n_t + NE], ones, before[:, n_t, :], start=True, stop=True)
            m = pe.mark(i)
            dve.need(m)
            v_op(DVE.tensor_copy(rank, r_ps))
            eid = view(eid_at, NSL)
            v_op(DVE.tensor_copy(eid[:, 0:NE], const[:, C_IO:C_IO + NE]))
            cap, most = tile(NE), tile(2)
            counts = tile(NE)
            bank_free[b] = v_op(DVE.tensor_copy(counts, psum[b][:, NE * n_t:NE * n_t + NE]))
            v_op(DVE.tensor_reduce(most[:, 0:1], counts, AX.X, ALU.max))
            v_op(DVE.tensor_scalar(most[:, 0:1], most[:, 0:1], float(CAP), None, ALU.is_gt))
            if NX:
                over, nth, take, to2 = tile(NE), tile(NE), tile(NX, NE), tile(NE)
                v_op(DVE.tensor_scalar(over, counts, float(P), None, ALU.is_gt))
                v_op(DVE.memset(nth[:, 0:1], 0.0))
                for e in range(1, NE):
                    v_op(DVE.tensor_tensor(nth[:, e:e + 1], nth[:, e - 1:e], over[:, e - 1:e], ALU.add))
                v_op(DVE.tensor_tensor(most[:, 1:2], nth[:, NE - 1:NE], over[:, NE - 1:NE], ALU.add))
                v_op(DVE.tensor_scalar(most[:, 1:2], most[:, 1:2], float(NX), None, ALU.is_gt))
                v_op(DVE.tensor_tensor(most[:, 0:1], most[:, 0:1], most[:, 1:2], ALU.add))
                v_op(DVE.tensor_tensor(take, nth.unsqueeze(1).to_broadcast([P, NX, NE]), const[:, C_IO:C_IO + NX].unsqueeze(2).to_broadcast([P, NX, NE]), ALU.is_equal))
                v_op(DVE.tensor_tensor(take, take, over.unsqueeze(1).to_broadcast([P, NX, NE]), ALU.mult))
                v_op(DVE.tensor_scalar(cap, nth, float(NX), None, ALU.is_lt))
                v_op(DVE.tensor_tensor(cap, cap, over, ALU.mult))
                v_op(DVE.tensor_scalar(cap, cap, float(P), float(P), ALU.mult, ALU.add))
                v_op(DVE.tensor_tensor(to2, nth, const[:, C_IO:C_IO + NE], ALU.subtract))
                v_op(DVE.tensor_scalar(to2, to2, float(P), float((NE - 1) * P), ALU.mult, ALU.add))
                tke = tile(NX, NE)
                v_op(DVE.tensor_tensor(tke, take, const[:, C_IO:C_IO + NE].unsqueeze(1).to_broadcast([P, NX, NE]), ALU.mult))
                v_op(DVE.tensor_reduce(eid[:, NE:NSL], tke, AX.X, ALU.add))
            eid_i = view(eid_at + NE + 4, NSL).bitcast(mybir.dt.int32)
            m_eid = v_op(DVE.tensor_copy(eid_i, eid))
            most_i = view(stat_at + 700 + l, 1).bitcast(mybir.dt.int32)
            m_most = v_op(DVE.tensor_copy(most_i, most[:, 0:1]))
            place_i = tile(2, n_t).bitcast(mybir.dt.int32)
            fits = tile(2, n_t)
            rk, ei, hi, mv = tile(n_t), tile(n_t), tile(n_t), tile(n_t)

            def of_choice(dst, c, x):
                v_op(DVE.tensor_tensor(tmp, ch[c], x, ALU.mult))
                v_op(DVE.tensor_reduce(dst, tmp, AX.X, ALU.add))

            def over_tiles(x):
                return x.unsqueeze(1).to_broadcast([P, n_t, NE])
            wfit = tile(2, n_t)
            def places(c):
                of_choice(rk, c, rank)
                of_choice(ei, c, over_tiles(const[:, C_IO:C_IO + NE]))
                v_op(DVE.scalar_tensor_tensor(ei, ei, float(P), rk, ALU.mult, ALU.add))
                if NX:
                    of_choice(mv, c, over_tiles(cap))
                    v_op(DVE.tensor_tensor(fits[:, c, :], rk, mv, ALU.is_lt))
                    of_choice(mv, c, over_tiles(to2))
                    v_op(DVE.tensor_scalar(hi, rk, float(P), None, ALU.is_ge))
                    v_op(DVE.tensor_tensor(hi, hi, mv, ALU.mult))
                    v_op(DVE.tensor_tensor(ei, ei, hi, ALU.add))
                else:
                    v_op(DVE.tensor_scalar(fits[:, c, :], rk, float(P), None, ALU.is_lt))
                v_op(DVE.tensor_tensor(wfit[:, c, :], wt[:, c, :], fits[:, c, :], ALU.mult))
                v_op(DVE.tensor_tensor(place_i[:, c, :], ei, fits[:, c, :], ALU.mult))
            rs_ = tile(n_t, NSL)
            rank1 = tile(n_t, NE)
            v_op(DVE.scalar_tensor_tensor(rank1, rank, 1.0, both, ALU.add, ALU.mult))
            v_op(DVE.tensor_scalar(rs_[:, :, 0:NE], rank1, -1.0, None, ALU.add))
            for x in range(NX):
                v_op(DVE.tensor_tensor(tmp, rank1, over_tiles(take[:, x, :]), ALU.mult))
                v_op(DVE.tensor_reduce(mv, tmp, AX.X, ALU.add))
                v_op(DVE.tensor_scalar(rs_[:, :, NE + x], mv, -1.0 - P, None, ALU.add))
            BF = mybir.dt.bfloat16
            tokb = tile(NT).bitcast(BF)
            v_op(DVE.tensor_copy(tokb, const[:, C_TOK:C_TOK + 2 * NT]))
            HB = 4
            hot = [tile(HB, P // 2).bitcast(BF) for _ in range(3)]
            b = bank()
            seen = [None] * 3
            nh = 0
            for e in range(0, NSL, HB):
                for t in range(n_t):
                    hv = hot[nh % 3]
                    dve.need(seen[nh % 3])
                    m = dve.mark(DVE.tensor_tensor(hv, const[:, C_IO:C_IO + P].unsqueeze(1).to_broadcast([P, HB, P]),
                                                   rs_[:, t, e:e + HB].unsqueeze(2).to_broadcast([P, HB, P]), ALU.is_equal))
                    pe.need(m)
                    for k in range(HB):
                        o = (e + k) * n_t + t
                        i = PE.matmul(psum[b][:, 2 * o:2 * o + 2], hv[:, k, :], tokb[:, 2 * t:2 * t + 2], start=True, stop=True)
                    seen[nh % 3] = pe.mark(i)
                    nh += 1
            dve.need(seen[(nh - 1) % 3])
            tab = tile(NSL, 2)
            tabi = tile(NSL).bitcast(mybir.dt.int32)
            v_op(DVE.tensor_reduce(tab, psum[b][:, 0:2 * NSL * n_t].rearrange("p (e t j) -> p e j t", t=n_t, j=2), AX.X, ALU.add))
            bank_free[b] = m
            v_op(DVE.scalar_tensor_tensor(tabi, tab[:, :, 1], float(P), tab[:, :, 0], ALU.mult, ALU.add))
            assert q[0] <= lg_at + 3200, q[0] - lg_at
            act.need(m_xd)
            phase("experts")
            pool.need(m_xd)
            bank_free[b] = None
            z = xm_at
            gx = [view(z + n * D, D) for n in range(2)]; z += 4 * D
            gxT = [view(z + n * D, KC, P) for n in range(2)]; z += 2 * D
            z = xm_at + NT * D
            yb = [view(z + n * D, D) for n in range(2)]; z += 2 * D
            silg = [view(z + n * FF, FF) for n in range(2)]; z += 2 * FF
            hidb = [view(z + n * FF, FF) for n in range(2)]; z += 2 * FF
            hidT = [view(z + n * FF, 2, P) for n in range(2)]; z += 2 * FF
            idx = view(z, 2).bitcast(mybir.dt.int32); z += 2
            spare = view(z, 1); z += 1
            pool.need(pool.mark(POOL.memset(spare, 0.0)))
            assert z <= lg_at
            use = {}

            def pair_of_experts(lp, i, more):
                def old(key):
                    return use.get(key) or (lp.prev(key) if lp else None)
                def slc(j):
                    return bass.ts(j, 1) if lp else slice(j, j + 1)
                gathered = {}
                for g in range(2):
                    pool.need(old(f"turned{g}"))
                    m = pool.mark(POOL.tensor_copy(idx[:, g:g + 1], tabi[:, slc(2 * i + g)]))
                    pool.need(m)
                    pool.mark(POOL.tensor_tensor(spare, spare, spare, ALU.add))
                    gathered[g] = gx_full[g].mark(nc.gpsimd.indirect_dma_start(
                        out=gx[g], out_offset=None, in_=tok_dram[l][:, :],
                        in_offset=bass.IndirectOffsetOnAxis(ap=idx[:, g:g + 1], axis=0)))
                nb_ = [0]

                def bk(*marks, n=1):
                    got = [(nb_[0] + j) % 8 for j in range(n)]
                    nb_[0] += n
                    pe.need(*marks, *(old(f"bank{b}") for b in got))
                    return got if n > 1 else got[0]

                def turn(n):
                    g = s = n
                    bs = bk(gathered[g], n=2)
                    for h in range(2):
                        b = bs[h]
                        for j in range(4):
                            x = PE.transpose(psum[b][:, j * P:(j + 1) * P], gx[g][:, (4 * h + j) * P:(4 * h + j + 1) * P], ident)
                        m = pe.mark(x)
                        o = gxT[s][:, 4 * h:4 * h + 4, :].rearrange("p a b -> p (a b)")
                        dve.need(m, old(f"gate{s}"))
                        use[f"bank{b}"] = dve.mark(DVE.tensor_copy(o, psum[b][:]))
                        use[f"gxT{s}{h}"] = use[f"bank{b}"]
                    use[f"turned{g}"] = m

                def gate_up(n):
                    u = s = n
                    b = bk(ready_gu[u])
                    for c in range(KC):
                        pe.need(use[f"gxT{s}{c // 4}"])
                        x = PE.matmul(psum[b][:], gxT[s][:, c, :], w_gu[u][:, c, :], start=c == 0, stop=c == KC - 1)
                    m = pe.mark(x)
                    use[f"gate{s}"] = m
                    use[f"gu{u}"] = m
                    act.need(m, old(f"hid{s}"))
                    m = act.mark(ACTE.activation(silg[s], psum[b][:, 0:FF], ACT.Silu))
                    dve.need(m, old(f"hT{s}"))
                    m = dve.mark(DVE.tensor_tensor(hidb[s], silg[s], psum[b][:, FF:2 * FF], ALU.mult))
                    use[f"bank{b}"] = use[f"hid{s}"] = m

                def turn_hidden(n):
                    s = n
                    b = bk(use[f"hid{s}"])
                    for c in range(2):
                        x = PE.transpose(psum[b][:, c * P:(c + 1) * P], hidb[s][:, c * P:(c + 1) * P], ident)
                    m = pe.mark(x)
                    use[f"hT{s}"] = m
                    dve.need(m, old(f"down{s}"))
                    m = dve.mark(DVE.tensor_copy(hidT[s].rearrange("p a b -> p (a b)"), psum[b][:, 0:2 * P]))
                    use[f"bank{b}"] = use[f"hidT{s}"] = m

                def down(n):
                    u = s = n
                    b0, b1 = bk(use[f"hidT{s}"], ready_dn[u], n=2)
                    for h, b in ((0, b0), (1, b1)):
                        for c in range(2):
                            x = PE.matmul(psum[b][:], hidT[s][:, c, :], w_dn[u][:, c, h * 512:(h + 1) * 512], start=c == 0, stop=c == 1)
                    m = pe.mark(x)
                    use[f"down{s}"] = m
                    use[f"dn{u}"] = m
                    dve.need(m, old(f"stored{s}"))
                    m0 = use[f"bank{b0}"] = dve.mark(DVE.tensor_copy(yb[s][:, 0:512], psum[b0][:]))
                    m1 = use[f"bank{b1}"] = dve.mark(DVE.tensor_copy(yb[s][:, 512:1024], psum[b1][:]))
                    use[f"y{s}"] = (m0, m1)

                def store(n):
                    s = n
                    act.need(*use[f"y{s}"])
                    dst = out_dram[l].rearrange("(b p) d -> b p d", p=P)[slc(2 * i + n), :, :].rearrange("b p d -> (b p) d")
                    use[f"stored{s}"] = y_stored[s].mark(nc.scalar.dma_start(dst, yb[s]))
                next_e = {}

                def next_gu(u):
                    if not more:
                        return
                    e = next_e[u] = nc.values_load(eid_i[0:1, slc(2 * i + 2 + u)], engines=[mybir.EngineType.SP], min_val=0, max_val=NE - 1)
                    spl.need(use[f"gu{u}"])
                    use[f"next{u}"] = (load_gu(bass.ds(e, 1), u),)

                def next_dn(u):
                    if more:
                        spl.need(use[f"dn{u}"])
                        use[f"next{u}"] += (load_dn(bass.ds(next_e[u], 1), u),)
                turn(0)
                turn(1)
                if not more:
                    places(0)
                gate_up(0)
                if not more:
                    places(1)
                next_gu(0)
                gate_up(1)
                next_gu(1)
                turn_hidden(0)
                down(0)
                store(0)
                next_dn(0)
                turn_hidden(1)
                down(1)
                store(1)
                next_dn(1)
                return use

            for x in (pe, dve, act, pool):
                x.need(dve.last(), pool.last())
            NPAIR = NSL // 2
            spl.need(m_eid)
            with loop_over(f"experts{l}", NPAIR - 1) as lp:
                ready_gu = [lp.ahead(slot_full[2 * u], 0) for u in range(2)]
                ready_dn = [lp.ahead(slot_full[2 * u + 1], 0) for u in range(2)]
                use = {}
                pair_of_experts(lp, lp.i, True)
                for key, mk in use.items():
                    if isinstance(mk, tuple):
                        continue
                    lp.carry(key, mk)
                last_use = dict(use)
            ready_gu = [slot_full[2 * u].last() for u in range(2)]
            ready_dn = [slot_full[2 * u + 1].last() for u in range(2)]
            use = last_use
            pair_of_experts(None, NPAIR - 1, False)
            for n in range(8):
                bank_free[n] = [dve.last(), act.last()]
            for n in range(NSLOT):
                slot_free[n] = pe.last()
            phase("combine")
            pool.need(use["stored0"], use["stored1"], dve.last())
            z = xm_at
            yg = [view(z + n * D, D) for n in range(4)]; z += 4 * D
            free = [None] * 4
            for n, t in enumerate(mt):
                which = 0 if t < NXT else 1
                got = []
                for c in range(2):
                    s = 2 * (n % 2) + c
                    pool.need(free[s])
                    got.append(yg_full[s].mark(nc.gpsimd.indirect_dma_start(
                        out=yg[s], out_offset=None, in_=out_dram[l][:, :],
                        in_offset=bass.IndirectOffsetOnAxis(ap=place_i[:, c, t:t + 1], axis=0))))
                a, c_ = yg[2 * (n % 2)], yg[2 * (n % 2) + 1]
                act.need(got[0])
                m = act.mark(ACTE.activation(a, a, ACT.Copy, scale=wfit[:, 0, t:t + 1]))
                dve.need(m, got[1])
                m = dve.mark(DVE.scalar_tensor_tensor(a, c_, wfit[:, 1, t:t + 1], a, ALU.mult, ALU.add))
                dve.need(m)
                m = dve.mark(DVE.tensor_tensor(a, a, gates[:, which, :], ALU.mult))
                dve.need(m)
                m = dve.mark(DVE.tensor_tensor(resid[:, t, :], resid[:, t, :], a, ALU.add))
                free[2 * (n % 2)] = free[2 * (n % 2) + 1] = m
            phase("overflow")

            for x in (pe, dve, act, pool, spl):
                x.need(m_most)
            busiest = nc.values_load(most_i[0:1, 0:1], min_val=0, max_val=2)
            kept = [(x, x.sem, x.count, x.seen) for x in (pe, dve, act, pool, spl)]
            spl.need(*slot_free)
            with nc.If(busiest > 0):
                for x, nm in zip((pe, dve, act, pool, spl), ("pe", "dve", "act", "pool", "sync")):
                    x.sem, x.count, x.seen = sem(f"overflow{l}_{nm}_done"), 0, {}
                    book.sems[x.sem.name] = x.sem
                o_full = [Lane(book, None, sem(f"overflow{l}_{nm}_full"), 16) for nm in ("gu", "down")]
                for n in range(8):
                    bank_free[n] = None
                acc = view(xm_at, NT, D)
                z = xm_at + NT * D
                hidn = view(z, 2, 512); z += 1024
                silo = view(z, 512); z += 512
                cwl = view(z, NE, n_t); z += NE * NT
                wl, tw = view(z, 2, n_t), view(z + 2 * NT, n_t, NE); z += 2 * NT + NE * NT
                m = dve.mark(DVE.tensor_tensor(wl, wt, wfit, ALU.subtract))
                dve.need(m)
                ce = cwl.rearrange("p e t -> p t e")
                m = dve.mark(DVE.tensor_tensor(ce, ch[0], wl[:, 0, :].unsqueeze(2).to_broadcast([P, n_t, NE]), ALU.mult))
                m = dve.mark(DVE.tensor_tensor(tw, ch[1], wl[:, 1, :].unsqueeze(2).to_broadcast([P, n_t, NE]), ALU.mult))
                dve.need(m)
                m = dve.mark(DVE.tensor_tensor(ce, ce, tw, ALU.add))
                m = dve.mark(DVE.memset(acc[:, 0:n_t, :], 0.0))
                dve.need(m)
                with loop_over(f"overflow{l}", NE) as lp:
                    i = lp.i
                    spl.need(lp.prev("down"))
                    for j, name in enumerate(("w_gate_2", "w_up_2")):
                        r1 = o_full[0].mark(sp.dma_start(w_gu[0][:, :, j * FF:(j + 1) * FF],
                                                         ins[name][l][bass.ts(i, 1), :, :].rearrange("e (k p) n -> p (e k) n", p=P)))
                    r2 = o_full[1].mark(sp.dma_start(w_dn[0], ins["w_down_2"][l][bass.ts(i, 1), :, :].rearrange("e (k p) n -> p (e k) n", p=P)))
                    pe.need(lp.prev("acc"))
                    pe.need(r1, r2)
                    ma = lp.prev("acc")
                    for ts, which in full:
                        c, n = slice(ts[0] * P, (ts[-1] + 1) * P), len(ts) * P
                        for f in range(2):
                            pe.need(ma)
                            for j in range(2):
                                for k in range(KC):
                                    x = PE.matmul(psum[j][:, 0:n], w_gu[0][:, k, j * FF + f * P:j * FF + (f + 1) * P], tT[:, k, c], start=k == 0, stop=k == KC - 1)
                            m = pe.mark(x)
                            act.need(m, ma)
                            m = act.mark(ACTE.activation(silo[:, 0:n], psum[0][:, 0:n], ACT.Silu))
                            dve.need(m, ma)
                            ma = dve.mark(DVE.tensor_tensor(hidn[:, f, 0:n], silo[:, 0:n], psum[1][:, 0:n], ALU.mult))
                        for j, t in enumerate(ts):
                            for h in range(2):
                                pe.need(ma)
                                for k in range(2):
                                    x = PE.matmul(psum[2][:], hidn[:, k, j * P:(j + 1) * P], w_dn[0][:, k, h * 512:(h + 1) * 512], start=k == 0, stop=k == 1)
                                m = pe.mark(x)
                                dve.need(m, ma)
                                a = acc[:, t, h * 512:(h + 1) * 512]
                                ma = dve.mark(DVE.scalar_tensor_tensor(a, psum[2][:], cwl[:, bass.ts(i, 1), t], a, ALU.mult, ALU.add))
                    lp.carry("acc", ma)
                    lp.carry("down", m)
                dve.need(dve.last())
                for t in mt:
                    which = 0 if t < NXT else 1
                    m = dve.mark(DVE.tensor_tensor(acc[:, t, :], acc[:, t, :], gates[:, which, :], ALU.mult))
                    dve.need(m)
                    m = dve.mark(DVE.tensor_tensor(resid[:, t, :], resid[:, t, :], acc[:, t, :], ALU.add))
                phase("overflow end")
                spl.need(pe.last())
            for n in range(8):
                bank_free[n] = None
            for x, s_, c_, n_ in kept:
                x.sem, x.count, x.seen = s_, c_, n_
            assert all(x.last().value() == x.count for x in lanes)

        s_gf = sem("final_gain_loaded")
        spl.need(pe.last(), act.last())
        sp.dma_start(bc[:, B_GF:B_GF + D], ins["g_final_2"].partition_broadcast(P)).then_inc(s_gf, 16)
        yo = view(zone, NXT, D)
        m = rms_rows(list(range(NXT)), D, lambda t: resid[:, t, :], yo[:, 0, :])
        dve.need(m)
        s_out = sem("out_stored")
        dve.need(Mark(s_gf, 16, None))
        for t in range(NXT):
            m = dve.mark(DVE.scalar_tensor_tensor(yo[:, t, :], resid[:, t, :], stats[:, t:t + 1], bc[:, B_GF:B_GF + D], ALU.mult, ALU.mult))
            spl.need(m)
            sp.dma_start(out[0, t * P:(t + 1) * P, :], yo[:, t, :]).then_inc(s_out, 16)
        sp.wait_ge(s_out, 16 * NXT)
    return book.found


_NAMES = ["x", "norm_gain", "w_in", "q_norm_a", "k_norm_a", "sinks_a", "q_norm_b", "k_norm_b", "w_out", "c_2", "ctx_2",
          "c_ctx_2", "w_ada_2", "b_ada_2", "g_mix_2", "g_ffn_2", "w_in_2", "conv_w_2", "conv_b_2", "conv_ln_g_2",
          "conv_ln_b_2", "ssd_conv_w_2", "ssd_conv_b_2", "dt_bias_2", "a_log_2", "d_skip_2", "ssd_norm_g_2",
          "w_out_2", "w_router_group_2", "b_router_group_2", "w_router_expert_2", "b_router_expert_2", "w_gate_2",
          "w_up_2", "w_down_2", "g_final_2"]


def _constants():
    import numpy as np
    r, s = np.arange(P)[:, None], np.arange(P)[None, :]
    c = np.zeros((P, NCONST), np.float32)
    c[:, C_ID:C_ID + P] = r == s
    c[:, C_LE:C_LE + P] = r <= s
    c[:, C_LT:C_LT + P] = r < s
    c[:, C_GE:C_GE + P] = r >= s
    c[:, C_GT:C_GT + P] = r > s
    c[:, C_ONE:C_ONE + P] = 1.0
    dist = r - np.arange(2 * P)[None, :] + P
    c[:, C_MA:C_MA + 2 * P] = np.where((dist >= 0) & (dist <= P - 1), 0.0, NEG)
    dist = r - np.arange(4 * P)[None, :] + 3 * P
    count = ((dist >= 0) & (dist <= 128)) * 1 + ((dist >= 0) & (dist % 4 == 0)) * 1 + ((dist >= 0) & (dist % 16 == 0)) * 1
    c[:, C_MB:C_MB + 4 * P] = np.where(count > 0, np.log(np.maximum(count, 1)) / SCALE, NEG)
    half = HD // 2
    inv = np.float32(10000.0) ** (-np.arange(half, dtype=np.float32) / np.float32(half))
    ang = (np.arange(SEQ, dtype=np.float32)[:, None] * inv[None, :]).astype(np.float32)
    tab = np.concatenate([np.cos(ang), np.sin(ang)], axis=1).reshape(NXT, P, HD)
    c[:, C_IO:C_IO + 256] = np.arange(256)
    c[:, C_TOK:C_TOK + 2 * NT:2] = np.arange(P)[:, None]
    c[:, C_TOK + 1:C_TOK + 2 * NT:2] = np.arange(NT)
    c[:, C_CS:C_CS + NXT * HD] = tab.transpose(1, 0, 2).reshape(P, NXT * HD)
    return c


def kernel(**inputs):
    import numpy as np
    import concourse.bacc as bacc
    from concourse.bass_utils import run_bass_kernel_spmd as run
    arrays = {n: np.ascontiguousarray(inputs[n]) for n in _NAMES}
    arrays["consts"] = _constants()
    known = {}
    for _ in range(2):
        nc = bacc.Bacc("TRN2", target_bir_lowering=False, num_devices=1)
        ins = {n: nc.dram_tensor("in_" + n, a.shape, mybir.dt.from_np(a.dtype), kind="ExternalInput").ap()
               for n, a in arrays.items()}
        out = nc.dram_tensor("out", (1, SEQ, D), F32, kind="ExternalOutput").ap()
        known = program(nc, ins, out, known)
    r = run(nc, [{"in_" + n: a for n, a in arrays.items()}], core_ids=[0])
    return r.results[0]["out"]
```
